# Optimizing a Trainium2 kernel written in Bass

```python
import math
import jax, jax.numpy as jnp
from jax import lax
import numpy as np

D_MODEL = 2048
BATCH = 1
SEQ = 256
DEPTH = 2

EXPAND = 2
D_INNER = EXPAND * D_MODEL
N_MIXERS = 2
POOL_WINDOWS = (2, 4, 8, 16)
POOL_GROUPS = len(POOL_WINDOWS)
POOL_GROUP_DIM = D_INNER // POOL_GROUPS
SSM_GROUP_DIM = 16
SSM_GROUPS = D_INNER // SSM_GROUP_DIM
SSM_STATE = 64
SSM_GROUP_CHUNK = 32
SSM_N_CHUNKS = SSM_GROUPS // SSM_GROUP_CHUNK
DT_MIN = 1e-3
DT_MAX = 1e-1
NORM_EPS = 1e-6
N_POOL_LAYERS = (DEPTH + 1) // 2
N_SSM_LAYERS = DEPTH // 2

kernel_name = "hybrid_pool_s5_interleaved"

def _rmsnorm(x, g):
    x32 = x.astype(jnp.float32)
    inv = lax.rsqrt(jnp.mean(x32 * x32, axis=-1, keepdims=True) + NORM_EPS)
    return (x32 * inv * g.astype(jnp.float32)).astype(x.dtype)

def _pool_mixer(u, w_grp, scale):
    b, l, _ = u.shape
    u32 = u.astype(jnp.float32)
    cs = jnp.cumsum(u32, axis=1)
    pos = jnp.arange(l)
    outs = []
    for g, w in enumerate(POOL_WINDOWS):
        sl = slice(g * POOL_GROUP_DIM, (g + 1) * POOL_GROUP_DIM)
        csg = cs[..., sl]
        lag = jnp.pad(csg, ((0, 0), (w, 0), (0, 0)))[:, :l]
        cnt = jnp.minimum(pos + 1, w).astype(jnp.float32)[None, :, None]
        outs.append((csg - lag) / cnt - u32[..., sl])
    p = jnp.stack(outs, axis=2)
    m = jnp.einsum('blgc,gcd->blgd', p, w_grp.astype(jnp.float32)).reshape(b, l, D_INNER)
    return m * scale.astype(jnp.float32)

def _cplx_linrec(e1, e2):
    a1r, a1i, b1r, b1i = e1
    a2r, a2i, b2r, b2i = e2
    ar = a2r * a1r - a2i * a1i
    ai = a2r * a1i + a2i * a1r
    br = a2r * b1r - a2i * b1i + b2r
    bi = a2r * b1i + a2i * b1r + b2i
    return (ar, ai, br, bi)

def _ssm_chunk(args):
    u_c, abr, abi, bbr, bbi, cr, ci = args
    bu_r = jnp.einsum('blgp,gnp->blgn', u_c, bbr)
    bu_i = jnp.einsum('blgp,gnp->blgn', u_c, bbi)
    ar = jnp.broadcast_to(abr, bu_r.shape)
    ai = jnp.broadcast_to(abi, bu_r.shape)
    _, _, hr, hi = lax.associative_scan(_cplx_linrec, (ar, ai, bu_r, bu_i), axis=1)
    return jnp.einsum('blgn,gpn->blgp', hr, cr) - jnp.einsum('blgn,gpn->blgp', hi, ci)

def _s5_mixer(u, a_re, a_im, log_dt, b_re, b_im, c_re, c_im, d_skip, w_glu, b_glu):
    f32 = jnp.float32
    b, l, _ = u.shape
    u32 = u.astype(f32)
    a_re = a_re.astype(f32); a_im = a_im.astype(f32)
    dt = jnp.exp(log_dt.astype(f32))[:, None]
    mag = jnp.exp(a_re * dt)
    abr = mag * jnp.cos(a_im * dt)
    abi = mag * jnp.sin(a_im * dt)
    den = a_re * a_re + a_im * a_im
    nr = abr - 1.0
    fr = (nr * a_re + abi * a_im) / den
    fi = (abi * a_re - nr * a_im) / den
    b_re = b_re.astype(f32); b_im = b_im.astype(f32)
    bbr = fr[..., None] * b_re - fi[..., None] * b_im
    bbi = fr[..., None] * b_im + fi[..., None] * b_re
    nc, gc = SSM_N_CHUNKS, SSM_GROUP_CHUNK
    u_ch = u32.reshape(b, l, nc, gc, SSM_GROUP_DIM).transpose(2, 0, 1, 3, 4)
    y = lax.map(_ssm_chunk, (u_ch,
                             abr.reshape(nc, gc, SSM_STATE), abi.reshape(nc, gc, SSM_STATE),
                             bbr.reshape(nc, gc, SSM_STATE, SSM_GROUP_DIM),
                             bbi.reshape(nc, gc, SSM_STATE, SSM_GROUP_DIM),
                             c_re.astype(f32).reshape(nc, gc, SSM_GROUP_DIM, SSM_STATE),
                             c_im.astype(f32).reshape(nc, gc, SSM_GROUP_DIM, SSM_STATE)))
    y = y.transpose(1, 2, 0, 3, 4).reshape(b, l, D_INNER) + d_skip.astype(f32) * u32
    g = jax.nn.gelu(y)
    return g * jax.nn.sigmoid(g @ w_glu.astype(f32) + b_glu.astype(f32))

def setup_inputs(seed: int = 0) -> dict:
    key = jax.random.key(seed)
    ks = jax.random.split(key, 24)
    f32 = jnp.float32
    D, E, G, N, P = D_MODEL, D_INNER, SSM_GROUPS, SSM_STATE, SSM_GROUP_DIM
    NP_, NS_ = N_POOL_LAYERS, N_SSM_LAYERS
    nrm = lambda k, s, sc: jax.random.normal(k, s, f32) * sc
    x = jax.random.normal(ks[0], (BATCH, SEQ, D), f32)
    norm_g = 1.0 + nrm(ks[1], (DEPTH, D), 0.02)
    final_norm_g = 1.0 + nrm(ks[2], (D,), 0.02)
    pool_w_in = nrm(ks[3], (NP_, D, 2 * E), D ** -0.5)
    pool_w_grp = nrm(ks[4], (NP_, POOL_GROUPS, POOL_GROUP_DIM, POOL_GROUP_DIM), POOL_GROUP_DIM ** -0.5)
    pool_scale = 1.0 + nrm(ks[5], (NP_, E), 0.02)
    pool_w_out = nrm(ks[6], (NP_, E, D), E ** -0.5)
    ssm_w_in = nrm(ks[7], (NS_, D, 2 * E), D ** -0.5)
    n_idx = jnp.arange(N, dtype=f32)
    ssm_a_re = -0.5 + nrm(ks[8], (NS_, G, N), 0.01)
    ssm_a_im = math.pi * n_idx[None, None, :] + nrm(ks[9], (NS_, G, N), 0.01)
    ssm_log_dt = math.log(DT_MIN) + jax.random.uniform(ks[10], (NS_, G), f32) * (math.log(DT_MAX) - math.log(DT_MIN))
    ssm_b_re = nrm(ks[11], (NS_, G, N, P), (2.0 * P) ** -0.5)
    ssm_b_im = nrm(ks[12], (NS_, G, N, P), (2.0 * P) ** -0.5)
    ssm_c_re = nrm(ks[13], (NS_, G, P, N), (2.0 * N) ** -0.5)
    ssm_c_im = nrm(ks[14], (NS_, G, P, N), (2.0 * N) ** -0.5)
    ssm_d = nrm(ks[15], (NS_, E), 1.0)
    ssm_w_glu = nrm(ks[16], (NS_, E, E), E ** -0.5)
    ssm_b_glu = nrm(ks[17], (NS_, E), 0.02)
    ssm_w_out = nrm(ks[18], (NS_, E, D), E ** -0.5)
    return {"x": x, "norm_g": norm_g, "final_norm_g": final_norm_g,
            "pool_w_in": pool_w_in, "pool_w_grp": pool_w_grp, "pool_scale": pool_scale, "pool_w_out": pool_w_out,
            "ssm_w_in": ssm_w_in, "ssm_a_re": ssm_a_re, "ssm_a_im": ssm_a_im, "ssm_log_dt": ssm_log_dt,
            "ssm_b_re": ssm_b_re, "ssm_b_im": ssm_b_im, "ssm_c_re": ssm_c_re, "ssm_c_im": ssm_c_im,
            "ssm_d": ssm_d, "ssm_w_glu": ssm_w_glu, "ssm_b_glu": ssm_b_glu, "ssm_w_out": ssm_w_out}

def reference(x, norm_g, final_norm_g, pool_w_in, pool_w_grp, pool_scale, pool_w_out,
              ssm_w_in, ssm_a_re, ssm_a_im, ssm_log_dt, ssm_b_re, ssm_b_im, ssm_c_re, ssm_c_im,
              ssm_d, ssm_w_glu, ssm_b_glu, ssm_w_out):
    for i in range(DEPTH):
        h = _rmsnorm(x, norm_g[i])
        j = i // N_MIXERS
        if i % N_MIXERS == 0:
            uz = h @ pool_w_in[j]
            u, z = uz[..., :D_INNER], uz[..., D_INNER:]
            y = _pool_mixer(u, pool_w_grp[j], pool_scale[j])
            w_out = pool_w_out[j]
        else:
            uz = h @ ssm_w_in[j]
            u, z = uz[..., :D_INNER], uz[..., D_INNER:]
            y = _s5_mixer(u, ssm_a_re[j], ssm_a_im[j], ssm_log_dt[j], ssm_b_re[j], ssm_b_im[j],
                          ssm_c_re[j], ssm_c_im[j], ssm_d[j], ssm_w_glu[j], ssm_b_glu[j])
            w_out = ssm_w_out[j]
        gated = (y * jax.nn.silu(z.astype(jnp.float32))).astype(x.dtype)
        x = x + (gated @ w_out).astype(x.dtype)
    return _rmsnorm(x, final_norm_g)


_drawn_inputs = setup_inputs


def setup_inputs(seed=0):
    import zlib

    import numpy as np

    out = dict(_drawn_inputs(seed))
    spreads = {}
    factors = {'norm_g': 3.786,
     'final_norm_g': 7.648,
     'pool_scale': 16.601,
     'ssm_a_re': 64.0,
     'ssm_a_im': 45.12,
     'ssm_log_dt': 46.304,
     'ssm_b_re': 64.0,
     'ssm_b_im': 63.712,
     'ssm_c_re': 63.632,
     'ssm_c_im': 63.936,
     'ssm_b_glu': 64.0}
    for name, (base, spread) in spreads.items():
        noise = np.random.default_rng([zlib.crc32(name.encode()), seed]).standard_normal(out[name].shape)
        drawn = base * np.exp(spread * noise) if base else spread * noise
        out[name] = __import__('jax').numpy.asarray(drawn.astype(out[name].dtype))
    for name, factor in factors.items():
        out[name] = (out[name] * factor).astype(out[name].dtype)
    return out
```

```python
import math
from contextlib import ExitStack

import numpy as np
import concourse.bass as bass
from concourse import mybir

F32 = mybir.dt.float32
F32R = mybir.dt.float32r
I32 = mybir.dt.int32
ALU = mybir.AluOpType
ACT = mybir.ActivationFunctionType

P = 128
L = 256
D = 2048
E = 4096
DT = D // P
ET = E // P
WINDOWS = (2, 4, 8, 16)
GT = ET // len(WINDOWS)
PAD = 16
NS = 64
PG = 16
NPAIR = 128
NQUAD = NPAIR // 4
T = 4
NC = L // T
EPS = 1e-6

UK = 4
NW = 256
RAW = 4
SPLIT = 2


class Phase:

    def __init__(self, name, ktiles, blocks, body_blocks, prev):
        self.name = name
        self.upb = ktiles // UK
        self.blocks = blocks
        self.bb = body_blocks
        self.bodies = blocks // body_blocks
        self.bu = self.upb * body_blocks
        self.u0 = prev.u0 + prev.units if prev else 0
        self.g0 = prev.g0 + prev.blocks if prev else 0
        self.units = self.upb * blocks
        self.prev = prev


U0 = Phase("u0", DT, 16, 2, None)
Z0 = Phase("z0", DT, 16, 2, U0)
GR = Phase("grp", GT, 16, 4, Z0)
O0 = Phase("out0", ET, 8, 2, GR)
U2 = Phase("u2", DT, 16, 2, O0)
Z2 = Phase("z2", DT, 16, 2, U2)
GL = Phase("glu", ET, 16, 2, Z2)
O2 = Phase("out2", ET, 8, 2, GL)

V_NORM, V_FINAL, V_SCALE, V_BGLU, V_D = 0, 32, 48, 80, 112



def build_program(nc, x, norm_g, final_norm_g, pool_w_in, pool_w_grp, pool_scale, pool_w_out,
                  ssm_w_in, a_re, a_im, log_dt, b_re, b_im, c_re, c_im, ssm_d, w_glu, b_glu,
                  ssm_w_out, out):
    KB = 1024
    base = -(-nc.sbuf_base // 512) * 512
    A, B, C = base, base + 66 * KB, base + 130 * KB
    RING, MISC = base + 162 * KB, base + 194 * KB

    def at(name, shape, dt, offset):
        return nc.alloc_sbuf_tensor_at(name, shape, dt, offset=offset)

    h = at("h", [P, DT, 2, L], F32R, A)
    u0 = at("u0", [P, ET, PAD + L], F32, A + 32 * KB)
    u2 = at("u2", [P, ET, L], F32, A + 32 * KB)
    gated = at("gated", [P, ET, 2, L], F32R, A)
    xrows = at("xrows", [P, 2, D], F32, A + 32 * KB)
    orows = at("orows", [P, 2, D], F32, A)
    m2ring = at("m2ring", [P, 2, 2, 4, T, 32], F32, A)
    bdring = at("bdring", [P, 2, T, P], F32, A + 8 * KB)
    state = at("state", [P, 2, 2, 4, NC], F32, A + 12 * KB)
    rec1 = at("rec1", [P, NQUAD, 2, 4], F32, A + 64 * KB)
    rec2 = at("rec2", [P, NQUAD, 2, 4], F32, A + 65 * KB)
    pooled = at("pooled", [P, ET, 2, L], F32R, B)
    pwin_b = at("pwin_b", [P, ET, 2 * L], F32, B)
    XS = at("XS", [P, NQUAD, 2, 4, NC], F32, B)
    g = at("g", [P, ET, 2, L], F32R, B)
    BT = at("BT", [P, 2, NPAIR, PG], F32, B)
    CT = at("CT", [P, 2, NPAIR, PG], F32, B + 16 * KB)
    PW = at("PW", [P, 2, NPAIR, 2 * T], F32, B + 32 * KB)
    MB = at("MB", [P, 2, 2, 4, T, 2, PG], F32, B + 40 * KB)
    MC = at("MC", [P, 2, 2, 4, T + 1, 2, PG], F32, B + 48 * KB)
    prodb = at("prodb", [P, 4, 4, T, PG], F32, B + 58 * KB)
    bdst = [at(f"bdst{i}", [P, T, 4, 32], F32, o) for i, o in enumerate((B + 62 * KB, C + 29 * KB))]
    zs = at("zs", [P, ET, L], F32, C)
    xT = at("xT", [P, DT, L], F32, C)
    praw = at("praw", [P, 4, NPAIR * PG], F32, C)
    m1st = at("m1st", [P, 2, 2, 4, P], F32, C + 16 * KB)
    prodc = at("prodc", [P, 4, 4, T + 1, PG], F32, C + 24 * KB)
    m1ring = at("m1ring", [P, 2, 2, 2, 4, P], F32, C + 16 * KB)
    uj = at("uj", [P, 2, 2, 4, NC], F32, C + 12 * KB)
    raw = [at(f"raw{i}", [P, UK, NW], F32, RING + i * 4 * KB) for i in range(RAW)]
    whi = [at(f"whi{i}", [P, UK, NW], F32R, RING + (16 + i * 8) * KB) for i in range(SPLIT)]
    wlo = [at(f"wlo{i}", [P, UK, NW], F32R, RING + (20 + i * 8) * KB) for i in range(SPLIT)]
    tmp = at("tmp", [P, 2, 2, L], F32, MISC)
    vrow = at("vrow", [P, 2, P], F32, MISC)
    v = at("v", [P, 2, 2, L], F32, MISC + 4 * KB)
    ident = at("ident", [P, P], F32, MISC + 8 * KB)
    ones = at("ones", [P, P], F32, MISC + 8 * KB + 512)
    qmask = at("qmask", [P, 4, 32], F32, MISC + 9 * KB)
    vec = at("vec", [P, 144], F32, MISC + 9 * KB + 512)
    a4a = at("a4a", [P, NQUAD, 2, 4], F32, MISC + 10 * KB + 512)
    a4b = at("a4b", [P, NQUAD, 2, 4], F32, MISC + 11 * KB + 512)
    pwin_a = at("pwin_a", [P, PAD + L], F32, MISC + 10 * KB + 512)
    corr = at("corr", [P, len(WINDOWS), PAD], F32, MISC + 12 * KB + 512)
    sw = [at(f"sw{i}", [P, P], F32, A + i * 512) for i in range(24)]
    swi = [at(f"swi{i}", [P, P], I32, A + 12 * KB + i * 512) for i in range(2)]
    ldt = at("ldt", [P, 2], F32, A + 13 * KB)
    bbar = at("bbar", [P, 2, NPAIR * PG], F32, A + 16 * KB)
    fbp = at("fbp", [P, 4, NPAIR * PG], F32, A + 32 * KB)

    ctx = ExitStack()
    with ctx:
        def sem(name):
            return ctx.enter_context(nc.semaphore(name))

        def psum(name, shape):
            return ctx.enter_context(nc.psum_tensor(name, shape, F32))

        acc = [psum(f"acc{i}", [P, 2, 512]) for i in range(2)]
        tb01 = psum("tb01", [P, 2, 512])
        tb2 = [psum(f"tb{i}", [P, 512]) for i in (2, 3)]

        m1_dram = nc.dram_tensor("m1_scratch", (NQUAD, P, 8 * P), F32).ap()
        m2_dram = nc.dram_tensor("m2_scratch", (NQUAD, P, 8 * T * 32), F32).ap()
        bd_dram = nc.dram_tensor("bd_scratch", (NQUAD, P, T * P), F32).ap()
        tab_dram = [nc.dram_tensor(f"tab_scratch{i}", (P, n), F32).ap()
                    for i, n in enumerate((2 * NPAIR * PG, 2 * NPAIR * PG, 2 * NPAIR * 2 * T))]
        x_dram = [nc.dram_tensor(f"x_scratch{i}", (P, DT * L), F32).ap() for i in range(2)]

        raw_loaded = [sem(f"raw_loaded{i}") for i in range(RAW)]
        hi_ready, lo_ready = sem("hi_ready"), sem("lo_ready")
        unit_done = sem("unit_done")
        tmp_ready, nb_evac = sem("tmp_ready"), sem("nb_evac")
        vec_loaded, params_loaded, x_loaded = sem("vec_loaded"), sem("params_loaded"), sem("x_loaded")
        consts = sem("consts")
        vec_turned, vec_ready = sem("vec_turned"), sem("vec_ready")
        chain = sem("chain")
        chain_done, par_turned, par_evac = sem("chain_done"), sem("par_turned"), sem("par_evac")
        tab_stored, tab_back, tab_zeroed = sem("tab_stored"), sem("tab_back"), sem("tab_zeroed")
        prods_ready, mb_ready, mc_ready = sem("prods_ready"), sem("mb_ready"), sem("mc_ready")
        quad_turned, k_ready = sem("quad_turned"), sem("k_ready")
        m1_evac, bd_ready = sem("m1_evac"), sem("bd_ready")
        m1_stored = [sem(f"m1_stored{i}") for i in range(2)]
        m2_stored = [sem(f"m2_stored{i}") for i in range(2)]
        bd_stored = [sem(f"bd_stored{i}") for i in range(2)]
        xt_turned, xt_ready = sem("xt_turned"), sem("xt_ready")
        sq_ready, sq_summed = sem("sq_ready"), sem("sq_summed")
        norm_step, var_ready, root_ready = sem("norm_step"), sem("var_ready"), sem("root_ready")
        hn_ready, hn_hi, hn_lo = sem("hn_ready"), sem("hn_hi"), sem("hn_lo")
        x_stored, x_back = sem("x_stored"), sem("x_back")
        pool_step, pooled_ready = sem("pool_step"), sem("pooled_ready")
        silu_done = sem("silu_done")
        gated_ready, gated_hi, gated_lo = sem("gated_ready"), sem("gated_hi"), sem("gated_lo")
        resid_half = sem("resid_half")
        m1_loaded = [sem(f"m1_loaded{i}") for i in range(2)]
        uj_ready, m1_done, xs_ready = sem("uj_ready"), sem("m1_done"), sem("xs_ready")
        rec_a, rec_b, rec_half, rec_done = sem("rec_a"), sem("rec_b"), sem("rec_half"), sem("rec_done")
        m2_loaded = [sem(f"m2_loaded{i}") for i in range(2)]
        state_ready = sem("state_ready")
        y_done, yd_ready, gelu_ready = sem("y_done"), sem("yd_ready"), sem("gelu_ready")
        g_hi, g_lo, gz_ready = sem("g_hi"), sem("g_lo"), sem("gz_ready")
        sig_ready = sem("sig_ready")
        out_turned, out_evac, out_stored = sem("out_turned"), sem("out_evac"), sem("out_stored")

        block = ctx.enter_context(nc.Block())

        tables = [(BT[:].rearrange("p r q a -> p (r q a)"), tab_dram[0]),
                  (CT[:].rearrange("p r q a -> p (r q a)"), tab_dram[1]),
                  (PW[:].rearrange("p r q k -> p (r q k)"), tab_dram[2])]
        QUAD_AT = {s: k for k, s in enumerate(range(1, O0.bu, 2))}
        QUAD_AT_FIRST = {s: k for k, s in enumerate((7, 9, 10, 11, 12, 13, 14, 15))}
        QPB = O0.bu // 2

        def quad_at(first, s):
            return (QUAD_AT_FIRST if first else QUAD_AT).get(s)

        def bodies(eng, ph, body):
            body(0, True)
            with eng.Fori(1, ph.bodies) as i:
                body(i, False)

        def weight_rows(w):
            return w.rearrange("(k p) n -> p k n", p=P)

        ssm_cols = E // NW
        weights = {
            U0: (weight_rows(pool_w_in[0]), 0), Z0: (weight_rows(pool_w_in[0]), ssm_cols),
            GR: (weight_rows(pool_w_grp[0].rearrange("g k n -> (g k) n")), 0),
            O0: (weight_rows(pool_w_out[0]), 0),
            U2: (weight_rows(ssm_w_in[0]), 0), Z2: (weight_rows(ssm_w_in[0]), ssm_cols),
            GL: (weight_rows(w_glu[0]), 0), O2: (weight_rows(ssm_w_out[0]), 0),
        }

        @block.sync
        def _(sp):
            row = 0
            for vector, n in ((norm_g.rearrange("a (t p) -> (a t) p", p=P), 32),
                              (final_norm_g.rearrange("(t p) -> t p", p=P), 16),
                              (pool_scale.rearrange("a (t p) -> (a t) p", p=P), 32),
                              (b_glu.rearrange("a (t p) -> (a t) p", p=P), 32)):
                sp.dma_start(vrow[row:row + n, 0, :], vector).then_inc(vec_loaded, 16)
                row += n
            sp.dma_start(vrow[0:32, 1, :], ssm_d.rearrange("a (t p) -> (a t) p", p=P)).then_inc(vec_loaded, 16)
            sp.dma_start(sw[0][:], a_re[0].rearrange("(q s) n -> q (s n)", s=2)).then_inc(params_loaded, 16)
            sp.dma_start(sw[1][:], a_im[0].rearrange("(q s) n -> q (s n)", s=2)).then_inc(params_loaded, 16)
            sp.dma_start(ldt[:], log_dt[0].rearrange("(q s) -> q s", s=2)).then_inc(params_loaded, 16)
            for i, par in enumerate((b_re, b_im)):
                sp.dma_start(praw[:, i, :], par[0].rearrange("(q s) a b -> q (s a b)", s=2)).then_inc(params_loaded, 16)
            for i, par in enumerate((c_re, c_im)):
                for s in range(2):
                    sp.dma_start(praw[:, 2 + i, :].rearrange("q (a s n) -> q s a n", a=PG, s=2)[:, s],
                                 par[0].rearrange("(q s) a n -> q s a n", s=2)[:, s]).then_inc(params_loaded, 16)

            def load_unit(ph, i, s):
                w, col0 = weights[ph]
                U = ph.u0 + i * ph.bu + s
                b, su = divmod(s, ph.upb)
                if ph is GR:
                    k0, col = i * GT + su * UK, b * NW
                else:
                    k0, col = su * UK, (col0 + b) * NW + i * (ph.bb * NW)
                if ph.u0 + s >= RAW or not isinstance(i, int):
                    sp.wait_ge(lo_ready, U - RAW + 1)
                dst = raw[s % RAW]
                src = w[:, bass.ds(k0, UK), bass.ds(col, NW)]
                sp.dma_start(dst[:], src).then_inc(raw_loaded[s % RAW], 16)

            sp.wait_ge(par_turned, 16)
            sp.dma_start(xrows[:], x[0].rearrange("(s p) d -> p s d", p=P)).then_inc(x_loaded, 16)

            def plain(ph):
                def body(i, first):
                    for s in range(ph.bu):
                        load_unit(ph, i, s)
                return body

            def out0_body(i, first):
                for s in range(O0.bu):
                    load_unit(O0, i, s)
                    if first and s == 3:
                        sp.wait_ge(unit_done, O0.u0)
                        sp.wait_ge(tab_stored, 16 * 3)
                        for sbuf, dram in tables:
                            sp.dma_start(sbuf, dram).then_inc(tab_back, 16)
                    if first and s == O0.upb - 1:
                        sp.wait_ge(gated_ready, GR.blocks)
                        sp.wait_ge(x_stored, 16)
                        sp.dma_start(xT[:], x_dram[0].rearrange("p (t l) -> p t l", t=DT)).then_inc(x_back, 16)

            def u2_body(i, first):
                for b in range(U2.bb):
                    for su in range(U2.upb):
                        load_unit(U2, i, b * U2.upb + su)
                    if first and b == 0:
                        for st in m1_stored + bd_stored:
                            sp.wait_ge(st, 8 * NQUAD)
                        sp.wait_ge(gated_ready, GR.blocks)
                    if not first:
                        sp.wait_ge(m1_done, 2 * (i * 2 + b) - 2)
                    src = m1_dram[bass.ds(i * 4 + 2 * b, 2)].rearrange("q p m -> p q m")
                    sp.dma_start(m1ring[:, b].rearrange("p q r s m -> p q (r s m)"), src).then_inc(m1_loaded[b], 16)

            def load_quad(i, b):
                src2 = m2_dram[bass.ds(i * 2 + b, 1)].rearrange("q p m -> p (q m)")
                srcb = bd_dram[bass.ds(i * 2 + b, 1)].rearrange("q p m -> p (q m)")
                sp.dma_start(m2ring[:, b].rearrange("p r s j m -> p (r s j m)"), src2).then_inc(m2_loaded[b], 16)
                sp.dma_start(bdring[:, b].rearrange("p l m -> p (l m)"), srcb).then_inc(m2_loaded[b], 16)

            def glu_body(i, first):
                for s in range(GL.bu):
                    load_unit(GL, i, s)
                    if first and s == 3:
                        sp.wait_ge(unit_done, GL.u0)
                        for st in m2_stored + bd_stored:
                            sp.wait_ge(st, 8 * NQUAD)
                        load_quad(0, 0)
                        load_quad(0, 1)
                        with sp.Fori(1, NQUAD // 2) as j:
                            for b in range(2):
                                sp.wait_ge(y_done, 2 * j + b - 1)
                                load_quad(j, b)

            def out2_body(i, first):
                for s in range(O2.bu):
                    load_unit(O2, i, s)
                    if first and s == O2.upb - 1:
                        sp.wait_ge(gated_ready, GR.blocks + GL.blocks)
                        sp.wait_ge(x_stored, 32)
                        sp.dma_start(xT[:], x_dram[1].rearrange("p (t l) -> p t l", t=DT)).then_inc(x_back, 16)

            bodies(sp, U0, plain(U0))
            bodies(sp, Z0, plain(Z0))
            bodies(sp, GR, plain(GR))
            bodies(sp, O0, out0_body)
            bodies(sp, U2, u2_body)
            bodies(sp, Z2, plain(Z2))
            bodies(sp, GL, glu_body)
            bodies(sp, O2, out2_body)
            for n in range(DT // 4):
                sp.wait_ge(out_evac, 2 * (n + 1))
                sp.dma_start(out[0].rearrange("(s p) d -> p s d", p=P)[:, :, n * 512:(n + 1) * 512],
                             orows[:, :, n * 512:(n + 1) * 512]).then_inc(out_stored, 16)
            sp.wait_ge(out_stored, 16 * (DT // 4))

        @block.gpsimd
        def _(pool):
            pool.memset(ident[:], 0.0).then_inc(consts, 1)
            pool.memset(ones[:], 1.0).then_inc(consts, 1)
            pool.memset(qmask[:], 0.0).then_inc(consts, 1)
            pool.wait_ge(consts, 3)
            pool.affine_select(out=ident[:], in_=ident[:], compare_op=ALU.not_equal, fill=1.0, base=0,
                               pattern=[[-1, P]], channel_multiplier=1).then_inc(consts, 1)
            for q in range(4):
                pool.wait_ge(consts, 4 + q)
                pool.memset(qmask[32 * q:32 * q + 32, q, :], 1.0).then_inc(consts, 1)
            pool.wait_ge(consts, 8)
            for wi, w in enumerate(WINDOWS):
                pool.memset(corr[:, wi, w - 1:], 1.0 / w).then_inc(consts, 1)
                for t in range(w - 1):
                    pool.memset(corr[:, wi, t:t + 1], 1.0 / (t + 1)).then_inc(consts, 1)

            pool.wait_ge(xt_ready, 8)
            pool.memset(u0[:, :, 0:PAD], 0.0).then_inc(pool_step, 1)
            pool.wait_ge(tab_stored, 16 * 3)
            steps = 1
            for wi, w in enumerate(WINDOWS):
                nd = wi + 1
                per = nd + 4
                with pool.Fori(0, GT // 2) as i:
                    for b in range(2):
                        t = wi * GT + i * 2 + b
                        at0 = steps + i * (2 * per) + b * per
                        if b == 0:
                            pool.wait_ge(nb_evac, wi * (GT // 2) + i + 1)
                        src = u0[:, bass.ds(t, 1), :].rearrange("p a l -> p (a l)")
                        spot = pwin_b[:, bass.ds(t, 1), :].rearrange("p a l -> p (a l)")
                        bufs = (pwin_a[:], spot)
                        if nd % 2 == 0:
                            order = (0, 1)
                        else:
                            order = (1, 0)
                        cur, lo = src, 0
                        for k in range(nd):
                            sh = 1 << k
                            lo += sh
                            dst = bufs[order[k % 2]]
                            pool.wait_ge(pool_step, at0 + k)
                            pool.tensor_tensor(dst[:, lo:PAD + L], cur[:, lo:PAD + L],
                                               cur[:, lo - sh:PAD + L - sh], ALU.add).then_inc(pool_step, 1)
                            cur = dst
                        pool.wait_ge(pool_step, at0 + nd)
                        pool.tensor_tensor(pwin_a[:, PAD:2 * PAD], cur[:, PAD:2 * PAD], corr[:, wi, :], ALU.mult)
                        pool.tensor_tensor(pwin_a[:, 2 * PAD:], cur[:, 2 * PAD:PAD + L],
                                           corr[:, wi, PAD - 1:].to_broadcast([P, L - PAD]),
                                           ALU.mult).then_inc(pool_step, 1)
                        pool.wait_ge(pool_step, at0 + nd + 1)
                        pool.tensor_tensor(pwin_a[:, PAD:], pwin_a[:, PAD:], src[:, PAD:PAD + L],
                                           ALU.subtract).then_inc(pool_step, 1)
                        pool.wait_ge(pool_step, at0 + nd + 2)
                        hi = pooled[:, bass.ds(t, 1), 0, :].rearrange("p a l -> p (a l)")
                        low = pooled[:, bass.ds(t, 1), 1, :].rearrange("p a l -> p (a l)")
                        pool.tensor_copy(hi, pwin_a[:, PAD:]).then_inc(pool_step, 1)
                        pool.wait_ge(pool_step, at0 + nd + 3)
                        pool.tensor_tensor(low, pwin_a[:, PAD:], hi.bitcast(F32), ALU.subtract).then_inc(pool_step, 1)
                    pool.wait_ge(pool_step, steps + i * (2 * per) + 2 * per)
                    pool.sem_inc(pooled_ready, 1)
                steps += per * GT

            pool.wait_ge(unit_done, O0.u0)
            pool.memset(MB[:], 0.0).then_inc(tab_zeroed, 1)
            pool.memset(MC[:], 0.0).then_inc(tab_zeroed, 1)
            pool.wait_ge(gated_ready, GR.blocks)
            pool.wait_ge(tab_back, 16 * 3)

            def quad_products(i):
                for src, K, pr, used in ((BT, T, prodb, mb_ready), (CT, T + 1, prodc, mc_ready)):
                    if not isinstance(i, int):
                        pool.wait_ge(used, i)
                    for n, (r, part) in enumerate(((0, 0), (1, 1), (0, 1), (1, 0))):
                        in0 = src[:, r, bass.ds(i * 4, 4), :].unsqueeze(2).to_broadcast([P, 4, K, PG])
                        powers = slice(0, T) if src is BT else slice(T - 1, 2 * T)
                        pw = PW[:, part, bass.ds(i * 4, 4), powers]
                        ins = pool.tensor_tensor(pr[:, n], in0, pw.unsqueeze(3).to_broadcast([P, 4, K, PG]), ALU.mult)
                    ins.then_inc(prods_ready, 1)

            quad_products(0)
            with pool.Fori(1, NQUAD) as i:
                quad_products(i)

            pool.wait_ge(xs_ready, NQUAD)
            with pool.Fori(0, 7) as i:
                for k in range(9):
                    c1 = i * 9 + k
                    pool.wait_ge(rec_done, c1 + 1)
                    src = XS[:, :, :, :, bass.ds(c1, 1)].rearrange("p a r s c -> p a r (s c)")
                    pool.tensor_tensor(rec2[:, :, ::-1, :], a4b[:], src, ALU.mult).then_inc(rec_b, 1)

            pool.wait_ge(silu_done, Z0.blocks + Z2.blocks)
            with pool.Fori(0, NQUAD // 2) as i:
                for b in range(2):
                    qd = i * 2 + b
                    pool.wait_ge(gelu_ready, qd + 1)
                    z = zs[:, bass.ds(qd, 1), :].rearrange("p a l -> p (a l)")
                    pool.tensor_tensor(z, z, tmp[:, b, 1, :], ALU.mult).then_inc(gz_ready, 1)

        @block.scalar
        def _(act):
            def split(ph, i, s):
                U = ph.u0 + i * ph.bu + s
                act.wait_ge(raw_loaded[s % RAW], 16 * ((ph.u0 + s) // RAW + 1) + i * (16 * ph.bu // RAW))
                if ph.u0 + s >= SPLIT or not isinstance(i, int):
                    act.wait_ge(unit_done, U - SPLIT + 1)
                act.copy(whi[s % SPLIT][:], raw[s % RAW][:]).then_inc(hi_ready, 1)

            def evac(ph, i, b):
                G = ph.g0 + i * ph.bb + b
                act.wait_ge(unit_done, ph.u0 + i * ph.bu + (b + 1) * ph.upb)
                if ph is U0 and (b > 0 or not isinstance(i, int)):
                    act.wait_ge(nb_evac, G)
                elif ph is not U0:
                    act.wait_ge(nb_evac, G - 1)
                act.copy(tmp[:, b % 2], acc[b % 2][:, :, L:2 * L]).then_inc(tmp_ready, 1)

            def before(ph, i, b, lag):
                b -= lag
                if b < 0:
                    b += ph.bb
                    i = i - 1
                return i, b

            def silu(ph, i, b):
                act.wait_ge(nb_evac, ph.g0 + i * ph.bb + b + 1)
                act.activation(zs[:, bass.ds(i * (2 * ph.bb) + 2 * b, 2), :], v[:, b % 2], ACT.Silu)\
                   .then_inc(silu_done, 1)

            def gated_round(ph, i, b, counted):
                n = counted + i * ph.bb + b
                act.wait_ge(gated_ready, n + 1)
                act.copy(gated[:, bass.ds(i * (2 * ph.bb) + 2 * b, 2), 0, :], v[:, b % 2]).then_inc(gated_hi, 1)

            act.wait_ge(vec_turned, 1)
            act.copy(vec[:, 0:112], tb2[0][:, 0:112]).then_inc(vec_ready, 1)
            act.copy(vec[:, 112:144], tb2[0][:, 112:144]).then_inc(vec_ready, 1)

            n_par = [0]

            def par_out(dst, src, scale=None):
                act.wait_ge(par_turned, n_par[0] + 1)
                ins = act.copy(dst, src) if scale is None else act.mul(dst, src, scale)
                ins.then_inc(par_evac, 1)
                n_par[0] += 1

            for r in range(4):
                for p4 in range(PG // 4):
                    dst = (BT if r < 2 else CT)[:, r % 2, :, 4 * p4:4 * p4 + 4].rearrange("p q a -> p a q")
                    src = tb01[:, n_par[0] % 2, :].rearrange("p (a q) -> p a q", a=4)
                    par_out(dst, src, -1.0 if r == 3 else None)
            for r in range(2):
                src = tb01[:, n_par[0] % 2, :].rearrange("p (k q) -> p k q", k=T)
                act.wait_ge(par_turned, n_par[0] + 1)
                for k in range(1, T):
                    act.copy(PW[:, r, :, T - 1 - k], src[:, k - 1, :])
                par_out(PW[:, r, :, T:2 * T].rearrange("p q k -> p k q"), src)
            assert n_par[0] == N_PAR_EVAC

            act.wait_ge(chain_done, 1)
            act.wait_ge(par_evac, N_PAR_EVAC)
            for sbuf, dram in tables:
                act.dma_start(dram, sbuf).then_inc(tab_stored, 16)

            def quad_out(i, k):
                b, qd = k % 2, i * QPB + k
                act.wait_ge(quad_turned, qd + 1)
                if k >= 2 or not isinstance(i, int):
                    act.wait_ge(m1_stored[b], i * (8 * QPB) + 16 * (k // 2))
                act.copy(m1st[:, b].rearrange("p r s m -> p (r s m)"),
                         tb01[:].rearrange("p r m -> p (r m)")).then_inc(m1_evac, 1)
                act.wait_ge(m1_evac, qd + 1)
                act.dma_start(m1_dram[bass.ds(qd, 1)].rearrange("q p m -> p (q m)"),
                              m1st[:, b].rearrange("p r s m -> p (r s m)")).then_inc(m1_stored[b], 16)
                act.wait_ge(mc_ready, qd + 1)
                act.dma_start(m2_dram[bass.ds(qd, 1)].rearrange("q p (r m) -> p (q r) m", r=8),
                              MC[:, b, :, :, 1:T + 1].rearrange("p r s k g a -> p (r s) (k g a)"))\
                   .then_inc(m2_stored[b], 16)
                act.wait_ge(bd_ready, qd + 1)
                act.dma_start(bd_dram[bass.ds(qd, 1)].rearrange("q p m -> p (q m)"),
                              bdst[b][:].rearrange("p l s m -> p (l s m)")).then_inc(bd_stored[b], 16)

            for n in range(DT // 2):
                act.wait_ge(xt_turned, n + 1)
                act.copy(xT[:, 2 * n:2 * n + 2, :], tb01[:, n % 2, :].rearrange("p (t l) -> p t l", t=2))\
                   .then_inc(xt_ready, 1)
            act.wait_ge(xt_ready, DT // 2)
            act.dma_start(x_dram[0].rearrange("p (t l) -> p t l", t=DT), xT[:]).then_inc(x_stored, 16)

            def norm(which, final=False):
                for n in range(DT // 2):
                    if n >= 2:
                        act.wait_ge(sq_summed, which * 8 + n - 1)
                    act.activation(v[:, n % 2], xT[:, 2 * n:2 * n + 2, :], ACT.Square).then_inc(sq_ready, 1)
                act.wait_ge(var_ready, which + 1)
                act.activation(tmp[:, 0, 1, :], tmp[:, 0, 0, :], ACT.Sqrt).then_inc(root_ready, 1)
                if final:
                    for n in range(DT // 2):
                        act.wait_ge(out_turned, n + 1)
                        act.copy(orows[:, :, 256 * n:256 * n + 256],
                                 tb01[:, n % 2, :].rearrange("p (s c) -> p s c", s=2)).then_inc(out_evac, 1)
                    return
                for n in range(DT // 2):
                    act.wait_ge(hn_ready, which * 8 + n + 1)
                    act.copy(h[:, 2 * n:2 * n + 2, 0, :], v[:, n % 2]).then_inc(hn_hi, 1)

            norm(0)

            def u0_body(i, first):
                for b in range(U0.bb):
                    for su in range(U0.upb):
                        split(U0, i, b * U0.upb + su)
                        if su == 1 and not (first and b == 0):
                            evac(U0, *before(U0, i, b, 1))

            def z0_body(i, first):
                for b in range(Z0.bb):
                    for su in range(Z0.upb):
                        split(Z0, i, b * Z0.upb + su)
                        if first and b == 0:
                            if su == 1:
                                evac(U0, U0.bodies - 1, U0.bb - 1)
                                act.wait_ge(x_stored, 16)
                        elif su == 1:
                            evac(Z0, *before(Z0, i, b, 1))
                        elif su == 3:
                            silu(Z0, *before(Z0, i, b, 1))

            def grp_body(i, first):
                for b in range(GR.bb):
                    for su in range(GR.upb):
                        split(GR, i, b * GR.upb + su)
                        if su == 0 and not (first and b < 2):
                            gated_round(GR, *before(GR, i, b, 2), 0)
                        if su == 1:
                            if first and b == 0:
                                evac(Z0, Z0.bodies - 1, Z0.bb - 1)
                                silu(Z0, Z0.bodies - 1, Z0.bb - 1)
                                act.wait_ge(pooled_ready, ET // 2)
                            else:
                                evac(GR, *before(GR, i, b, 1))

            def out0_body(i, first):
                for b in range(O0.bb):
                    for su in range(O0.upb):
                        split(O0, i, b * O0.upb + su)
                        if first and b == 0:
                            if su == 0:
                                gated_round(GR, GR.bodies - 1, GR.bb - 2, 0)
                            if su == 1:
                                evac(GR, GR.bodies - 1, GR.bb - 1)
                            if su == 3:
                                gated_round(GR, GR.bodies - 1, GR.bb - 1, 0)
                        elif su == 1:
                            evac(O0, *before(O0, i, b, 1))
                        k = quad_at(first, b * O0.upb + su)
                        if k is not None and not (first and k == 0):
                            quad_out(i if k else i - 1, (k - 1) % QPB)

            def chunk_inputs_out(n):
                for tt in range(2):
                    act.wait_ge(m1_done, 2 * n + tt + 1)
                    act.copy(XS[:, bass.ds(2 * n + tt, 1)].rearrange("p a r s c -> p (a r s c)"),
                             tb01[:, tt, :]).then_inc(xs_ready, 1)

            def u2_body(i, first):
                for b in range(U2.bb):
                    for su in range(U2.upb):
                        split(U2, i, b * U2.upb + su)
                        if su == 1:
                            if first and b == 0:
                                quad_out(O0.bodies - 1, QPB - 1)
                                evac(O0, O0.bodies - 1, O0.bb - 1)
                                act.wait_ge(nb_evac, U2.g0)
                                act.dma_start(x_dram[1].rearrange("p (t l) -> p t l", t=DT), xT[:])\
                                   .then_inc(x_stored, 16)
                                norm(1)
                            else:
                                evac(U2, *before(U2, i, b, 1))
                        if su == 1 and not (first and b < 2):
                            chunk_inputs_out(i * 2 + b - 2)

            def z2_body(i, first):
                for b in range(Z2.bb):
                    for su in range(Z2.upb):
                        split(Z2, i, b * Z2.upb + su)
                        if first and b == 0:
                            if su == 1:
                                evac(U2, U2.bodies - 1, U2.bb - 1)
                                chunk_inputs_out(U2.blocks - 2)
                        elif su == 1:
                            evac(Z2, *before(Z2, i, b, 1))
                            if first:
                                chunk_inputs_out(U2.blocks - 1)
                        elif su == 3:
                            silu(Z2, *before(Z2, i, b, 1))

            def state_out(j, bb):
                act.copy(state[:, bb].rearrange("p r s c -> p (r s c)"),
                         XS[:, bass.ds(j * 2 + bb, 1)].rearrange("p a r s c -> p (a r s c)")).then_inc(state_ready, 1)

            def gelu_out(j, bb):
                qd = j * 2 + bb
                act.wait_ge(yd_ready, qd + 1)
                act.activation(tmp[:, bb, 1, :], tmp[:, bb, 0, :], ACT.Gelu_apprx_tanh).then_inc(gelu_ready, 1)
                act.wait_ge(gelu_ready, qd + 1)
                act.copy(g[:, bass.ds(qd, 1), 0, :].rearrange("p a l -> p (a l)"), tmp[:, bb, 1, :])\
                   .then_inc(g_hi, 1)

            def glu_body(i, first):
                for b in range(GL.bb):
                    for su in range(GL.upb):
                        split(GL, i, b * GL.upb + su)
                        if first and b == 0:
                            if su == 1:
                                evac(Z2, Z2.bodies - 1, Z2.bb - 1)
                                silu(Z2, Z2.bodies - 1, Z2.bb - 1)
                                act.wait_ge(rec_done, NC)
                                act.wait_ge(unit_done, GL.u0)
                                state_out(0, 0)
                                state_out(0, 1)
                                with act.Fori(1, NQUAD // 2) as j:
                                    for bb in range(2):
                                        act.wait_ge(y_done, 2 * j + bb - 1)
                                        state_out(j, bb)
                                        gelu_out(j - 1, bb)
                                gelu_out(NQUAD // 2 - 1, 0)
                                gelu_out(NQUAD // 2 - 1, 1)
                        elif su == 1:
                            if first:
                                act.wait_ge(gz_ready, NQUAD)
                            evac(GL, *before(GL, i, b, 1))
                        elif su == 3:
                            sigmoid(*before(GL, i, b, 1))
                        elif su == 5:
                            gated_round(GL, *before(GL, i, b, 1), GR.blocks)

            def sigmoid(i, b):
                act.wait_ge(nb_evac, GL.g0 + i * 2 + b + 1)
                for tt in range(2):
                    bias = vec[:, bass.ds(V_BGLU + i * 4 + b * 2 + tt, 1)]
                    ins = act.activation(v[:, b % 2, tt, :], v[:, b % 2, tt, :], ACT.Sigmoid, bias=bias)
                ins.then_inc(sig_ready, 1)

            def out2_body(i, first):
                for b in range(O2.bb):
                    for su in range(O2.upb):
                        split(O2, i, b * O2.upb + su)
                        if first and b == 0:
                            if su == 1:
                                evac(GL, GL.bodies - 1, GL.bb - 1)
                                sigmoid(GL.bodies - 1, GL.bb - 1)
                            if su == 3:
                                gated_round(GL, GL.bodies - 1, GL.bb - 1, GR.blocks)
                        elif su == 1:
                            evac(O2, *before(O2, i, b, 1))

            bodies(act, U0, u0_body)
            bodies(act, Z0, z0_body)
            bodies(act, GR, grp_body)
            bodies(act, O0, out0_body)
            bodies(act, U2, u2_body)
            bodies(act, Z2, z2_body)
            bodies(act, GL, glu_body)
            bodies(act, O2, out2_body)
            evac(O2, O2.bodies - 1, O2.bb - 1)
            act.wait_ge(nb_evac, O2.g0 + O2.blocks)
            norm(2, final=True)

        @block.vector
        def _(dve):
            done = [0]

            def step(ins):
                ins.then_inc(chain, 1)
                done[0] += 1
                dve.wait_ge(chain, done[0])

            def mul(o, a, b):
                step(dve.tensor_tensor(o, a, b, ALU.mult))

            def add(o, a, b):
                step(dve.tensor_tensor(o, a, b, ALU.add))

            def sub(o, a, b):
                step(dve.tensor_tensor(o, a, b, ALU.subtract))

            def affine(o, a, m, c):
                step(dve.tensor_scalar(o, a, m, c, ALU.mult, ALU.add))

            MAGIC = 12582912.0

            def nearest(o, a, m):
                affine(o, a, m, MAGIC)
                step(dve.tensor_scalar(o, o, MAGIC, None, ALU.subtract))

            def cody(c, *bits):
                parts, rest = [], c
                for b in bits:
                    e = math.floor(math.log2(abs(rest)))
                    q = 2.0 ** (e - b + 1)
                    parts.append(math.floor(rest / q) * q)
                    rest -= parts[-1]
                return parts + [float(np.float32(rest))]

            def reduce_by(o, a, k, parts):
                for n, part in enumerate(parts):
                    step(dve.scalar_tensor_tensor(o, k, -part, a if n == 0 else o, ALU.mult, ALU.add))

            def exp(o, a, t):
                k, r, e = t
                step(dve.tensor_scalar(o, a, -110.0, 90.0, ALU.max, ALU.min))
                nearest(k, o, 1.0 / math.log(2.0))
                reduce_by(r, o, k, cody(math.log(2.0), 9, 12))
                step(dve.tensor_scalar(e, r, 1.0 / math.factorial(7), None, ALU.mult))
                for n in range(6, 0, -1):
                    step(dve.scalar_tensor_tensor(e, e, 1.0 / math.factorial(n), r, ALU.add, ALU.mult))
                step(dve.tensor_scalar(e, e, 1.0, None, ALU.add))
                nearest(r, k, 0.5)
                sub(k, k, r)
                for half in (r, k):
                    pw = swi[0] if half is r else swi[1]
                    pw = pw[:, 0:half.shape[1]]
                    step(dve.tensor_scalar(half, half, 127.0, None, ALU.add))
                    step(dve.tensor_copy(pw, half))
                    step(dve.tensor_scalar(pw, pw, 23, None, ALU.logical_shift_left))
                    mul(e if half is r else o, e, pw.bitcast(F32))

            dve.wait_ge(params_loaded, 16 * 9)
            are, aim = sw[0][:], sw[1][:]
            dtv = sw[2][:, 0:2]
            exp(dtv, ldt[:], (sw[3][:, 0:2], sw[4][:, 0:2], sw[5][:, 0:2]))
            dtb = sw[2][:, 0:2].unsqueeze(2).to_broadcast([P, 2, NS])
            y, th, mag = sw[6][:], sw[7][:], sw[8][:]
            mul(y.rearrange("p (s n) -> p s n", s=2), are.rearrange("p (s n) -> p s n", s=2), dtb)
            mul(th.rearrange("p (s n) -> p s n", s=2), aim.rearrange("p (s n) -> p s n", s=2), dtb)
            exp(mag, y, (sw[3][:], sw[4][:], sw[5][:]))
            q, r, r2, m = sw[3][:], sw[4][:], sw[5][:], sw[6][:]
            nearest(q, th, 2.0 / math.pi)
            reduce_by(r, th, q, cody(math.pi / 2, 8, 11, 11))
            mul(r2, r, r)
            sn, cs = sw[9][:], sw[10][:]
            for o, top, low in ((sn, 9, 3), (cs, 8, 2)):
                sign = lambda n: -1.0 if n % 4 in (2, 3) else 1.0
                step(dve.tensor_scalar(o, r2, sign(top) / math.factorial(top), None, ALU.mult))
                for n in range(top - 2, low - 1, -2):
                    step(dve.scalar_tensor_tensor(o, o, sign(n) / math.factorial(n), r2, ALU.add, ALU.mult))
                step(dve.tensor_scalar(o, o, 1.0, None, ALU.add))
            mul(sn, sn, r)
            nearest(m, q, 0.25)
            step(dve.scalar_tensor_tensor(m, m, -4.0, q, ALU.mult, ALU.add))
            ab, cm, sm = sw[11][:], sw[12][:], sw[13][:]
            step(dve.tensor_scalar(ab, m, -1.0, None, ALU.mult))
            step(dve.tensor_tensor(ab, ab, m, ALU.max))
            affine(cm, ab, -1.0, 1.0)
            affine(sm, ab, -1.0, 2.0)
            mul(sm, sm, m)
            t0, t1 = sw[14][:], sw[15][:]
            co, si = sw[16][:], sw[17][:]
            mul(t0, cs, cm)
            mul(t1, sn, sm)
            sub(co, t0, t1)
            mul(t0, sn, cm)
            mul(t1, cs, sm)
            add(si, t0, t1)
            mul(co, co, mag)
            mul(si, si, mag)
            for k in range(2, T + 1):
                pr, pi = sw[14 + 2 * (k - 1)][:], sw[15 + 2 * (k - 1)][:]
                nr_, ni_ = sw[14 + 2 * k][:], sw[15 + 2 * k][:]
                mul(t0, pr, co)
                mul(t1, pi, si)
                sub(nr_, t0, t1)
                mul(t0, pr, si)
                mul(t1, pi, co)
                add(ni_, t0, t1)
            nr, den, fr, fi = sw[3][:], sw[4][:], sw[5][:], sw[6][:]
            step(dve.tensor_scalar(nr, co, -1.0, None, ALU.add))
            mul(t0, are, are)
            mul(t1, aim, aim)
            add(den, t0, t1)
            step(dve.reciprocal(den, den))
            mul(t0, nr, are)
            mul(t1, si, aim)
            add(fr, t0, t1)
            mul(fr, fr, den)
            mul(t0, si, are)
            mul(t1, nr, aim)
            sub(fi, t0, t1)
            mul(fi, fi, den)
            view = lambda a: a.rearrange("p (s a) -> p s a", a=PG)
            frb = fr.unsqueeze(2).to_broadcast([P, 2 * NS, PG])
            fib = fi.unsqueeze(2).to_broadcast([P, 2 * NS, PG])
            for n, (f, i_) in enumerate(((frb, 0), (fib, 1), (frb, 1), (fib, 0))):
                mul(view(fbp[:, n, :]), view(praw[:, i_, :]), f)
            sub(bbar[:, 0, :], fbp[:, 0, :], fbp[:, 1, :])
            add(bbar[:, 1, :], fbp[:, 2, :], fbp[:, 3, :])
            dve.memset(PW[:, 0, :, T - 1], 1.0).then_inc(chain, 1)
            dve.memset(PW[:, 1, :, T - 1], 0.0).then_inc(chain_done, 1)
            done[0] += 1

            def powers_for_recurrence():
                dve.wait_ge(tab_back, 16 * 3)
                for r_, scale, dst in ((0, 1.0, a4a[:, :, 0, :]), (0, 1.0, a4a[:, :, 1, :]),
                                       (1, 1.0, a4b[:, :, 0, :]), (1, -1.0, a4b[:, :, 1, :])):
                    pw = PW[:, r_, :, 2 * T - 1].rearrange("p (a s) -> p a s", s=4)
                    ins = dve.tensor_scalar(dst, pw, scale, None, ALU.mult)
                ins.then_inc(chain_done, 1)

            def quad_sums(i, k):
                b, qd = k % 2, i * QPB + k
                for M, pr, ready, minus in ((MB, prodb, mb_ready, 0), (MC, prodc, mc_ready, 1)):
                    dve.wait_ge(prods_ready, 2 * qd + minus + 1)
                    if k >= 2 or not isinstance(i, int):
                        if minus == 0:
                            dve.wait_ge(quad_turned, qd - 1)
                            dve.wait_ge(k_ready, qd - 1)
                        else:
                            dve.wait_ge(m2_stored[b], i * (8 * QPB) + 16 * (k // 2))
                    for r in range(2):
                        a_, b_ = (0, 1) if r == 0 else ((2, 3) if minus == 0 else (3, 2))
                        for half in range(2):
                            rows = slice(64 * half, 64 * half + 64)
                            ins = dve.tensor_tensor(M[rows, b, r, :, :, half, :], pr[rows, a_], pr[rows, b_],
                                                    ALU.subtract if r == minus else ALU.add)
                    ins.then_inc(ready, 1)

            def quad_blocks(i, k):
                b, qd = k % 2, i * QPB + k
                dve.wait_ge(k_ready, qd + 1)
                if k >= 2 or not isinstance(i, int):
                    dve.wait_ge(bd_stored[b], i * (8 * QPB) + 16 * (k // 2))
                src = tb2[b][:, 0:T * 32].rearrange("p (l m) -> p l m", l=T).unsqueeze(2).to_broadcast([P, T, 4, 32])
                mask = qmask[:].unsqueeze(1).to_broadcast([P, T, 4, 32])
                dve.tensor_tensor(bdst[b][:], src, mask, ALU.mult).then_inc(bd_ready, 1)

            norm_steps = [0]

            def nstep(ins):
                ins.then_inc(norm_step, 1)
                norm_steps[0] += 1
                dve.wait_ge(norm_step, norm_steps[0])

            def norm(which, v_gain, order, final=False):
                var, root, inv, t = tmp[:, 0, 0, :], tmp[:, 0, 1, :], tmp[:, 1, 0, :], tmp[:, 1, 1, :]
                dve.wait_ge(sq_summed, which * 8 + 8)
                dve.tensor_scalar(var, tb2[1][:, 0:L], 1.0 / D, EPS, ALU.mult, ALU.add).then_inc(var_ready, 1)
                dve.wait_ge(root_ready, which + 1)
                nstep(dve.reciprocal(inv, root))
                nstep(dve.tensor_tensor(t, inv, inv, ALU.mult))
                nstep(dve.tensor_tensor(t, t, var, ALU.mult))
                nstep(dve.tensor_scalar(t, t, -0.5, 1.5, ALU.mult, ALU.add))
                nstep(dve.tensor_tensor(inv, inv, t, ALU.mult))
                for n in range(DT // 2 + 1):
                    if n < DT // 2:
                        if n >= 2:
                            if final:
                                dve.wait_ge(out_turned, n - 1)
                            else:
                                dve.wait_ge(hn_lo, which * 8 + n - 1)
                        for tt in range(2):
                            ft = 2 * n + tt
                            o, i_, iv = v[:, n % 2, tt, :], xT[:, ft, :], inv
                            if order == "chunks":
                                o = o.rearrange("p (j c) -> p c j", j=T)
                                i_ = i_.rearrange("p (c j) -> p c j", j=T)
                                iv = iv.rearrange("p (c j) -> p c j", j=T)
                            ins = dve.scalar_tensor_tensor(o, i_, vec[:, v_gain + ft:v_gain + ft + 1], iv,
                                                           ALU.mult, ALU.mult)
                        ins.then_inc(hn_ready, 1)
                    if n >= 1 and not final:
                        m_ = n - 1
                        dve.wait_ge(hn_hi, which * 8 + n)
                        dve.tensor_tensor(h[:, 2 * m_:2 * m_ + 2, 1, :], v[:, m_ % 2],
                                          h[:, 2 * m_:2 * m_ + 2, 0, :].bitcast(F32), ALU.subtract)\
                           .then_inc(hn_lo, 1)

            dve.wait_ge(vec_ready, 2)
            norm(0, V_NORM, "tokens")

            def split(ph, i, s):
                U = ph.u0 + i * ph.bu + s
                dve.wait_ge(hi_ready, U + 1)
                dve.tensor_tensor(wlo[s % SPLIT][:], raw[s % RAW][:], whi[s % SPLIT][:].bitcast(F32),
                                  ALU.subtract).then_inc(lo_ready, 1)

            def before(ph, i, b, lag):
                b -= lag
                if b < 0:
                    b += ph.bb
                    i = i - 1
                return i, b

            def add_up(ph, i, b, dst):
                G = ph.g0 + i * ph.bb + b
                dve.wait_ge(tmp_ready, G + 1)
                dve.tensor_tensor(dst, acc[b % 2][:, :, 0:L], tmp[:, b % 2], ALU.add).then_inc(nb_evac, 1)

            def tiles(i, ph, b):
                return bass.ds(i * (2 * ph.bb) + 2 * b, 2)

            def gated_low(ph, i, b, counted):
                n = counted + i * ph.bb + b
                dve.wait_ge(gated_hi, n + 1)
                dve.tensor_tensor(gated[:, tiles(i, ph, b), 1, :], v[:, b % 2],
                                  gated[:, tiles(i, ph, b), 0, :].bitcast(F32), ALU.subtract).then_inc(gated_lo, 1)

            def u0_out(i, b):
                add_up(U0, i, b, u0[:, tiles(i, U0, b), PAD:PAD + L])

            def u0_body(i, first):
                for b in range(U0.bb):
                    for su in range(U0.upb):
                        split(U0, i, b * U0.upb + su)
                        if su == 1 and not (first and b == 0):
                            if first:
                                dve.wait_ge(xt_ready, 8)
                            u0_out(*before(U0, i, b, 1))

            def z_out(ph, i, b, counted):
                n = counted + i * ph.bb + b
                if not isinstance(i, int) or i * ph.bb + b > 0 or counted > 0:
                    dve.wait_ge(silu_done, n)
                add_up(ph, i, b, v[:, b % 2])

            def z0_body(i, first):
                for b in range(Z0.bb):
                    for su in range(Z0.upb):
                        split(Z0, i, b * Z0.upb + su)
                        if su == 1:
                            if first and b == 0:
                                u0_out(U0.bodies - 1, U0.bb - 1)
                            else:
                                z_out(Z0, *before(Z0, i, b, 1), 0)

            def grp_out(i, b):
                n = i * GR.bb + b
                if not (isinstance(i, int) and i == 0 and b < 2):
                    dve.wait_ge(gated_lo, n - 1)
                if isinstance(i, int) and i == 0 and b == 0:
                    dve.wait_ge(silu_done, Z0.blocks)
                add_up(GR, i, b, v[:, b % 2])
                dve.wait_ge(nb_evac, GR.g0 + n + 1)
                for tt in range(2):
                    ft = i * (2 * GR.bb) + 2 * b + tt
                    ins = dve.scalar_tensor_tensor(
                        v[:, b % 2, tt, :], v[:, b % 2, tt, :], vec[:, bass.ds(V_SCALE + ft, 1)],
                        zs[:, bass.ds(ft, 1), :].rearrange("p a l -> p (a l)"), ALU.mult, ALU.mult)
                ins.then_inc(gated_ready, 1)

            def grp_body(i, first):
                for b in range(GR.bb):
                    for su in range(GR.upb):
                        split(GR, i, b * GR.upb + su)
                        if su == 0 and not (first and b < 2):
                            gated_low(GR, *before(GR, i, b, 2), 0)
                        if su == 1:
                            if first and b == 0:
                                z_out(Z0, Z0.bodies - 1, Z0.bb - 1, 0)
                            else:
                                grp_out(*before(GR, i, b, 1))

            def resid(ph, i, b, order, counted):
                G = ph.g0 + i * ph.bb + b
                xv = xT[:, tiles(i, ph, b), :]
                hl, hh = tmp[:, b % 2], acc[b % 2][:, :, 0:L]
                if order == "chunks":
                    xv = xv.rearrange("p t (c j) -> p t c j", j=T)
                    hl = hl.rearrange("p t (j c) -> p t c j", j=T)
                    hh = hh.rearrange("p t (j c) -> p t c j", j=T)
                dve.wait_ge(tmp_ready, G + 1)
                dve.tensor_tensor(xv, xv, hl, ALU.add).then_inc(resid_half, 1)
                dve.wait_ge(resid_half, counted + i * ph.bb + b + 1)
                dve.tensor_tensor(xv, hh, xv, ALU.add).then_inc(nb_evac, 1)

            def out0_body(i, first):
                for b in range(O0.bb):
                    for su in range(O0.upb):
                        split(O0, i, b * O0.upb + su)
                        if first and b == 0:
                            if su == 0:
                                gated_low(GR, GR.bodies - 1, GR.bb - 2, 0)
                            if su == 1:
                                grp_out(GR.bodies - 1, GR.bb - 1)
                            if su == 3:
                                gated_low(GR, GR.bodies - 1, GR.bb - 1, 0)
                        elif su == 1:
                            if first:
                                dve.wait_ge(x_back, 16)
                            resid(O0, *before(O0, i, b, 1), "tokens", 0)
                        k = quad_at(first, b * O0.upb + su)
                        if k is not None:
                            if first and k == 0:
                                powers_for_recurrence()
                                dve.wait_ge(tab_zeroed, 2)
                                dve.wait_ge(consts, N_CONSTS)
                            quad_sums(i, k)
                            if not (first and k == 0):
                                quad_blocks(i if k else i - 1, (k - 1) % QPB)

            def u2_out(i, b):
                n = i * 2 + b
                add_up(U2, i, b, u2[:, tiles(i, U2, b), :])
                if isinstance(i, int) and i == 0 and b == 0:
                    dve.wait_ge(x_stored, 32)
                if not isinstance(i, int) or n > 0:
                    dve.wait_ge(m1_done, 2 * n)
                dve.wait_ge(nb_evac, U2.g0 + n + 1)
                for j in range(T):
                    for q in range(4):
                        ins = dve.tensor_scalar(uj[32 * j:32 * j + 32, b, :, q, :],
                                                u2[32 * q:32 * q + 32, tiles(i, U2, b), NC * j:NC * j + NC],
                                                1.0, None, ALU.mult)
                ins.then_inc(uj_ready, 1)

            def u2_body(i, first):
                for b in range(U2.bb):
                    for su in range(U2.upb):
                        split(U2, i, b * U2.upb + su)
                        if su == 1:
                            if first and b == 0:
                                quad_blocks(O0.bodies - 1, QPB - 1)
                                resid(O0, O0.bodies - 1, O0.bb - 1, "tokens", 0)
                                norm(1, V_NORM + DT, "chunks")
                            else:
                                u2_out(*before(U2, i, b, 1))

            def rec_products(k, i):
                c1 = i * 9 + k
                prev = XS[:, :, :, :, bass.ds(c1, 1)].rearrange("p a r s c -> p a r (s c)")
                dve.wait_ge(rec_done, c1 + 1)
                dve.tensor_tensor(rec1[:], a4a[:], prev, ALU.mult).then_inc(rec_a, 1)

            def rec_sums(k, i):
                c1 = i * 9 + k
                cur = XS[:, :, :, :, bass.ds(c1 + 1, 1)].rearrange("p a r s c -> p a r (s c)")
                dve.wait_ge(rec_a, c1 + 1)
                dve.tensor_tensor(cur, cur, rec1[:], ALU.add).then_inc(rec_half, 1)
                dve.wait_ge(rec_half, c1 + 1)
                dve.wait_ge(rec_b, c1 + 1)
                dve.tensor_tensor(cur, cur, rec2[:], ALU.add).then_inc(rec_done, 1)

            def z2_first():
                for b in range(Z2.bb):
                    for su in range(Z2.upb):
                        split(Z2, 0, b * Z2.upb + su)
                        if su == 1:
                            if b == 0:
                                u2_out(U2.bodies - 1, U2.bb - 1)
                            else:
                                z_out(Z2, 0, b - 1, Z0.blocks)

            def z2_body(i):
                for b in range(Z2.bb):
                    for su in range(Z2.upb):
                        s = b * Z2.upb + su
                        rec_products(s, i - 1)
                        split(Z2, i, s)
                        rec_sums(s, i - 1)
                        if su == 1:
                            z_out(Z2, *before(Z2, i, b, 1), Z0.blocks)
                rec_products(8, i - 1)
                rec_sums(8, i - 1)

            def glu_out(i, b):
                if not (isinstance(i, int) and i == 0 and b < 2):
                    dve.wait_ge(gated_lo, GR.blocks + i * 2 + b - 1)
                add_up(GL, i, b, v[:, b % 2])

            def glu_gate(i, b):
                dve.wait_ge(sig_ready, i * 2 + b + 1)
                dve.tensor_tensor(v[:, b % 2], v[:, b % 2], zs[:, tiles(i, GL, b), :], ALU.mult)\
                   .then_inc(gated_ready, 1)

            def y_skip(j, bb):
                qd = j * 2 + bb
                dve.wait_ge(y_done, qd + 1)
                if not isinstance(j, int):
                    dve.wait_ge(gz_ready, qd - 1)
                dve.scalar_tensor_tensor(tmp[:, bb, 0, :], u2[:, bass.ds(qd, 1), :].rearrange("p a l -> p (a l)"),
                                         vec[:, bass.ds(V_D + qd, 1)], tb2[bb][:, 0:L], ALU.mult, ALU.add)\
                   .then_inc(yd_ready, 1)

            def y_low(j, bb):
                qd = j * 2 + bb
                dve.wait_ge(g_hi, qd + 1)
                gv = g[:, bass.ds(qd, 1)].rearrange("p a r l -> p (a r) l")
                dve.tensor_tensor(gv[:, 1, :], tmp[:, bb, 1, :], gv[:, 0, :].bitcast(F32), ALU.subtract)\
                   .then_inc(g_lo, 1)

            def glu_body(i, first):
                for b in range(GL.bb):
                    for su in range(GL.upb):
                        split(GL, i, b * GL.upb + su)
                        if first and b == 0:
                            if su == 1:
                                z_out(Z2, Z2.bodies - 1, Z2.bb - 1, Z0.blocks)
                                for bb in range(2):
                                    y_skip(0, bb)
                                    y_low(0, bb)
                                with dve.Fori(1, NQUAD // 2) as j:
                                    for bb in range(2):
                                        y_skip(j, bb)
                                        y_low(j, bb)
                                dve.wait_ge(gz_ready, NQUAD)
                        elif su == 1:
                            glu_out(*before(GL, i, b, 1))
                        elif su == 3:
                            glu_gate(*before(GL, i, b, 1))
                        elif su == 5:
                            gated_low(GL, *before(GL, i, b, 1), GR.blocks)

            def out2_body(i, first):
                for b in range(O2.bb):
                    for su in range(O2.upb):
                        split(O2, i, b * O2.upb + su)
                        if first and b == 0:
                            if su == 1:
                                glu_out(GL.bodies - 1, GL.bb - 1)
                                glu_gate(GL.bodies - 1, GL.bb - 1)
                            if su == 3:
                                gated_low(GL, GL.bodies - 1, GL.bb - 1, GR.blocks)
                        elif su == 1:
                            if first:
                                dve.wait_ge(x_back, 32)
                            resid(O2, *before(O2, i, b, 1), "chunks", O0.blocks)

            bodies(dve, U0, u0_body)
            bodies(dve, Z0, z0_body)
            bodies(dve, GR, grp_body)
            bodies(dve, O0, out0_body)
            bodies(dve, U2, u2_body)
            z2_first()
            dve.wait_ge(xs_ready, NQUAD)
            dve.sem_inc(rec_done, 1)
            with dve.Fori(1, Z2.bodies) as i:
                z2_body(i)
            bodies(dve, GL, glu_body)
            bodies(dve, O2, out2_body)
            resid(O2, O2.bodies - 1, O2.bb - 1, "chunks", O0.blocks)
            norm(2, V_FINAL, "tokens", final=True)

        @block.tensor
        def _(pe):
            mm = pe.matmul

            def unit(ph, i, s, operand, ready=None, count=0):
                U = ph.u0 + i * ph.bu + s
                b, su = divmod(s, ph.upb)
                ps = acc[b % 2]
                pe.wait_ge(lo_ready, U + 1)
                if su == 0 and (ph.g0 + b >= 2 or not isinstance(i, int)):
                    pe.wait_ge(nb_evac, ph.g0 + i * ph.bb + b - 1)
                for kk in range(UK):
                    kt = su * UK + kk
                    if ready is not None and kt % 2 == 0:
                        pe.wait_ge(ready, count + kt // 2 + 1)
                    rhs = operand(kt)
                    for tt in range(2):
                        cols = slice(tt * P, tt * P + P)
                        mm(ps[:, tt, :], whi[s % SPLIT][:, kk, cols], rhs[:, 0:2, :],
                           start=(kt == 0), stop=False, skip_group_check=True)
                        ins = mm(ps[:, tt, 0:L], wlo[s % SPLIT][:, kk, cols], rhs[:, 0, :],
                                 start=False, stop=(su == ph.upb - 1 and kk == UK - 1), skip_group_check=True)
                ins.then_inc(unit_done, 1)

            pe.wait_ge(consts, N_CONSTS)
            pe.wait_ge(vec_loaded, 16 * 5)
            pe.transpose(tb2[0][:, 0:112], vrow[0:112, 0, :], ident[0:112, 0:112])
            pe.transpose(tb2[0][:, 112:144], vrow[0:32, 1, :], ident[0:32, 0:32]).then_inc(vec_turned, 1)

            pe.wait_ge(chain_done, 1)
            n_par = 0
            for r in range(4):
                for p4 in range(PG // 4):
                    if n_par >= 2:
                        pe.wait_ge(par_evac, n_par - 1)
                    for a in range(4):
                        p_ = 4 * p4 + a
                        if r < 2:
                            src = bbar[:, r, :].rearrange("q (s a) -> q s a", a=PG)[:, :, p_]
                        else:
                            src = praw[:, r, p_ * P:p_ * P + P]
                        ins = pe.transpose(tb01[:, n_par % 2, a * P:a * P + P], src, ident[:])
                    ins.then_inc(par_turned, 1)
                    n_par += 1
            for r in range(2):
                pe.wait_ge(par_evac, n_par - 1)
                for k in range(1, T + 1):
                    ins = pe.transpose(tb01[:, n_par % 2, (k - 1) * P:k * P], sw[14 + 2 * k + r][:], ident[:])
                ins.then_inc(par_turned, 1)
                n_par += 1

            def quad(i, k):
                b, qd = k % 2, i * QPB + k
                pe.wait_ge(mb_ready, qd + 1)
                if k or not isinstance(i, int):
                    pe.wait_ge(m1_evac, qd)
                for r in range(2):
                    for q in range(4):
                        ins = pe.transpose(tb01[:, r, q * P:q * P + P],
                                           MB[:, b, r, q].rearrange("p j g a -> p (j g a)"), ident[:])
                ins.then_inc(quad_turned, 1)
                pe.wait_ge(mc_ready, qd + 1)
                if k >= 2 or not isinstance(i, int):
                    pe.wait_ge(bd_ready, qd - 1)
                for q in range(4):
                    for r in range(2):
                        ins = mm(tb2[b][32 * q:32 * q + 32, 0:T * 32],
                                 MB[:, b, r, q, T - 1].rearrange("p g a -> p (g a)"),
                                 MC[:, b, r, q, 0:T].rearrange("p k g a -> p (k g a)"),
                                 start=(r == 0), stop=(r == 1))
                ins.then_inc(k_ready, 1)

            pe.wait_ge(x_loaded, 16)
            pe.wait_ge(par_evac, N_PAR_EVAC)
            for n in range(DT // 2):
                if n >= 2:
                    pe.wait_ge(xt_ready, n - 1)
                for tt in range(2):
                    for s in range(2):
                        ft = 2 * n + tt
                        ins = pe.transpose(tb01[:, n % 2, tt * L + s * P:tt * L + s * P + P],
                                           xrows[:, s, ft * P:ft * P + P], ident[:])
                ins.then_inc(xt_turned, 1)

            def sum_squares(which):
                if which == 0:
                    pe.wait_ge(vec_ready, 2)
                elif which == 1:
                    pe.wait_ge(bd_ready, NQUAD)
                else:
                    pe.wait_ge(yd_ready, NQUAD)
                for n in range(DT // 2):
                    pe.wait_ge(sq_ready, which * 8 + n + 1)
                    for tt in range(2):
                        ins = mm(tb2[1][:, 0:L], ones[:], v[:, n % 2, tt, :],
                                 start=(n == 0 and tt == 0), stop=(n == 7 and tt == 1))
                    ins.then_inc(sq_summed, 1)

            sum_squares(0)

            def h_operand(kt):
                return h[:, kt]

            def gated_operand(kt):
                return gated[:, kt]

            def u0_body(i, first):
                for s in range(U0.bu):
                    unit(U0, i, s, h_operand, hn_lo if first and s < U0.upb else None, 0)

            def z0_body(i, first):
                for s in range(Z0.bu):
                    unit(Z0, i, s, h_operand)

            def grp_body(i, first):
                for s in range(GR.bu):
                    def operand(kt):
                        return pooled[:, bass.ds(i * GT + kt, 1)].rearrange("p a r l -> p (a r) l")
                    unit(GR, i, s, operand, pooled_ready if s < GR.upb else None, i * (GT // 2))

            def out0_body(i, first):
                for s in range(O0.bu):
                    unit(O0, i, s, gated_operand, gated_lo if first and s < O0.upb else None, 0)
                    k = quad_at(first, s)
                    if k is not None:
                        quad(i, k)

            def m1_products(i, b):
                n = i * 2 + b
                pe.wait_ge(m1_loaded[b], i * 16 + 16)
                pe.wait_ge(uj_ready, n + 1)
                for tt in range(2):
                    if not (isinstance(i, int) and i == 0 and b == 0):
                        pe.wait_ge(xs_ready, 2 * n + tt - 1)
                    for r in range(2):
                        for q in range(4):
                            col = (r * 4 + q) * NC
                            ins = mm(tb01[:, tt, col:col + NC], m1ring[:, b, tt, r, q, :], uj[:, b, tt, q, :],
                                     start=True, stop=True)
                    ins.then_inc(m1_done, 1)

            def u2_body(i, first):
                for b in range(U2.bb):
                    for su in range(U2.upb):
                        unit(U2, i, b * U2.upb + su, h_operand,
                             hn_lo if first and b == 0 else None, 8)
                        if su == 3 and not (first and b == 0):
                            m1_products(i - 1, 1) if b == 0 else m1_products(i, 0)

            def z2_body(i, first):
                for b in range(Z2.bb):
                    for su in range(Z2.upb):
                        unit(Z2, i, b * Z2.upb + su, h_operand)
                        if first and b == 0 and su == 3:
                            m1_products(U2.bodies - 1, 1)

            def y_products(j, bb):
                qd = j * 2 + bb
                pe.wait_ge(m2_loaded[bb], j * 32 + 32)
                if not isinstance(j, int):
                    pe.wait_ge(yd_ready, qd - 1)
                ps = tb2[bb]
                ut = u2[:, bass.ds(qd, 1), :].rearrange("p a l -> p (a l)")
                for l in range(T):
                    mm(ps[:, NC * l:L], bdring[:, bb, l, :], ut[:, 0:L - NC * l],
                       start=(l == 0), stop=False, skip_group_check=True)
                pe.wait_ge(state_ready, qd + 1)
                for q in range(4):
                    for r in range(2):
                        for jt in range(T):
                            ins = mm(ps[32 * q:32 * q + 32, NC * jt + 1:NC * jt + NC],
                                     m2ring[:, bb, r, q, jt, :], state[:, bb, r, q, 0:NC - 1],
                                     start=False, stop=(q == 3 and r == 1), skip_group_check=True)
                ins.then_inc(y_done, 1)

            def g_operand(kt):
                return g[:, kt]

            def glu_body(i, first):
                if first:
                    pe.wait_ge(rec_done, NC)
                    y_products(0, 0)
                    y_products(0, 1)
                    with pe.Fori(1, NQUAD // 2) as j:
                        y_products(j, 0)
                        y_products(j, 1)
                    pe.wait_ge(g_lo, NQUAD)
                for s in range(GL.bu):
                    unit(GL, i, s, g_operand)

            def out2_body(i, first):
                for s in range(O2.bu):
                    unit(O2, i, s, gated_operand, gated_lo if first and s < O2.upb else None, GR.blocks)

            bodies(pe, U0, u0_body)
            bodies(pe, Z0, z0_body)
            bodies(pe, GR, grp_body)
            bodies(pe, O0, out0_body)
            sum_squares(1)
            bodies(pe, U2, u2_body)
            bodies(pe, Z2, z2_body)
            bodies(pe, GL, glu_body)
            bodies(pe, O2, out2_body)
            sum_squares(2)
            for n in range(DT // 2):
                pe.wait_ge(hn_ready, 16 + n + 1)
                if n >= 2:
                    pe.wait_ge(out_evac, n - 1)
                for s in range(2):
                    for tt in range(2):
                        ins = pe.transpose(tb01[:, n % 2, s * L + tt * P:s * L + tt * P + P],
                                           v[:, n % 2, tt, s * P:s * P + P], ident[:])
                ins.then_inc(out_turned, 1)


N_PAR_EVAC = 18
N_CONSTS = 3 + 1 + 4 + sum(WINDOWS)

_INS = ["x", "norm_g", "final_norm_g", "pool_w_in", "pool_w_grp", "pool_scale", "pool_w_out",
        "ssm_w_in", "ssm_a_re", "ssm_a_im", "ssm_log_dt", "ssm_b_re", "ssm_b_im", "ssm_c_re",
        "ssm_c_im", "ssm_d", "ssm_w_glu", "ssm_b_glu", "ssm_w_out"]
_OUT = (1, L, D)


def kernel(**inputs):
    import concourse.bacc as bacc
    from concourse.bass_utils import run_bass_kernel_spmd

    nc = bacc.Bacc("TRN2", target_bir_lowering=False, num_devices=1)
    arrays, args = {}, []
    for name in _INS:
        a = np.ascontiguousarray(inputs[name])
        arrays[f"in_{name}"] = a
        args.append(nc.dram_tensor(f"in_{name}", a.shape, mybir.dt.from_np(a.dtype), kind="ExternalInput").ap())
    args.append(nc.dram_tensor("out_0", _OUT, F32, kind="ExternalOutput").ap())
    build_program(nc, *args)
    r = run_bass_kernel_spmd(nc, [arrays], core_ids=[0])
    return r.results[0]["out_0"]
```

```python
import math
from contextlib import ExitStack

import numpy as np
import concourse.bass as bass
from concourse import mybir

F32 = mybir.dt.float32
F32R = mybir.dt.float32r
I32 = mybir.dt.int32
ALU = mybir.AluOpType
ACT = mybir.ActivationFunctionType

P = 128
L = 256
D = 2048
E = 4096
DT = D // P
ET = E // P
WINDOWS = (2, 4, 8, 16)
GT = ET // len(WINDOWS)
PAD = 16
NS = 64
PG = 16
NPAIR = 128
NQUAD = NPAIR // 4
T = 4
NC = L // T
EPS = 1e-6

UK = 4
NW = 256
RAW = 4
SPLIT = 2


class Phase:

    def __init__(self, name, ktiles, blocks, body_blocks, prev):
        self.name = name
        self.upb = ktiles // UK
        self.blocks = blocks
        self.bb = body_blocks
        self.bodies = blocks // body_blocks
        self.bu = self.upb * body_blocks
        self.u0 = prev.u0 + prev.units if prev else 0
        self.g0 = prev.g0 + prev.blocks if prev else 0
        self.units = self.upb * blocks
        self.prev = prev


U0 = Phase("u0", DT, 16, 2, None)
Z0 = Phase("z0", DT, 16, 2, U0)
GR = Phase("grp", GT, 16, 4, Z0)
O0 = Phase("out0", ET, 8, 2, GR)
U2 = Phase("u2", DT, 16, 2, O0)
Z2 = Phase("z2", DT, 16, 2, U2)
GL = Phase("glu", ET, 16, 2, Z2)
O2 = Phase("out2", ET, 8, 2, GL)

V_NORM, V_SCALE, V_BGLU, V_D = 0, 32, 64, 96



def build_program(nc, x, norm_g, final_norm_g, pool_w_in, pool_w_grp, pool_scale, pool_w_out,
                  ssm_w_in, a_re, a_im, log_dt, b_re, b_im, c_re, c_im, ssm_d, w_glu, b_glu,
                  ssm_w_out, out):
    KB = 1024
    base = -(-nc.sbuf_base // 512) * 512
    A, B, C = base, base + 66 * KB, base + 130 * KB
    RING, MISC = base + 162 * KB, base + 194 * KB

    def at(name, shape, dt, offset):
        return nc.alloc_sbuf_tensor_at(name, shape, dt, offset=offset)

    h = at("h", [P, DT, 2, L], F32R, A)
    u0 = at("u0", [P, ET, PAD + L], F32, A + 32 * KB)
    u2 = at("u2", [P, ET, L], F32, A + 32 * KB)
    gated = at("gated", [P, ET, 2, L], F32R, A)
    xrows = at("xrows", [P, 2, D], F32, A + 32 * KB)
    sqsum = at("sqsum", [P, 2, L], F32, A + 64 * KB)
    m2ring = at("m2ring", [P, 2, 2, 4, T, 32], F32, A)
    bdring = at("bdring", [P, 2, T, P], F32, A + 8 * KB)
    state = at("state", [P, 2, 2, 4, NC], F32, A + 12 * KB)
    rec1 = at("rec1", [P, NQUAD, 2, 4], F32, A + 64 * KB)
    rec2 = at("rec2", [P, NQUAD, 2, 4], F32, A + 65 * KB)
    pooled = at("pooled", [P, ET, 2, L], F32R, B)
    pwin_b = at("pwin_b", [P, ET, 2 * L], F32, B)
    XS = at("XS", [P, NQUAD, 2, 4, NC], F32, B)
    g = at("g", [P, ET, 2, L], F32R, B)
    orows = at("orows", [P, 2, D], F32, B)
    gain = at("gain", [P, D], F32, B + 16 * KB)
    last = at("last", [P, 2, 2, L], F32, B + 24 * KB)
    BT = at("BT", [P, 2, NPAIR, PG], F32, B)
    CT = at("CT", [P, 2, NPAIR, PG], F32, B + 16 * KB)
    PW = at("PW", [P, 2, NPAIR, 2 * T], F32, B + 32 * KB)
    MB = at("MB", [P, 2, 2, 4, T, 2, PG], F32, B + 40 * KB)
    MC = at("MC", [P, 2, 2, 4, T + 1, 2, PG], F32, B + 48 * KB)
    prodb = at("prodb", [P, 4, 4, T, PG], F32, B + 58 * KB)
    bdst = [at(f"bdst{i}", [P, T, 4, 32], F32, o) for i, o in enumerate((B + 62 * KB, C + 29 * KB))]
    zs = at("zs", [P, ET, L], F32, C)
    xT = at("xT", [P, DT, L], F32, C)
    m1st = at("m1st", [P, 2, 2, 4, P], F32, C + 16 * KB)
    prodc = at("prodc", [P, 4, 4, T + 1, PG], F32, C + 24 * KB)
    m1ring = at("m1ring", [P, 2, 2, 2, 4, P], F32, C + 16 * KB)
    uj = at("uj", [P, 2, 2, 4, NC], F32, C + 12 * KB)
    raw = [at(f"raw{i}", [P, UK, NW], F32, RING + i * 4 * KB) for i in range(RAW)]
    whi = [at(f"whi{i}", [P, UK, NW], F32R, RING + (16 + i * 8) * KB) for i in range(SPLIT)]
    wlo = [at(f"wlo{i}", [P, UK, NW], F32R, RING + (20 + i * 8) * KB) for i in range(SPLIT)]
    tmp = at("tmp", [P, 2, 2, L], F32, MISC)
    vrow = at("vrow", [P, P], F32, MISC)
    v = at("v", [P, 2, 2, L], F32, MISC + 4 * KB)
    ident = at("ident", [P, P], F32, MISC + 8 * KB)
    ones = at("ones", [P, P], F32, MISC + 8 * KB + 512)
    qmask = at("qmask", [P, 4, 32], F32, MISC + 9 * KB)
    vec = at("vec", [P, P], F32, MISC + 9 * KB + 512)
    a4a = at("a4a", [P, NQUAD, 2, 4], F32, MISC + 10 * KB + 512)
    a4b = at("a4b", [P, NQUAD, 2, 4], F32, MISC + 11 * KB + 512)
    pwin_a = at("pwin_a", [P, PAD + L], F32, MISC + 10 * KB + 512)
    corr = at("corr", [P, len(WINDOWS), PAD], F32, MISC + 12 * KB + 512)
    praw = at("praw", [P, 4, NPAIR * PG], F32, B)
    bbar = at("bbar", [P, 2, NPAIR * PG], F32, B + 32 * KB)
    fbp = at("fbp", [P, NPAIR * PG], F32, C)
    sw = [at(f"sw{i}", [P, P], F32, C + 16 * KB + i * 512) for i in range(24)]
    swi = [at(f"swi{i}", [P, P], I32, C + 28 * KB + i * 512) for i in range(2)]
    sden = at("sden", [P, P], F32, C + 29 * KB)
    ldt = at("ldt", [P, 2], F32, C + 30 * KB)
    BTst = at("BTst", [P, 2, NPAIR, PG], F32, B + 48 * KB)
    CTst = at("CTst", [P, 2, NPAIR, PG], F32, B)
    PWst = at("PWst", [P, 2, NPAIR, 2 * T], F32, C)

    ctx = ExitStack()
    with ctx:
        def sem(name):
            return ctx.enter_context(nc.semaphore(name))

        def psum(name, shape):
            return ctx.enter_context(nc.psum_tensor(name, shape, F32))

        acc = [psum(f"acc{i}", [P, 2, 512]) for i in range(2)]
        tb01 = psum("tb01", [P, 2, 512])
        tb2 = [psum(f"tb{i}", [P, 512]) for i in (2, 3)]

        m1_dram = nc.dram_tensor("m1_scratch", (NQUAD, P, 8 * P), F32).ap()
        m2_dram = nc.dram_tensor("m2_scratch", (NQUAD, P, 8 * T * 32), F32).ap()
        bd_dram = nc.dram_tensor("bd_scratch", (NQUAD, P, T * P), F32).ap()
        tab_dram = [nc.dram_tensor(f"tab_scratch{i}", (P, n), F32).ap()
                    for i, n in enumerate((2 * NPAIR * PG, 2 * NPAIR * PG, 2 * NPAIR * 2 * T))]
        x_dram = [nc.dram_tensor(f"x_scratch{i}", (P, DT * L), F32).ap() for i in range(2)]

        raw_loaded = [sem(f"raw_loaded{i}") for i in range(RAW)]
        hi_ready, lo_ready = sem("hi_ready"), sem("lo_ready")
        unit_done = sem("unit_done")
        tmp_ready, nb_evac = sem("tmp_ready"), sem("nb_evac")
        vec_loaded, params_loaded = sem("vec_loaded"), sem("params_loaded")
        x_loaded = [sem(f"x_loaded{i}") for i in range(2)]
        consts = sem("consts")
        vec_turned, vec_ready = sem("vec_turned"), sem("vec_ready")
        chain = sem("chain")
        chain_done, par_turned = sem("chain_done"), sem("par_turned")
        par_evac = [sem(f"par_evac{i}") for i in range(2)]
        den_ready, den_inverted = sem("den_ready"), sem("den_inverted")
        powers_turned, powers_ready = sem("powers_turned"), sem("powers_ready")
        tab_stored, tab_back, tab_zeroed = sem("tab_stored"), sem("tab_back"), sem("tab_zeroed")
        prods_ready, mb_ready, mc_ready = sem("prods_ready"), sem("mb_ready"), sem("mc_ready")
        quad_turned, k_ready = sem("quad_turned"), sem("k_ready")
        m1_evac, bd_ready = sem("m1_evac"), sem("bd_ready")
        m1_stored = [sem(f"m1_stored{i}") for i in range(2)]
        m2_stored = [sem(f"m2_stored{i}") for i in range(2)]
        bd_stored = [sem(f"bd_stored{i}") for i in range(2)]
        xt_turned, xt_ready = sem("xt_turned"), sem("xt_ready")
        sq_ready, sq_summed = sem("sq_ready"), sem("sq_summed")
        norm_step, var_ready, root_ready = sem("norm_step"), sem("var_ready"), sem("root_ready")
        hn_ready, hn_hi, hn_lo = sem("hn_ready"), sem("hn_hi"), sem("hn_lo")
        x_stored, x_back = sem("x_stored"), sem("x_back")
        pool_step, pooled_ready = sem("pool_step"), sem("pooled_ready")
        silu_done = sem("silu_done")
        gated_ready, gated_hi, gated_lo = sem("gated_ready"), sem("gated_hi"), sem("gated_lo")
        resid_half = sem("resid_half")
        m1_loaded = [sem(f"m1_loaded{i}") for i in range(2)]
        uj_ready, m1_done, xs_ready = sem("uj_ready"), sem("m1_done"), sem("xs_ready")
        rec_a, rec_b, rec_half, rec_done = sem("rec_a"), sem("rec_b"), sem("rec_half"), sem("rec_done")
        m2_loaded = [sem(f"m2_loaded{i}") for i in range(2)]
        state_ready = sem("state_ready")
        y_done, yd_ready, gelu_ready = sem("y_done"), sem("yd_ready"), sem("gelu_ready")
        g_hi, g_lo, gz_ready = sem("g_hi"), sem("g_lo"), sem("gz_ready")
        sig_ready = sem("sig_ready")
        out_turned, out_evac, out_stored = sem("out_turned"), sem("out_evac"), sem("out_stored")
        gain_loaded, out_ready, sq_added = sem("gain_loaded"), sem("out_ready"), sem("sq_added")

        block = ctx.enter_context(nc.Block())

        def flat(table):
            return table[:].rearrange("p r q a -> p (r q a)")

        QUAD_AT = {s: k for k, s in enumerate(range(1, O0.bu, 2))}
        QUAD_AT_FIRST = {s: k for k, s in enumerate((7, 9, 10, 11, 12, 13, 14, 15))}
        QPB = O0.bu // 2

        PAR_BODY = 4

        def quad_at(first, s):
            return (QUAD_AT_FIRST if first else QUAD_AT).get(s)

        def later(i):
            return not isinstance(i, int) or i > 0

        def u0_bodies(eng, body):
            body(0, True)
            with eng.Fori(1, PAR_BODY) as i:
                body(i, False)
            body(PAR_BODY, False, turning=True)
            with eng.Fori(PAR_BODY + 1, U0.bodies) as i:
                body(i, False)

        def bodies(eng, ph, body):
            body(0, True)
            with eng.Fori(1, ph.bodies) as i:
                body(i, False)

        def weight_rows(w):
            return w.rearrange("(k p) n -> p k n", p=P)

        ssm_cols = E // NW
        weights = {
            U0: (weight_rows(pool_w_in[0]), 0), Z0: (weight_rows(pool_w_in[0]), ssm_cols),
            GR: (weight_rows(pool_w_grp[0].rearrange("g k n -> (g k) n")), 0),
            O0: (weight_rows(pool_w_out[0]), 0),
            U2: (weight_rows(ssm_w_in[0]), 0), Z2: (weight_rows(ssm_w_in[0]), ssm_cols),
            GL: (weight_rows(w_glu[0]), 0), O2: (weight_rows(ssm_w_out[0]), 0),
        }

        def parameters_out(copy, n):
            table, r, col = (BTst, CTst)[n // 8], n // 4 % 2, n % 4 * 4
            return copy(table[:, r, :, col:col + 4].rearrange("p q a -> p a q"),
                        tb01[:, n % 2, :].rearrange("p (a q) -> p a q", a=4), -1.0 if n // 4 == 3 else 1.0)

        def powers_out(copy, r):
            src = tb2[r][:].rearrange("p (k q) -> p k q", k=T)
            for k in range(1, T):
                copy(PWst[:, r, :, T - 1 - k], src[:, k - 1, :], 1.0)
            return copy(PWst[:, r, :, T:2 * T].rearrange("p q k -> p k q"), src, 1.0)

        @block.sync
        def _(sp):
            for half in range(2):
                cols = slice(half * (D // 2), (half + 1) * (D // 2))
                sp.dma_start(xrows[:, :, cols], x[0].rearrange("(s p) d -> p s d", p=P)[:, :, cols])\
                  .then_inc(x_loaded[half], 16)
            for col, vector in ((V_NORM, norm_g), (V_SCALE, pool_scale), (V_BGLU, b_glu), (V_D, ssm_d)):
                sp.dma_start(vrow[col:col + 32, :], vector.rearrange("a (t p) -> (a t) p", p=P)).then_inc(vec_loaded, 16)

            def load_unit(ph, i, s):
                w, col0 = weights[ph]
                U = ph.u0 + i * ph.bu + s
                b, su = divmod(s, ph.upb)
                if ph is GR:
                    k0, col = i * GT + su * UK, b * NW
                else:
                    k0, col = su * UK, (col0 + b) * NW + i * (ph.bb * NW)
                if ph.u0 + s >= RAW or later(i):
                    sp.wait_ge(lo_ready, U - RAW + 1)
                dst = raw[s % RAW]
                src = w[:, bass.ds(k0, UK), bass.ds(col, NW)]
                sp.dma_start(dst[:], src).then_inc(raw_loaded[s % RAW], 16)

            def plain(ph):
                def body(i, first):
                    for s in range(ph.bu):
                        load_unit(ph, i, s)
                return body

            def out0_body(i, first):
                for s in range(O0.bu):
                    load_unit(O0, i, s)
                    if first and s == 3:
                        sp.wait_ge(unit_done, O0.u0)
                        sp.wait_ge(tab_stored, 16 * 3)
                        for table, dram in zip((BT, CT, PW), tab_dram):
                            sp.dma_start(flat(table), dram).then_inc(tab_back, 16)
                    if first and s == O0.upb - 1:
                        sp.wait_ge(gated_ready, GR.blocks)
                        sp.wait_ge(x_stored, 16)
                        sp.dma_start(xT[:], x_dram[0].rearrange("p (t l) -> p t l", t=DT)).then_inc(x_back, 16)

            def u2_body(i, first):
                for b in range(U2.bb):
                    for su in range(U2.upb):
                        load_unit(U2, i, b * U2.upb + su)
                    if first and b == 0:
                        for st in m1_stored + bd_stored:
                            sp.wait_ge(st, 8 * NQUAD)
                        sp.wait_ge(gated_ready, GR.blocks)
                    if not first:
                        sp.wait_ge(m1_done, 2 * (i * 2 + b) - 2)
                    src = m1_dram[bass.ds(i * 4 + 2 * b, 2)].rearrange("q p m -> p q m")
                    sp.dma_start(m1ring[:, b].rearrange("p q r s m -> p q (r s m)"), src).then_inc(m1_loaded[b], 16)

            def load_quad(i, b):
                src2 = m2_dram[bass.ds(i * 2 + b, 1)].rearrange("q p m -> p (q m)")
                srcb = bd_dram[bass.ds(i * 2 + b, 1)].rearrange("q p m -> p (q m)")
                sp.dma_start(m2ring[:, b].rearrange("p r s j m -> p (r s j m)"), src2).then_inc(m2_loaded[b], 16)
                sp.dma_start(bdring[:, b].rearrange("p l m -> p (l m)"), srcb).then_inc(m2_loaded[b], 16)

            def glu_body(i, first):
                for s in range(GL.bu):
                    load_unit(GL, i, s)
                    if first and s == 3:
                        sp.wait_ge(unit_done, GL.u0)
                        for st in m2_stored + bd_stored:
                            sp.wait_ge(st, 8 * NQUAD)
                        load_quad(0, 0)
                        load_quad(0, 1)
                        with sp.Fori(1, NQUAD // 2) as j:
                            for b in range(2):
                                sp.wait_ge(y_done, 2 * j + b - 1)
                                load_quad(j, b)

            def out2_body(i, first):
                for s in range(O2.bu):
                    load_unit(O2, i, s)
                    if first and s == 3:
                        sp.wait_ge(unit_done, O2.u0)
                        sp.dma_start(gain[:], final_norm_g.unsqueeze(0).to_broadcast([P, D])).then_inc(gain_loaded, 16)
                    if first and s == O2.upb - 1:
                        sp.wait_ge(gated_ready, GR.blocks + GL.blocks)
                        sp.wait_ge(x_stored, 32)
                        sp.dma_start(xT[:], x_dram[1].rearrange("p (t l) -> p t l", t=DT)).then_inc(x_back, 16)

            bodies(sp, U0, plain(U0))
            bodies(sp, Z0, plain(Z0))
            bodies(sp, GR, plain(GR))
            bodies(sp, O0, out0_body)
            bodies(sp, U2, u2_body)
            bodies(sp, Z2, plain(Z2))
            bodies(sp, GL, glu_body)
            bodies(sp, O2, out2_body)
            rows = out[0].rearrange("(s p) d -> p s d", p=P)
            for n in range(4):
                cols = slice(n // 2 * (D // 2), (n // 2 + 1) * (D // 2))
                sp.wait_ge(out_ready, n + 1)
                sp.dma_start(rows[:, n % 2, cols], orows[:, n % 2, cols]).then_inc(out_stored, 16)
            sp.wait_ge(out_stored, 16 * 4)

        @block.gpsimd
        def _(pool):
            pool.memset(ident[:], 0.0).then_inc(consts, 1)
            pool.memset(ones[:], 1.0).then_inc(consts, 1)
            pool.memset(qmask[:], 0.0).then_inc(consts, 1)
            pool.wait_ge(consts, 3)
            pool.affine_select(out=ident[:], in_=ident[:], compare_op=ALU.not_equal, fill=1.0, base=0,
                               pattern=[[-1, P]], channel_multiplier=1).then_inc(consts, 1)
            for q in range(4):
                pool.wait_ge(consts, 4 + q)
                pool.memset(qmask[32 * q:32 * q + 32, q, :], 1.0).then_inc(consts, 1)
            pool.wait_ge(consts, 8)
            for wi, w in enumerate(WINDOWS):
                pool.memset(corr[:, wi, w - 1:], 1.0 / w).then_inc(consts, 1)
                for t in range(w - 1):
                    pool.memset(corr[:, wi, t:t + 1], 1.0 / (t + 1)).then_inc(consts, 1)

            done = [0]

            def step(ins):
                ins.then_inc(chain, 1)
                done[0] += 1
                pool.wait_ge(chain, done[0])

            def mul(o, a, b):
                step(pool.tensor_tensor(o, a, b, ALU.mult))

            def add(o, a, b):
                step(pool.tensor_tensor(o, a, b, ALU.add))

            def sub(o, a, b):
                step(pool.tensor_tensor(o, a, b, ALU.subtract))

            def affine(o, a, m, c):
                step(pool.tensor_scalar(o, a, m, c, ALU.mult, ALU.add))

            MAGIC = 12582912.0

            def nearest(o, a, m):
                affine(o, a, m, MAGIC)
                step(pool.tensor_scalar(o, o, MAGIC, None, ALU.subtract))

            def cody(c, *bits):
                parts, rest = [], c
                for b in bits:
                    e = math.floor(math.log2(abs(rest)))
                    q = 2.0 ** (e - b + 1)
                    parts.append(math.floor(rest / q) * q)
                    rest -= parts[-1]
                return parts + [float(np.float32(rest))]

            def reduce_by(o, a, k, parts, t):
                for n, part in enumerate(parts):
                    step(pool.tensor_scalar(t, k, -part, None, ALU.mult))
                    add(o, a if n == 0 else o, t)

            def horner(o, c, r):
                step(pool.tensor_scalar(o, o, c, None, ALU.add))
                mul(o, o, r)

            def exp(o, a, t):
                k, r, e = t
                step(pool.tensor_scalar(o, a, -110.0, 90.0, ALU.max, ALU.min))
                nearest(k, o, 1.0 / math.log(2.0))
                reduce_by(r, o, k, cody(math.log(2.0), 9, 12), e)
                step(pool.tensor_scalar(e, r, 1.0 / math.factorial(7), None, ALU.mult))
                for n in range(6, 0, -1):
                    horner(e, 1.0 / math.factorial(n), r)
                step(pool.tensor_scalar(e, e, 1.0, None, ALU.add))
                nearest(r, k, 0.5)
                sub(k, k, r)
                for half in (r, k):
                    pw = swi[0] if half is r else swi[1]
                    pw = pw[:, 0:half.shape[1]]
                    affine(half, half, 2.0 ** 23, 127.0 * 2.0 ** 23)
                    step(pool.tensor_copy(pw, half))
                    mul(e if half is r else o, e, pw.bitcast(F32))

            pool.wait_ge(params_loaded, 16 * 9)
            are, aim = sw[0][:], sw[1][:]
            t0, t1, den = sw[14][:], sw[15][:], sden[:]
            mul(t0, are, are)
            mul(t1, aim, aim)
            add(den, t0, t1)
            pool.sem_inc(den_ready, 1)
            dtv = sw[2][:, 0:2]
            exp(dtv, ldt[:], (sw[3][:, 0:2], sw[4][:, 0:2], sw[5][:, 0:2]))
            dtb = sw[2][:, 0:2].unsqueeze(2).to_broadcast([P, 2, NS])
            y, th, mag = sw[6][:], sw[7][:], sw[8][:]
            mul(y.rearrange("p (s n) -> p s n", s=2), are.rearrange("p (s n) -> p s n", s=2), dtb)
            mul(th.rearrange("p (s n) -> p s n", s=2), aim.rearrange("p (s n) -> p s n", s=2), dtb)
            exp(mag, y, (sw[3][:], sw[4][:], sw[5][:]))
            q, r, r2, m = sw[3][:], sw[4][:], sw[5][:], sw[6][:]
            nearest(q, th, 2.0 / math.pi)
            reduce_by(r, th, q, cody(math.pi / 2, 8, 11, 11), r2)
            mul(r2, r, r)
            sn, cs = sw[9][:], sw[10][:]
            for o, top, low in ((sn, 9, 3), (cs, 8, 2)):
                sign = lambda n: -1.0 if n % 4 in (2, 3) else 1.0
                step(pool.tensor_scalar(o, r2, sign(top) / math.factorial(top), None, ALU.mult))
                for n in range(top - 2, low - 1, -2):
                    horner(o, sign(n) / math.factorial(n), r2)
                step(pool.tensor_scalar(o, o, 1.0, None, ALU.add))
            mul(sn, sn, r)
            nearest(m, q, 0.25)
            step(pool.tensor_scalar(m, m, -4.0, None, ALU.mult))
            add(m, m, q)
            ab, cm, sm = sw[11][:], sw[12][:], sw[13][:]
            step(pool.tensor_scalar(ab, m, 0.0, 2.0, ALU.max, ALU.mult))
            sub(ab, ab, m)
            affine(cm, ab, -1.0, 1.0)
            affine(sm, ab, -1.0, 2.0)
            mul(sm, sm, m)
            co, si = sw[16][:], sw[17][:]
            mul(t0, cs, cm)
            mul(t1, sn, sm)
            sub(co, t0, t1)
            mul(t0, sn, cm)
            mul(t1, cs, sm)
            add(si, t0, t1)
            mul(co, co, mag)
            mul(si, si, mag)
            for k in range(2, T + 1):
                pr, pi = sw[14 + 2 * (k - 1)][:], sw[15 + 2 * (k - 1)][:]
                nr_, ni_ = sw[14 + 2 * k][:], sw[15 + 2 * k][:]
                mul(t0, pr, co)
                mul(t1, pi, si)
                sub(nr_, t0, t1)
                mul(t0, pr, si)
                mul(t1, pi, co)
                add(ni_, t0, t1)
            nr, fr, fi = sw[3][:], sw[5][:], sw[6][:]
            step(pool.tensor_scalar(nr, co, -1.0, None, ALU.add))
            pool.wait_ge(den_inverted, 1)
            mul(t0, nr, are)
            mul(t1, si, aim)
            add(fr, t0, t1)
            mul(fr, fr, den)
            mul(t0, si, are)
            mul(t1, nr, aim)
            sub(fi, t0, t1)
            mul(fi, fi, den)
            view = lambda a: a.rearrange("p (s a) -> p s a", a=PG)
            frb = fr.unsqueeze(2).to_broadcast([P, 2 * NS, PG])
            fib = fi.unsqueeze(2).to_broadcast([P, 2 * NS, PG])
            pool.wait_ge(x_stored, 16)
            pool.wait_ge(hn_ready, DT // 2)
            mul(view(bbar[:, 0, :]), view(praw[:, 0, :]), frb)
            mul(view(fbp[:]), view(praw[:, 1, :]), fib)
            sub(bbar[:, 0, :], bbar[:, 0, :], fbp[:])
            mul(view(bbar[:, 1, :]), view(praw[:, 1, :]), frb)
            mul(view(fbp[:]), view(praw[:, 0, :]), fib)
            add(bbar[:, 1, :], bbar[:, 1, :], fbp[:])
            pool.sem_inc(chain_done, 1)

            pool.wait_ge(xt_ready, 8)
            pool.memset(u0[:, :, 0:PAD], 0.0).then_inc(pool_step, 1)
            pool.wait_ge(tab_stored, 16 * 3)
            steps = 1
            for wi, w in enumerate(WINDOWS):
                nd = wi + 1
                per = nd + 4
                with pool.Fori(0, GT // 2) as i:
                    for b in range(2):
                        t = wi * GT + i * 2 + b
                        at0 = steps + i * (2 * per) + b * per
                        if b == 0:
                            pool.wait_ge(nb_evac, wi * (GT // 2) + i + 1)
                        src = u0[:, bass.ds(t, 1), :].rearrange("p a l -> p (a l)")
                        spot = pwin_b[:, bass.ds(t, 1), :].rearrange("p a l -> p (a l)")
                        bufs = (pwin_a[:], spot)
                        if nd % 2 == 0:
                            order = (0, 1)
                        else:
                            order = (1, 0)
                        cur, lo = src, 0
                        for k in range(nd):
                            sh = 1 << k
                            lo += sh
                            dst = bufs[order[k % 2]]
                            pool.wait_ge(pool_step, at0 + k)
                            pool.tensor_tensor(dst[:, lo:PAD + L], cur[:, lo:PAD + L],
                                               cur[:, lo - sh:PAD + L - sh], ALU.add).then_inc(pool_step, 1)
                            cur = dst
                        pool.wait_ge(pool_step, at0 + nd)
                        pool.tensor_tensor(pwin_a[:, PAD:2 * PAD], cur[:, PAD:2 * PAD], corr[:, wi, :], ALU.mult)
                        pool.tensor_tensor(pwin_a[:, 2 * PAD:], cur[:, 2 * PAD:PAD + L],
                                           corr[:, wi, PAD - 1:].to_broadcast([P, L - PAD]),
                                           ALU.mult).then_inc(pool_step, 1)
                        pool.wait_ge(pool_step, at0 + nd + 1)
                        pool.tensor_tensor(pwin_a[:, PAD:], pwin_a[:, PAD:], src[:, PAD:PAD + L],
                                           ALU.subtract).then_inc(pool_step, 1)
                        pool.wait_ge(pool_step, at0 + nd + 2)
                        hi = pooled[:, bass.ds(t, 1), 0, :].rearrange("p a l -> p (a l)")
                        low = pooled[:, bass.ds(t, 1), 1, :].rearrange("p a l -> p (a l)")
                        pool.tensor_copy(hi, pwin_a[:, PAD:]).then_inc(pool_step, 1)
                        pool.wait_ge(pool_step, at0 + nd + 3)
                        pool.tensor_tensor(low, pwin_a[:, PAD:], hi.bitcast(F32), ALU.subtract).then_inc(pool_step, 1)
                    pool.wait_ge(pool_step, steps + i * (2 * per) + 2 * per)
                    pool.sem_inc(pooled_ready, 1)
                steps += per * GT

            pool.wait_ge(unit_done, O0.u0)
            pool.memset(MB[:], 0.0).then_inc(tab_zeroed, 1)
            pool.memset(MC[:], 0.0).then_inc(tab_zeroed, 1)
            pool.wait_ge(gated_ready, GR.blocks)
            pool.wait_ge(tab_back, 16 * 3)

            def quad_products(i):
                for src, K, pr, used in ((BT, T, prodb, mb_ready), (CT, T + 1, prodc, mc_ready)):
                    if later(i):
                        pool.wait_ge(used, i)
                    for n, (r, part) in enumerate(((0, 0), (1, 1), (0, 1), (1, 0))):
                        in0 = src[:, r, bass.ds(i * 4, 4), :].unsqueeze(2).to_broadcast([P, 4, K, PG])
                        powers = slice(0, T) if src is BT else slice(T - 1, 2 * T)
                        pw = PW[:, part, bass.ds(i * 4, 4), powers]
                        ins = pool.tensor_tensor(pr[:, n], in0, pw.unsqueeze(3).to_broadcast([P, 4, K, PG]), ALU.mult)
                    ins.then_inc(prods_ready, 1)

            quad_products(0)
            with pool.Fori(1, NQUAD) as i:
                quad_products(i)

            pool.wait_ge(xs_ready, NQUAD)
            with pool.Fori(0, 7) as i:
                for k in range(9):
                    c1 = i * 9 + k
                    pool.wait_ge(rec_done, c1 + 1)
                    src = XS[:, :, :, :, bass.ds(c1, 1)].rearrange("p a r s c -> p a r (s c)")
                    pool.tensor_tensor(rec2[:, :, ::-1, :], a4b[:], src, ALU.mult).then_inc(rec_b, 1)

            pool.wait_ge(silu_done, Z0.blocks + Z2.blocks)
            with pool.Fori(0, NQUAD // 2) as i:
                for b in range(2):
                    qd = i * 2 + b
                    pool.wait_ge(gelu_ready, qd + 1)
                    z = zs[:, bass.ds(qd, 1), :].rearrange("p a l -> p (a l)")
                    pool.tensor_tensor(z, z, tmp[:, b, 1, :], ALU.mult).then_inc(gz_ready, 1)

        @block.scalar
        def _(act):
            def split(ph, i, s):
                U = ph.u0 + i * ph.bu + s
                act.wait_ge(raw_loaded[s % RAW], 16 * ((ph.u0 + s) // RAW + 1) + i * (16 * ph.bu // RAW))
                if ph.u0 + s >= SPLIT or later(i):
                    act.wait_ge(unit_done, U - SPLIT + 1)
                act.copy(whi[s % SPLIT][:], raw[s % RAW][:]).then_inc(hi_ready, 1)

            def evac(ph, i, b):
                G = ph.g0 + i * ph.bb + b
                act.wait_ge(unit_done, ph.u0 + i * ph.bu + (b + 1) * ph.upb)
                if ph is U0 and (b > 0 or later(i)):
                    act.wait_ge(nb_evac, G)
                elif ph is not U0:
                    act.wait_ge(nb_evac, G - 1)
                act.copy(tmp[:, b % 2], acc[b % 2][:, :, L:2 * L]).then_inc(tmp_ready, 1)

            def before(ph, i, b, lag):
                b -= lag
                if b < 0:
                    b += ph.bb
                    i = i - 1
                return i, b

            def silu(ph, i, b):
                act.wait_ge(nb_evac, ph.g0 + i * ph.bb + b + 1)
                act.activation(zs[:, bass.ds(i * (2 * ph.bb) + 2 * b, 2), :], v[:, b % 2], ACT.Silu)\
                   .then_inc(silu_done, 1)

            def gated_round(ph, i, b, counted):
                n = counted + i * ph.bb + b
                act.wait_ge(gated_ready, n + 1)
                act.copy(gated[:, bass.ds(i * (2 * ph.bb) + 2 * b, 2), 0, :], v[:, b % 2]).then_inc(gated_hi, 1)

            act.dma_start(sw[0][:], a_re[0].rearrange("(q s) n -> q (s n)", s=2)).then_inc(params_loaded, 16)
            act.dma_start(sw[1][:], a_im[0].rearrange("(q s) n -> q (s n)", s=2)).then_inc(params_loaded, 16)
            act.dma_start(ldt[:], log_dt[0].rearrange("(q s) -> q s", s=2)).then_inc(params_loaded, 16)
            for i, par in enumerate((b_re, b_im)):
                act.dma_start(praw[:, i, :], par[0].rearrange("(q s) a b -> q (s a b)", s=2)).then_inc(params_loaded, 16)
            for i, par in enumerate((c_re, c_im)):
                for s in range(2):
                    act.dma_start(praw[:, 2 + i, :].rearrange("q (a s n) -> q s a n", a=PG, s=2)[:, s],
                                 par[0].rearrange("(q s) a n -> q s a n", s=2)[:, s]).then_inc(params_loaded, 16)

            def quad_out(i, k):
                b, qd = k % 2, i * QPB + k
                act.wait_ge(quad_turned, qd + 1)
                if k >= 2 or later(i):
                    act.wait_ge(m1_stored[b], i * (8 * QPB) + 16 * (k // 2))
                act.copy(m1st[:, b].rearrange("p r s m -> p (r s m)"),
                         tb01[:].rearrange("p r m -> p (r m)")).then_inc(m1_evac, 1)
                act.wait_ge(m1_evac, qd + 1)
                act.dma_start(m1_dram[bass.ds(qd, 1)].rearrange("q p m -> p (q m)"),
                              m1st[:, b].rearrange("p r s m -> p (r s m)")).then_inc(m1_stored[b], 16)
                act.wait_ge(mc_ready, qd + 1)
                act.dma_start(m2_dram[bass.ds(qd, 1)].rearrange("q p (r m) -> p (q r) m", r=8),
                              MC[:, b, :, :, 1:T + 1].rearrange("p r s k g a -> p (r s) (k g a)"))\
                   .then_inc(m2_stored[b], 16)
                act.wait_ge(bd_ready, qd + 1)
                act.dma_start(bd_dram[bass.ds(qd, 1)].rearrange("q p m -> p (q m)"),
                              bdst[b][:].rearrange("p l s m -> p (l s m)")).then_inc(bd_stored[b], 16)

            for n in range(DT // 2):
                act.wait_ge(xt_turned, n + 1)
                act.copy(xT[:, 2 * n:2 * n + 2, :], tb01[:, n % 2, :].rearrange("p (t l) -> p t l", t=2))\
                   .then_inc(xt_ready, 1)
            act.wait_ge(vec_turned, 1)
            act.copy(vec[:], tb2[0][:, 0:P]).then_inc(vec_ready, 1)

            act.wait_ge(xt_ready, DT // 2)
            act.dma_start(x_dram[0].rearrange("p (t l) -> p t l", t=DT), xT[:]).then_inc(x_stored, 16)

            def root(which, src, dst):
                act.wait_ge(var_ready, which + 1)
                act.activation(dst, src, ACT.Sqrt).then_inc(root_ready, 1)

            def norm(which):
                root(which, tmp[:, 0, 0, :], tmp[:, 0, 1, :])
                for n in range(DT // 2):
                    act.wait_ge(hn_ready, which * 8 + n + 1)
                    act.copy(h[:, 2 * n:2 * n + 2, 0, :], v[:, n % 2]).then_inc(hn_hi, 1)

            def squares(ph, i, b, counted):
                n = i * ph.bb + b
                act.wait_ge(nb_evac, ph.g0 + n + 1)
                src = last[:, b] if ph is O2 else xT[:, bass.ds(2 * n, 2), :]
                if isinstance(i, int) and n == 0:
                    act.activation(sqsum[:], src, ACT.Square).then_inc(sq_ready, 1)
                else:
                    act.wait_ge(sq_added, counted + n)
                    act.activation(v[:, b % 2], src, ACT.Square).then_inc(sq_ready, 1)

            for n in range(DT // 2):
                if n >= 2:
                    act.wait_ge(sq_summed, n - 1)
                act.activation(v[:, n % 2], xT[:, 2 * n:2 * n + 2, :], ACT.Square).then_inc(sq_ready, 1)
            norm(0)

            def tables_out(s):
                if s == 0:
                    act.wait_ge(powers_turned, 1)
                    powers_out(act.mul, 0).then_inc(powers_ready, 1)
                act.wait_ge(par_turned, 2 * s + 1)
                parameters_out(act.mul, 2 * s).then_inc(par_evac[0], 1)
                if s == 2:
                    act.wait_ge(powers_ready, 3)
                    act.dma_start(tab_dram[2], flat(PWst)).then_inc(tab_stored, 16)
                if s in (U0.bu // 2 - 1, U0.bu - 1):
                    act.wait_ge(par_evac[0], s + 1)
                    act.wait_ge(par_evac[1], s + 1)
                    table, dram = ((BTst, tab_dram[0]), (CTst, tab_dram[1]))[s == U0.bu - 1]
                    act.dma_start(dram, flat(table)).then_inc(tab_stored, 16)

            def u0_body(i, first, turning=False):
                for b in range(U0.bb):
                    for su in range(U0.upb):
                        s = b * U0.upb + su
                        if not (first and s < SPLIT):
                            split(U0, i, s)
                        if su == 1 and not (first and b == 0):
                            evac(U0, *before(U0, i, b, 1))
                        if turning and s > 0:
                            tables_out(s - 1)
                if turning:
                    tables_out(U0.bu - 1)

            def z0_body(i, first):
                for b in range(Z0.bb):
                    for su in range(Z0.upb):
                        split(Z0, i, b * Z0.upb + su)
                        if first and b == 0:
                            if su == 1:
                                evac(U0, U0.bodies - 1, U0.bb - 1)
                                act.wait_ge(x_stored, 16)
                                act.wait_ge(tab_stored, 16 * 3)
                        elif su == 1:
                            evac(Z0, *before(Z0, i, b, 1))
                        elif su == 3:
                            silu(Z0, *before(Z0, i, b, 1))

            def grp_body(i, first):
                for b in range(GR.bb):
                    for su in range(GR.upb):
                        split(GR, i, b * GR.upb + su)
                        if su == 0 and not (first and b < 2):
                            gated_round(GR, *before(GR, i, b, 2), 0)
                        if su == 1:
                            if first and b == 0:
                                evac(Z0, Z0.bodies - 1, Z0.bb - 1)
                                silu(Z0, Z0.bodies - 1, Z0.bb - 1)
                                act.wait_ge(pooled_ready, ET // 2)
                            else:
                                evac(GR, *before(GR, i, b, 1))

            def out0_body(i, first):
                for b in range(O0.bb):
                    for su in range(O0.upb):
                        split(O0, i, b * O0.upb + su)
                        if first and b == 0:
                            if su == 0:
                                gated_round(GR, GR.bodies - 1, GR.bb - 2, 0)
                            if su == 1:
                                evac(GR, GR.bodies - 1, GR.bb - 1)
                            if su == 3:
                                gated_round(GR, GR.bodies - 1, GR.bb - 1, 0)
                        elif su == 1:
                            evac(O0, *before(O0, i, b, 1))
                        elif su == 3:
                            squares(O0, *before(O0, i, b, 1), 0)
                        k = quad_at(first, b * O0.upb + su)
                        if k is not None and not (first and k == 0):
                            quad_out(i if k else i - 1, (k - 1) % QPB)

            def chunk_inputs_out(n):
                for tt in range(2):
                    act.wait_ge(m1_done, 2 * n + tt + 1)
                    act.copy(XS[:, bass.ds(2 * n + tt, 1)].rearrange("p a r s c -> p (a r s c)"),
                             tb01[:, tt, :]).then_inc(xs_ready, 1)

            def u2_body(i, first):
                for b in range(U2.bb):
                    for su in range(U2.upb):
                        split(U2, i, b * U2.upb + su)
                        if su == 1:
                            if first and b == 0:
                                quad_out(O0.bodies - 1, QPB - 1)
                                evac(O0, O0.bodies - 1, O0.bb - 1)
                                act.wait_ge(nb_evac, U2.g0)
                                act.dma_start(x_dram[1].rearrange("p (t l) -> p t l", t=DT), xT[:])\
                                   .then_inc(x_stored, 16)
                                squares(O0, O0.bodies - 1, O0.bb - 1, 0)
                                norm(1)
                            else:
                                evac(U2, *before(U2, i, b, 1))
                        if su == 1 and not (first and b < 2):
                            chunk_inputs_out(i * 2 + b - 2)

            def z2_body(i, first):
                for b in range(Z2.bb):
                    for su in range(Z2.upb):
                        split(Z2, i, b * Z2.upb + su)
                        if first and b == 0:
                            if su == 1:
                                evac(U2, U2.bodies - 1, U2.bb - 1)
                                chunk_inputs_out(U2.blocks - 2)
                        elif su == 1:
                            evac(Z2, *before(Z2, i, b, 1))
                            if first:
                                chunk_inputs_out(U2.blocks - 1)
                        elif su == 3:
                            silu(Z2, *before(Z2, i, b, 1))

            def state_out(j, bb):
                act.copy(state[:, bb].rearrange("p r s c -> p (r s c)"),
                         XS[:, bass.ds(j * 2 + bb, 1)].rearrange("p a r s c -> p (a r s c)")).then_inc(state_ready, 1)

            def gelu_out(j, bb):
                qd = j * 2 + bb
                act.wait_ge(yd_ready, qd + 1)
                act.activation(tmp[:, bb, 1, :], tmp[:, bb, 0, :], ACT.Gelu_apprx_tanh).then_inc(gelu_ready, 1)
                act.wait_ge(gelu_ready, qd + 1)
                act.copy(g[:, bass.ds(qd, 1), 0, :].rearrange("p a l -> p (a l)"), tmp[:, bb, 1, :])\
                   .then_inc(g_hi, 1)

            def glu_body(i, first):
                for b in range(GL.bb):
                    for su in range(GL.upb):
                        split(GL, i, b * GL.upb + su)
                        if first and b == 0:
                            if su == 1:
                                evac(Z2, Z2.bodies - 1, Z2.bb - 1)
                                silu(Z2, Z2.bodies - 1, Z2.bb - 1)
                                act.wait_ge(rec_done, NC)
                                act.wait_ge(unit_done, GL.u0)
                                state_out(0, 0)
                                state_out(0, 1)
                                with act.Fori(1, NQUAD // 2) as j:
                                    for bb in range(2):
                                        gelu_out(j - 1, bb)
                                        act.wait_ge(y_done, 2 * j + bb - 1)
                                        state_out(j, bb)
                                gelu_out(NQUAD // 2 - 1, 0)
                                gelu_out(NQUAD // 2 - 1, 1)
                        elif su == 1:
                            if first:
                                act.wait_ge(gz_ready, NQUAD)
                            evac(GL, *before(GL, i, b, 1))
                        elif su == 3:
                            sigmoid(*before(GL, i, b, 1))
                        elif su == 5:
                            gated_round(GL, *before(GL, i, b, 1), GR.blocks)

            def sigmoid(i, b):
                act.wait_ge(nb_evac, GL.g0 + i * 2 + b + 1)
                for tt in range(2):
                    bias = vec[:, bass.ds(V_BGLU + i * 4 + b * 2 + tt, 1)]
                    ins = act.activation(v[:, b % 2, tt, :], v[:, b % 2, tt, :], ACT.Sigmoid, bias=bias)
                ins.then_inc(sig_ready, 1)

            def out2_body(i, first):
                for b in range(O2.bb):
                    for su in range(O2.upb):
                        split(O2, i, b * O2.upb + su)
                        if first and b == 0:
                            if su == 1:
                                evac(GL, GL.bodies - 1, GL.bb - 1)
                                sigmoid(GL.bodies - 1, GL.bb - 1)
                            if su == 3:
                                gated_round(GL, GL.bodies - 1, GL.bb - 1, GR.blocks)
                        elif su == 1:
                            evac(O2, *before(O2, i, b, 1))
                        elif su == 3:
                            squares(O2, *before(O2, i, b, 1), O0.blocks)
                        elif su == 5:
                            rows_out(*before(O2, i, b, 1))

            def rows_out(i, b):
                n = i * O2.bb + b
                act.wait_ge(out_turned, n + 1)
                act.copy(orows[:, :, bass.ds(256 * n, 256)], tb01[:, b % 2, :].rearrange("p (s c) -> p s c", s=2))\
                   .then_inc(out_evac, 1)

            u0_bodies(act, u0_body)
            bodies(act, Z0, z0_body)
            bodies(act, GR, grp_body)
            bodies(act, O0, out0_body)
            bodies(act, U2, u2_body)
            bodies(act, Z2, z2_body)
            bodies(act, GL, glu_body)
            bodies(act, O2, out2_body)
            evac(O2, O2.bodies - 1, O2.bb - 1)
            squares(O2, O2.bodies - 1, O2.bb - 1, O0.blocks)
            rows_out(O2.bodies - 1, O2.bb - 1)
            root(2, tmp[:, 0, 0, 0:2], tmp[:, 0, 1, 0:2])

        @block.vector
        def _(dve):
            def powers_for_recurrence():
                dve.wait_ge(tab_back, 16 * 3)
                for r_, scale, dst in ((0, 1.0, a4a[:, :, 0, :]), (0, 1.0, a4a[:, :, 1, :]),
                                       (1, 1.0, a4b[:, :, 0, :]), (1, -1.0, a4b[:, :, 1, :])):
                    pw = PW[:, r_, :, 2 * T - 1].rearrange("p (a s) -> p a s", s=4)
                    ins = dve.tensor_scalar(dst, pw, scale, None, ALU.mult)

            def quad_sums(i, k):
                b, qd = k % 2, i * QPB + k
                for M, pr, ready, minus in ((MB, prodb, mb_ready, 0), (MC, prodc, mc_ready, 1)):
                    dve.wait_ge(prods_ready, 2 * qd + minus + 1)
                    if k >= 2 or later(i):
                        if minus == 0:
                            dve.wait_ge(quad_turned, qd - 1)
                            dve.wait_ge(k_ready, qd - 1)
                        else:
                            dve.wait_ge(m2_stored[b], i * (8 * QPB) + 16 * (k // 2))
                    for r in range(2):
                        a_, b_ = (0, 1) if r == 0 else ((2, 3) if minus == 0 else (3, 2))
                        for half in range(2):
                            rows = slice(64 * half, 64 * half + 64)
                            ins = dve.tensor_tensor(M[rows, b, r, :, :, half, :], pr[rows, a_], pr[rows, b_],
                                                    ALU.subtract if r == minus else ALU.add)
                    ins.then_inc(ready, 1)

            def quad_blocks(i, k):
                b, qd = k % 2, i * QPB + k
                dve.wait_ge(k_ready, qd + 1)
                if k >= 2 or later(i):
                    dve.wait_ge(bd_stored[b], i * (8 * QPB) + 16 * (k // 2))
                src = tb2[b][:, 0:T * 32].rearrange("p (l m) -> p l m", l=T).unsqueeze(2).to_broadcast([P, T, 4, 32])
                mask = qmask[:].unsqueeze(1).to_broadcast([P, T, 4, 32])
                dve.tensor_tensor(bdst[b][:], src, mask, ALU.mult).then_inc(bd_ready, 1)

            def split(ph, i, s):
                U = ph.u0 + i * ph.bu + s
                dve.wait_ge(hi_ready, U + 1)
                dve.tensor_tensor(wlo[s % SPLIT][:], raw[s % RAW][:], whi[s % SPLIT][:].bitcast(F32),
                                  ALU.subtract).then_inc(lo_ready, 1)

            norm_steps = [0]

            def nstep(ins):
                ins.then_inc(norm_step, 1)
                norm_steps[0] += 1
                dve.wait_ge(norm_step, norm_steps[0])

            def inverse_root(which, var, root, inv, t, sums, summed):
                dve.wait_ge(sq_summed, summed)
                dve.tensor_scalar(var, sums, 1.0 / D, EPS, ALU.mult, ALU.add).then_inc(var_ready, 1)
                dve.wait_ge(root_ready, which + 1)
                nstep(dve.reciprocal(inv, root))
                nstep(dve.tensor_tensor(t, inv, inv, ALU.mult))
                nstep(dve.tensor_tensor(t, t, var, ALU.mult))
                nstep(dve.tensor_scalar(t, t, -0.5, 1.5, ALU.mult, ALU.add))
                nstep(dve.tensor_tensor(inv, inv, t, ALU.mult))

            def norm(which, v_gain, order, summed):
                inv = tmp[:, 1, 0, :]
                inverse_root(which, tmp[:, 0, 0, :], tmp[:, 0, 1, :], inv, tmp[:, 1, 1, :], tb2[1][:, 0:L], summed)
                for n in range(DT // 2 + 1):
                    if n < DT // 2:
                        if n >= 2:
                            dve.wait_ge(hn_lo, which * 8 + n - 1)
                        for tt in range(2):
                            ft = 2 * n + tt
                            o, i_, iv = v[:, n % 2, tt, :], xT[:, ft, :], inv
                            if order == "chunks":
                                o = o.rearrange("p (j c) -> p c j", j=T)
                                i_ = i_.rearrange("p (c j) -> p c j", j=T)
                                iv = iv.rearrange("p (c j) -> p c j", j=T)
                            ins = dve.scalar_tensor_tensor(o, i_, vec[:, v_gain + ft:v_gain + ft + 1], iv,
                                                           ALU.mult, ALU.mult)
                        ins.then_inc(hn_ready, 1)
                    if n >= 1:
                        m_ = n - 1
                        dve.wait_ge(hn_hi, which * 8 + n)
                        dve.tensor_tensor(h[:, 2 * m_:2 * m_ + 2, 1, :], v[:, m_ % 2],
                                          h[:, 2 * m_:2 * m_ + 2, 0, :].bitcast(F32), ALU.subtract)\
                           .then_inc(hn_lo, 1)

            def add_squares(ph, i, b, counted):
                n = i * ph.bb + b
                dve.wait_ge(sq_ready, 8 + counted + n + 1)
                if isinstance(i, int) and n == 0:
                    dve.sem_inc(sq_added, 1)
                else:
                    dve.wait_ge(sq_added, counted + n)
                    dve.tensor_tensor(sqsum[:], sqsum[:], v[:, b % 2], ALU.add).then_inc(sq_added, 1)

            for s in range(SPLIT):
                dve.wait_ge(raw_loaded[s], 16)
                dve.tensor_copy(whi[s][:], raw[s][:]).then_inc(hi_ready, 1)
                split(U0, 0, s)
            dve.wait_ge(vec_ready, 1)
            norm(0, V_NORM, "tokens", DT // 2)

            def before(ph, i, b, lag):
                b -= lag
                if b < 0:
                    b += ph.bb
                    i = i - 1
                return i, b

            def add_up(ph, i, b, dst):
                G = ph.g0 + i * ph.bb + b
                dve.wait_ge(tmp_ready, G + 1)
                dve.tensor_tensor(dst, acc[b % 2][:, :, 0:L], tmp[:, b % 2], ALU.add).then_inc(nb_evac, 1)

            def tiles(i, ph, b):
                return bass.ds(i * (2 * ph.bb) + 2 * b, 2)

            def gated_low(ph, i, b, counted):
                n = counted + i * ph.bb + b
                dve.wait_ge(gated_hi, n + 1)
                dve.tensor_tensor(gated[:, tiles(i, ph, b), 1, :], v[:, b % 2],
                                  gated[:, tiles(i, ph, b), 0, :].bitcast(F32), ALU.subtract).then_inc(gated_lo, 1)

            def u0_out(i, b):
                add_up(U0, i, b, u0[:, tiles(i, U0, b), PAD:PAD + L])

            def scaled(dst, src, scale):
                return dve.tensor_scalar(dst, src, scale, None, ALU.mult)

            def tables_out(s):
                if s == 0:
                    dve.wait_ge(powers_turned, 1)
                    powers_out(scaled, 1).then_inc(powers_ready, 1)
                    dve.memset(PWst[:, 0, :, T - 1], 1.0)
                    dve.memset(PWst[:, 1, :, T - 1], 0.0).then_inc(powers_ready, 1)
                dve.wait_ge(par_turned, 2 * s + 2)
                parameters_out(scaled, 2 * s + 1).then_inc(par_evac[1], 1)

            def u0_body(i, first, turning=False):
                for b in range(U0.bb):
                    for su in range(U0.upb):
                        s = b * U0.upb + su
                        if not (first and s < SPLIT):
                            split(U0, i, s)
                        if turning and s > 0:
                            tables_out(s - 1)
                        if su == 1 and not (first and b == 0):
                            if first:
                                dve.wait_ge(xt_ready, 8)
                            u0_out(*before(U0, i, b, 1))
                if turning:
                    tables_out(U0.bu - 1)
                if first:
                    dve.wait_ge(den_ready, 1)
                    dve.reciprocal(sden[:], sden[:]).then_inc(den_inverted, 1)

            def z_out(ph, i, b, counted):
                n = counted + i * ph.bb + b
                if later(i) or i * ph.bb + b > 0 or counted > 0:
                    dve.wait_ge(silu_done, n)
                add_up(ph, i, b, v[:, b % 2])

            def z0_body(i, first):
                for b in range(Z0.bb):
                    for su in range(Z0.upb):
                        split(Z0, i, b * Z0.upb + su)
                        if su == 1:
                            if first and b == 0:
                                u0_out(U0.bodies - 1, U0.bb - 1)
                            else:
                                z_out(Z0, *before(Z0, i, b, 1), 0)

            def grp_out(i, b):
                n = i * GR.bb + b
                if not (isinstance(i, int) and i == 0 and b < 2):
                    dve.wait_ge(gated_lo, n - 1)
                if isinstance(i, int) and i == 0 and b == 0:
                    dve.wait_ge(silu_done, Z0.blocks)
                add_up(GR, i, b, v[:, b % 2])
                dve.wait_ge(nb_evac, GR.g0 + n + 1)
                for tt in range(2):
                    ft = i * (2 * GR.bb) + 2 * b + tt
                    ins = dve.scalar_tensor_tensor(
                        v[:, b % 2, tt, :], v[:, b % 2, tt, :], vec[:, bass.ds(V_SCALE + ft, 1)],
                        zs[:, bass.ds(ft, 1), :].rearrange("p a l -> p (a l)"), ALU.mult, ALU.mult)
                ins.then_inc(gated_ready, 1)

            def grp_body(i, first):
                for b in range(GR.bb):
                    for su in range(GR.upb):
                        split(GR, i, b * GR.upb + su)
                        if su == 0 and not (first and b < 2):
                            gated_low(GR, *before(GR, i, b, 2), 0)
                        if su == 1:
                            if first and b == 0:
                                z_out(Z0, Z0.bodies - 1, Z0.bb - 1, 0)
                            else:
                                grp_out(*before(GR, i, b, 1))

            def resid(ph, i, b, order, counted):
                G = ph.g0 + i * ph.bb + b
                xv = xT[:, tiles(i, ph, b), :]
                hl, hh = tmp[:, b % 2], acc[b % 2][:, :, 0:L]
                if order == "chunks":
                    xv = xv.rearrange("p t (c j) -> p t c j", j=T)
                    hl = hl.rearrange("p t (j c) -> p t c j", j=T)
                    hh = hh.rearrange("p t (j c) -> p t c j", j=T)
                dve.wait_ge(tmp_ready, G + 1)
                dve.tensor_tensor(xv, xv, hl, ALU.add).then_inc(resid_half, 1)
                dve.wait_ge(resid_half, counted + i * ph.bb + b + 1)
                if ph is O2:
                    n = i * ph.bb + b
                    if later(n):
                        dve.wait_ge(out_turned, n)
                        dve.wait_ge(sq_ready, 8 + O0.blocks + n)
                    dst = last[:, b].rearrange("p t (c j) -> p t c j", j=T)
                else:
                    dst = xv
                dve.tensor_tensor(dst, hh, xv, ALU.add).then_inc(nb_evac, 1)

            def out0_body(i, first):
                for b in range(O0.bb):
                    for su in range(O0.upb):
                        split(O0, i, b * O0.upb + su)
                        if first and b == 0:
                            if su == 0:
                                gated_low(GR, GR.bodies - 1, GR.bb - 2, 0)
                            if su == 1:
                                grp_out(GR.bodies - 1, GR.bb - 1)
                            if su == 3:
                                gated_low(GR, GR.bodies - 1, GR.bb - 1, 0)
                        elif su == 1:
                            if first:
                                dve.wait_ge(x_back, 16)
                            resid(O0, *before(O0, i, b, 1), "tokens", 0)
                        elif su == 5:
                            add_squares(O0, *before(O0, i, b, 1), 0)
                        k = quad_at(first, b * O0.upb + su)
                        if k is not None:
                            if first and k == 0:
                                powers_for_recurrence()
                                dve.wait_ge(tab_zeroed, 2)
                                dve.wait_ge(consts, N_CONSTS)
                            if not (first and k == 0):
                                quad_blocks(i if k else i - 1, (k - 1) % QPB)
                            quad_sums(i, k)

            def u2_out(i, b):
                n = i * 2 + b
                add_up(U2, i, b, u2[:, tiles(i, U2, b), :])
                if isinstance(i, int) and i == 0 and b == 0:
                    dve.wait_ge(x_stored, 32)
                if later(i) or n > 0:
                    dve.wait_ge(m1_done, 2 * n)
                dve.wait_ge(nb_evac, U2.g0 + n + 1)
                for j in range(T):
                    for q in range(4):
                        ins = dve.tensor_scalar(uj[32 * j:32 * j + 32, b, :, q, :],
                                                u2[32 * q:32 * q + 32, tiles(i, U2, b), NC * j:NC * j + NC],
                                                1.0, None, ALU.mult)
                ins.then_inc(uj_ready, 1)

            def u2_body(i, first):
                for b in range(U2.bb):
                    for su in range(U2.upb):
                        split(U2, i, b * U2.upb + su)
                        if su == 1:
                            if first and b == 0:
                                quad_blocks(O0.bodies - 1, QPB - 1)
                                resid(O0, O0.bodies - 1, O0.bb - 1, "tokens", 0)
                                add_squares(O0, O0.bodies - 1, O0.bb - 1, 0)
                                norm(1, V_NORM + DT, "chunks", DT // 2 + 1)
                            else:
                                u2_out(*before(U2, i, b, 1))

            def rec_products(k, i):
                c1 = i * 9 + k
                prev = XS[:, :, :, :, bass.ds(c1, 1)].rearrange("p a r s c -> p a r (s c)")
                dve.wait_ge(rec_done, c1 + 1)
                dve.tensor_tensor(rec1[:], a4a[:], prev, ALU.mult).then_inc(rec_a, 1)

            def rec_sums(k, i):
                c1 = i * 9 + k
                cur = XS[:, :, :, :, bass.ds(c1 + 1, 1)].rearrange("p a r s c -> p a r (s c)")
                dve.wait_ge(rec_a, c1 + 1)
                dve.tensor_tensor(cur, cur, rec1[:], ALU.add).then_inc(rec_half, 1)
                dve.wait_ge(rec_half, c1 + 1)
                dve.wait_ge(rec_b, c1 + 1)
                dve.tensor_tensor(cur, cur, rec2[:], ALU.add).then_inc(rec_done, 1)

            def z2_first():
                for b in range(Z2.bb):
                    for su in range(Z2.upb):
                        split(Z2, 0, b * Z2.upb + su)
                        if su == 1:
                            if b == 0:
                                u2_out(U2.bodies - 1, U2.bb - 1)
                            else:
                                z_out(Z2, 0, b - 1, Z0.blocks)

            def z2_body(i):
                for b in range(Z2.bb):
                    for su in range(Z2.upb):
                        s = b * Z2.upb + su
                        rec_products(s, i - 1)
                        split(Z2, i, s)
                        rec_sums(s, i - 1)
                        if su == 1:
                            z_out(Z2, *before(Z2, i, b, 1), Z0.blocks)
                rec_products(8, i - 1)
                rec_sums(8, i - 1)

            def glu_out(i, b):
                if not (isinstance(i, int) and i == 0 and b < 2):
                    dve.wait_ge(gated_lo, GR.blocks + i * 2 + b - 1)
                add_up(GL, i, b, v[:, b % 2])

            def glu_gate(i, b):
                dve.wait_ge(sig_ready, i * 2 + b + 1)
                dve.tensor_tensor(v[:, b % 2], v[:, b % 2], zs[:, tiles(i, GL, b), :], ALU.mult)\
                   .then_inc(gated_ready, 1)

            def y_skip(j, bb):
                qd = j * 2 + bb
                dve.wait_ge(y_done, qd + 1)
                if later(j):
                    dve.wait_ge(gz_ready, qd - 1)
                dve.scalar_tensor_tensor(tmp[:, bb, 0, :], u2[:, bass.ds(qd, 1), :].rearrange("p a l -> p (a l)"),
                                         vec[:, bass.ds(V_D + qd, 1)], tb2[bb][:, 0:L], ALU.mult, ALU.add)\
                   .then_inc(yd_ready, 1)

            def y_low(j, bb):
                qd = j * 2 + bb
                dve.wait_ge(g_hi, qd + 1)
                gv = g[:, bass.ds(qd, 1)].rearrange("p a r l -> p (a r) l")
                dve.tensor_tensor(gv[:, 1, :], tmp[:, bb, 1, :], gv[:, 0, :].bitcast(F32), ALU.subtract)\
                   .then_inc(g_lo, 1)

            def glu_body(i, first):
                for b in range(GL.bb):
                    for su in range(GL.upb):
                        split(GL, i, b * GL.upb + su)
                        if first and b == 0:
                            if su == 1:
                                z_out(Z2, Z2.bodies - 1, Z2.bb - 1, Z0.blocks)
                                for bb in range(2):
                                    y_skip(0, bb)
                                    y_low(0, bb)
                                with dve.Fori(1, NQUAD // 2) as j:
                                    for bb in range(2):
                                        y_skip(j, bb)
                                        y_low(j, bb)
                                dve.wait_ge(gz_ready, NQUAD)
                        elif su == 1:
                            glu_out(*before(GL, i, b, 1))
                        elif su == 3:
                            glu_gate(*before(GL, i, b, 1))
                        elif su == 5:
                            gated_low(GL, *before(GL, i, b, 1), GR.blocks)

            def out2_body(i, first):
                for b in range(O2.bb):
                    for su in range(O2.upb):
                        split(O2, i, b * O2.upb + su)
                        if first and b == 0:
                            if su == 1:
                                glu_out(GL.bodies - 1, GL.bb - 1)
                                glu_gate(GL.bodies - 1, GL.bb - 1)
                            if su == 3:
                                gated_low(GL, GL.bodies - 1, GL.bb - 1, GR.blocks)
                        elif su == 1:
                            if first:
                                dve.wait_ge(x_back, 32)
                            resid(O2, *before(O2, i, b, 1), "chunks", O0.blocks)
                        elif su == 5:
                            add_squares(O2, *before(O2, i, b, 1), O0.blocks)

            u0_bodies(dve, u0_body)
            bodies(dve, Z0, z0_body)
            bodies(dve, GR, grp_body)
            bodies(dve, O0, out0_body)
            bodies(dve, U2, u2_body)
            z2_first()
            dve.wait_ge(xs_ready, NQUAD)
            dve.sem_inc(rec_done, 1)
            with dve.Fori(1, Z2.bodies) as i:
                z2_body(i)
            bodies(dve, GL, glu_body)
            bodies(dve, O2, out2_body)
            resid(O2, O2.bodies - 1, O2.bb - 1, "chunks", O0.blocks)
            add_squares(O2, O2.bodies - 1, O2.bb - 1, O0.blocks)
            inverse_root(2, tmp[:, 0, 0, 0:2], tmp[:, 0, 1, 0:2], tmp[:, 1, 0, 0:2], tmp[:, 1, 1, 0:2],
                         tb2[1][:, 0:2], DT // 2 + 2)
            dve.wait_ge(gain_loaded, 16)
            dve.wait_ge(out_evac, O2.blocks)
            for n in range(4):
                cols = slice(n // 2 * (D // 2), (n // 2 + 1) * (D // 2))
                dve.scalar_tensor_tensor(orows[:, n % 2, cols], orows[:, n % 2, cols], tmp[:, 1, 0, n % 2:n % 2 + 1],
                                         gain[:, cols], ALU.mult, ALU.mult).then_inc(out_ready, 1)

        @block.tensor
        def _(pe):
            mm = pe.matmul

            def unit(ph, i, s, operand, ready=None, count=0):
                U = ph.u0 + i * ph.bu + s
                b, su = divmod(s, ph.upb)
                ps = acc[b % 2]
                pe.wait_ge(lo_ready, U + 1)
                if su == 0 and (ph.g0 + b >= 2 or later(i)):
                    pe.wait_ge(nb_evac, ph.g0 + i * ph.bb + b - 1)
                for kk in range(UK):
                    kt = su * UK + kk
                    if ready is not None and kt % 2 == 0:
                        pe.wait_ge(ready, count + kt // 2 + 1)
                    rhs = operand(kt)
                    for tt in range(2):
                        cols = slice(tt * P, tt * P + P)
                        mm(ps[:, tt, :], whi[s % SPLIT][:, kk, cols], rhs[:, 0:2, :],
                           start=(kt == 0), stop=False, skip_group_check=True)
                        ins = mm(ps[:, tt, 0:L], wlo[s % SPLIT][:, kk, cols], rhs[:, 0, :],
                                 start=False, stop=(su == ph.upb - 1 and kk == UK - 1), skip_group_check=True)
                ins.then_inc(unit_done, 1)

            def turn_powers():
                pe.wait_ge(chain_done, 1)
                for r in range(2):
                    for k in range(T):
                        ins = pe.transpose(tb2[r][:, k * P:k * P + P], sw[16 + 2 * k + r][:], ident[:])
                ins.then_inc(powers_turned, 1)

            def turn_parameters(n):
                if n >= 2:
                    pe.wait_ge(par_evac[n % 2], n // 2)
                for a in range(4):
                    r, feature = n // 4, n % 4 * 4 + a
                    if r < 2:
                        src = bbar[:, r, :].rearrange("q (s a) -> q s a", a=PG)[:, :, feature]
                    else:
                        src = praw[:, r, feature * P:feature * P + P]
                    ins = pe.transpose(tb01[:, n % 2, a * P:a * P + P], src, ident[:])
                ins.then_inc(par_turned, 1)

            def quad(i, k):
                b, qd = k % 2, i * QPB + k
                pe.wait_ge(mb_ready, qd + 1)
                if k or later(i):
                    pe.wait_ge(m1_evac, qd)
                for r in range(2):
                    for q in range(4):
                        ins = pe.transpose(tb01[:, r, q * P:q * P + P],
                                           MB[:, b, r, q].rearrange("p j g a -> p (j g a)"), ident[:])
                ins.then_inc(quad_turned, 1)
                pe.wait_ge(mc_ready, qd + 1)
                if k >= 2 or later(i):
                    pe.wait_ge(bd_ready, qd - 1)
                for q in range(4):
                    for r in range(2):
                        ins = mm(tb2[b][32 * q:32 * q + 32, 0:T * 32],
                                 MB[:, b, r, q, T - 1].rearrange("p g a -> p (g a)"),
                                 MC[:, b, r, q, 0:T].rearrange("p k g a -> p (k g a)"),
                                 start=(r == 0), stop=(r == 1))
                ins.then_inc(k_ready, 1)

            pe.wait_ge(consts, 4)
            for n in range(DT // 2):
                if n % (DT // 4) == 0:
                    pe.wait_ge(x_loaded[n // (DT // 4)], 16)
                if n >= 2:
                    pe.wait_ge(xt_ready, n - 1)
                for tt in range(2):
                    for s in range(2):
                        ft = 2 * n + tt
                        ins = pe.transpose(tb01[:, n % 2, tt * L + s * P:tt * L + s * P + P],
                                           xrows[:, s, ft * P:ft * P + P], ident[:])
                ins.then_inc(xt_turned, 1)

            pe.wait_ge(vec_loaded, 16 * 4)
            pe.transpose(tb2[0][:, 0:P], vrow[:], ident[:]).then_inc(vec_turned, 1)

            for n in range(DT // 2):
                pe.wait_ge(sq_ready, n + 1)
                for tt in range(2):
                    ins = mm(tb2[1][:, 0:L], ones[:], v[:, n % 2, tt, :],
                             start=(n == 0 and tt == 0), stop=(n == 7 and tt == 1))
                ins.then_inc(sq_summed, 1)

            def h_operand(kt):
                return h[:, kt]

            def gated_operand(kt):
                return gated[:, kt]

            def u0_body(i, first, turning=False):
                for s in range(U0.bu):
                    unit(U0, i, s, h_operand, hn_lo if first and s < U0.upb else None, 0)
                    if turning:
                        if s == 0:
                            turn_powers()
                        turn_parameters(2 * s)
                        turn_parameters(2 * s + 1)

            def z0_body(i, first):
                for s in range(Z0.bu):
                    unit(Z0, i, s, h_operand)

            def grp_body(i, first):
                for s in range(GR.bu):
                    def operand(kt):
                        return pooled[:, bass.ds(i * GT + kt, 1)].rearrange("p a r l -> p (a r) l")
                    unit(GR, i, s, operand, pooled_ready if s < GR.upb else None, i * (GT // 2))

            def out0_body(i, first):
                for s in range(O0.bu):
                    unit(O0, i, s, gated_operand, gated_lo if first and s < O0.upb else None, 0)
                    k = quad_at(first, s)
                    if k is not None:
                        quad(i, k)

            def m1_products(i, b):
                n = i * 2 + b
                pe.wait_ge(m1_loaded[b], i * 16 + 16)
                pe.wait_ge(uj_ready, n + 1)
                for tt in range(2):
                    if not (isinstance(i, int) and i == 0 and b == 0):
                        pe.wait_ge(xs_ready, 2 * n + tt - 1)
                    for r in range(2):
                        for q in range(4):
                            col = (r * 4 + q) * NC
                            ins = mm(tb01[:, tt, col:col + NC], m1ring[:, b, tt, r, q, :], uj[:, b, tt, q, :],
                                     start=True, stop=True)
                    ins.then_inc(m1_done, 1)

            def u2_body(i, first):
                for b in range(U2.bb):
                    for su in range(U2.upb):
                        unit(U2, i, b * U2.upb + su, h_operand,
                             hn_lo if first and b == 0 else None, 8)
                        if su == 3 and not (first and b == 0):
                            m1_products(i - 1, 1) if b == 0 else m1_products(i, 0)

            def z2_body(i, first):
                for b in range(Z2.bb):
                    for su in range(Z2.upb):
                        unit(Z2, i, b * Z2.upb + su, h_operand)
                        if first and b == 0 and su == 3:
                            m1_products(U2.bodies - 1, 1)

            def y_products(j, bb):
                qd = j * 2 + bb
                pe.wait_ge(m2_loaded[bb], j * 32 + 32)
                if later(j):
                    pe.wait_ge(yd_ready, qd - 1)
                ps = tb2[bb]
                ut = u2[:, bass.ds(qd, 1), :].rearrange("p a l -> p (a l)")
                for l in range(T):
                    mm(ps[:, NC * l:L], bdring[:, bb, l, :], ut[:, 0:L - NC * l],
                       start=(l == 0), stop=False, skip_group_check=True)
                pe.wait_ge(state_ready, qd + 1)
                for q in range(4):
                    for r in range(2):
                        for jt in range(T):
                            ins = mm(ps[32 * q:32 * q + 32, NC * jt + 1:NC * jt + NC],
                                     m2ring[:, bb, r, q, jt, :], state[:, bb, r, q, 0:NC - 1],
                                     start=False, stop=(q == 3 and r == 1), skip_group_check=True)
                ins.then_inc(y_done, 1)

            def g_operand(kt):
                return g[:, kt]

            def glu_body(i, first):
                if first:
                    pe.wait_ge(rec_done, NC)
                    y_products(0, 0)
                    y_products(0, 1)
                    with pe.Fori(1, NQUAD // 2) as j:
                        y_products(j, 0)
                        y_products(j, 1)
                    pe.wait_ge(g_lo, NQUAD)
                for s in range(GL.bu):
                    unit(GL, i, s, g_operand)

            def out2_body(i, first):
                for s in range(O2.bu):
                    unit(O2, i, s, gated_operand, gated_lo if first and s < O2.upb else None, GR.blocks)
                    if s % O2.upb == 3 and not (first and s < O2.upb):
                        turn_rows(i, 0) if s > O2.upb else turn_rows(i - 1, 1)

            def turn_rows(i, b):
                n = i * O2.bb + b
                pe.wait_ge(nb_evac, O2.g0 + n + 1)
                if later(i):
                    pe.wait_ge(out_evac, n - 1)
                for half in range(2):
                    for tt in range(2):
                        ins = pe.transpose(tb01[:, b, half * L + tt * P:half * L + tt * P + P],
                                           last[:, b, tt, half * P:half * P + P], ident[:])
                ins.then_inc(out_turned, 1)

            u0_bodies(pe, u0_body)
            bodies(pe, Z0, z0_body)
            bodies(pe, GR, grp_body)
            bodies(pe, O0, out0_body)
            pe.wait_ge(sq_added, O0.blocks)
            pe.wait_ge(bd_ready, NQUAD)
            for tt in range(2):
                ins = mm(tb2[1][:, 0:L], ones[:], sqsum[:, tt, :], start=(tt == 0), stop=(tt == 1))
            ins.then_inc(sq_summed, 1)
            bodies(pe, U2, u2_body)
            bodies(pe, Z2, z2_body)
            bodies(pe, GL, glu_body)
            bodies(pe, O2, out2_body)
            turn_rows(O2.bodies - 1, O2.bb - 1)
            pe.wait_ge(sq_added, O0.blocks + O2.blocks)
            pe.wait_ge(yd_ready, NQUAD)
            for half in range(2):
                for tt in range(2):
                    ins = mm(tb2[1][:, half:half + 1], sqsum[:, tt, half * P:half * P + P], ones[:, 0:1],
                             start=(tt == 0), stop=(tt == 1))
            ins.then_inc(sq_summed, 1)


N_CONSTS = 3 + 1 + 4 + sum(WINDOWS)

_INS = ["x", "norm_g", "final_norm_g", "pool_w_in", "pool_w_grp", "pool_scale", "pool_w_out",
        "ssm_w_in", "ssm_a_re", "ssm_a_im", "ssm_log_dt", "ssm_b_re", "ssm_b_im", "ssm_c_re",
        "ssm_c_im", "ssm_d", "ssm_w_glu", "ssm_b_glu", "ssm_w_out"]
_OUT = (1, L, D)


def kernel(**inputs):
    import concourse.bacc as bacc
    from concourse.bass_utils import run_bass_kernel_spmd

    nc = bacc.Bacc("TRN2", target_bir_lowering=False, num_devices=1)
    arrays, args = {}, []
    for name in _INS:
        a = np.ascontiguousarray(inputs[name])
        arrays[f"in_{name}"] = a
        args.append(nc.dram_tensor(f"in_{name}", a.shape, mybir.dt.from_np(a.dtype), kind="ExternalInput").ap())
    args.append(nc.dram_tensor("out_0", _OUT, F32, kind="ExternalOutput").ap())
    build_program(nc, *args)
    r = run_bass_kernel_spmd(nc, [arrays], core_ids=[0])
    return r.results[0]["out_0"]
```

```python
import math
from contextlib import ExitStack

import numpy as np
import concourse.bass as bass
from concourse import mybir

F32 = mybir.dt.float32
F32R = mybir.dt.float32r
I32 = mybir.dt.int32
ALU = mybir.AluOpType
ACT = mybir.ActivationFunctionType

P = 128
L = 256
D = 2048
E = 4096
DT = D // P
ET = E // P
WINDOWS = (2, 4, 8, 16)
GT = ET // len(WINDOWS)
PAD = 16
NS = 64
PG = 16
NPAIR = 128
NQUAD = NPAIR // 4
T = 4
NC = L // T
EPS = 1e-6

UK = 4
NW = 256
RAW = 4
SPLIT = 2


class Phase:

    def __init__(self, name, ktiles, blocks, body_blocks, prev):
        self.name = name
        self.upb = ktiles // UK
        self.blocks = blocks
        self.bb = body_blocks
        self.bodies = blocks // body_blocks
        self.bu = self.upb * body_blocks
        self.u0 = prev.u0 + prev.units if prev else 0
        self.g0 = prev.g0 + prev.blocks if prev else 0
        self.units = self.upb * blocks
        self.prev = prev


U0 = Phase("u0", DT, 16, 2, None)
Z0 = Phase("z0", DT, 16, 2, U0)
GR = Phase("grp", GT, 16, 4, Z0)
O0 = Phase("out0", ET, 8, 2, GR)
U2 = Phase("u2", DT, 16, 2, O0)
Z2 = Phase("z2", DT, 16, 2, U2)
GL = Phase("glu", ET, 16, 2, Z2)
O2 = Phase("out2", ET, 8, 2, GL)

V_NORM, V_SCALE, V_BGLU, V_D = 0, 32, 64, 96



def build_program(nc, x, norm_g, final_norm_g, pool_w_in, pool_w_grp, pool_scale, pool_w_out,
                  ssm_w_in, a_re, a_im, log_dt, b_re, b_im, c_re, c_im, ssm_d, w_glu, b_glu,
                  ssm_w_out, out):
    KB = 1024
    base = -(-nc.sbuf_base // 512) * 512
    A, B, C = base, base + 66 * KB, base + 130 * KB
    RING, MISC = base + 162 * KB, base + 194 * KB

    def at(name, shape, dt, offset):
        return nc.alloc_sbuf_tensor_at(name, shape, dt, offset=offset)

    h = at("h", [P, DT, 2, L], F32R, A)
    u0 = at("u0", [P, ET, PAD + L], F32, A + 32 * KB)
    u2 = at("u2", [P, ET, L], F32, A + 32 * KB)
    gated = at("gated", [P, ET, 2, L], F32R, A)
    xrows = at("xrows", [P, 2, D], F32, A + 32 * KB)
    sqsum = at("sqsum", [P, 2, L], F32, A + 64 * KB)
    m2ring = at("m2ring", [P, 4, 2, 4, T, 32], F32, A)
    bdring = at("bdring", [P, 2, T, P], F32, A + 16 * KB)
    kring = at("kring", [P, 4, T, 32], F32, A + 20 * KB)
    state = at("state", [P, 2, 2, 4, NC], F32, A + 24 * KB)
    rec1 = at("rec1", [P, NQUAD, 2, 4], F32, A + 64 * KB)
    rec2 = at("rec2", [P, NQUAD, 2, 4], F32, A + 65 * KB)
    pooled = at("pooled", [P, ET, 2, L], F32R, B)
    pwin_b = at("pwin_b", [P, ET, 2 * L], F32, B)
    XS = at("XS", [P, NQUAD, 2, 4, NC], F32, B)
    g = at("g", [P, ET, 2, L], F32R, B)
    orows = at("orows", [P, 2, D], F32, B)
    gain = at("gain", [P, D], F32, B + 16 * KB)
    last = at("last", [P, 2, 2, L], F32, B + 24 * KB)
    BT = at("BT", [P, 2, NPAIR, PG], F32, B)
    CT = at("CT", [P, 2, NPAIR, PG], F32, B + 16 * KB)
    PW = at("PW", [P, 2, NPAIR, 2 * T], F32, B + 32 * KB)
    MB = at("MB", [P, 2, 2, 4, T, 2, PG], F32, B + 40 * KB)
    MC = at("MC", [P, 2, 2, 4, T + 1, 2, PG], F32, B + 48 * KB)
    prodb = at("prodb", [P, 4, 4, T, PG], F32, B + 58 * KB)
    kst = at("kst", [P, 2, T * 32], F32, B + 62 * KB)
    zs = at("zs", [P, ET, L], F32, C)
    xT = at("xT", [P, DT, L], F32, C)
    m1st = at("m1st", [P, 2, 2, 4, P], F32, C + 16 * KB)
    prodc = at("prodc", [P, 4, 4, T + 1, PG], F32, C + 24 * KB)
    m1ring = at("m1ring", [P, 2, 2, 2, 4, P], F32, C + 16 * KB)
    uj = at("uj", [P, 2, 2, 4, NC], F32, C + 12 * KB)
    raw = [at(f"raw{i}", [P, UK, NW], F32, RING + i * 4 * KB) for i in range(RAW)]
    whi = [at(f"whi{i}", [P, UK, NW], F32R, RING + (16 + i * 8) * KB) for i in range(SPLIT)]
    wlo = [at(f"wlo{i}", [P, UK, NW], F32R, RING + (20 + i * 8) * KB) for i in range(SPLIT)]
    tmp = at("tmp", [P, 2, 2, L], F32, MISC)
    vrow = at("vrow", [P, P], F32, MISC)
    v = at("v", [P, 2, 2, L], F32, MISC + 4 * KB)
    ident = at("ident", [P, P], F32, MISC + 8 * KB)
    ones = at("ones", [P, P], F32, MISC + 8 * KB + 512)
    qmask = at("qmask", [P, 4, 32], F32, MISC + 9 * KB)
    vec = at("vec", [P, P], F32, MISC + 9 * KB + 512)
    a4a = at("a4a", [P, NQUAD, 2, 4], F32, MISC + 10 * KB + 512)
    a4b = at("a4b", [P, NQUAD, 2, 4], F32, MISC + 11 * KB + 512)
    pwin_a = at("pwin_a", [P, PAD + L], F32, MISC + 10 * KB + 512)
    corr = at("corr", [P, len(WINDOWS), PAD], F32, MISC + 12 * KB + 512)
    spare = at("spare", [P, 1], F32, MISC + 12 * KB + 960)
    praw = at("praw", [P, 4, NPAIR * PG], F32, B)
    bbar = at("bbar", [P, 2, NPAIR * PG], F32, B + 32 * KB)
    fbp = at("fbp", [P, NPAIR * PG], F32, C)
    sw = [at(f"sw{i}", [P, P], F32, C + 16 * KB + i * 512) for i in range(24)]
    swi = [at(f"swi{i}", [P, P], I32, C + 28 * KB + i * 512) for i in range(2)]
    sden = at("sden", [P, P], F32, C + 29 * KB)
    ldt = at("ldt", [P, 2], F32, C + 30 * KB)
    BTst = at("BTst", [P, 2, NPAIR, PG], F32, B + 48 * KB)
    CTst = at("CTst", [P, 2, NPAIR, PG], F32, B)
    PWst = at("PWst", [P, 2, NPAIR, 2 * T], F32, C)

    ctx = ExitStack()
    with ctx:
        def sem(name):
            return ctx.enter_context(nc.semaphore(name))

        def psum(name, shape):
            return ctx.enter_context(nc.psum_tensor(name, shape, F32))

        acc = [psum(f"acc{i}", [P, 2, 512]) for i in range(2)]
        tb01 = psum("tb01", [P, 2, 512])
        tb2 = [psum(f"tb{i}", [P, 512]) for i in (2, 3)]

        m1_dram = nc.dram_tensor("m1_scratch", (NQUAD, P, 8 * P), F32).ap()
        m2_dram = nc.dram_tensor("m2_scratch", (NQUAD, P, 8 * T * 32), F32).ap()
        k_dram = nc.dram_tensor("k_scratch", (NQUAD, P, T * 32), F32).ap()
        tab_dram = [nc.dram_tensor(f"tab_scratch{i}", (P, n), F32).ap()
                    for i, n in enumerate((2 * NPAIR * PG, 2 * NPAIR * PG, 2 * NPAIR * 2 * T))]
        x_dram = [nc.dram_tensor(f"x_scratch{i}", (P, DT * L), F32).ap() for i in range(2)]

        raw_loaded = [sem(f"raw_loaded{i}") for i in range(RAW)]
        hi_ready, lo_ready = sem("hi_ready"), sem("lo_ready")
        unit_done = sem("unit_done")
        tmp_ready, nb_evac = sem("tmp_ready"), sem("nb_evac")
        vec_loaded, params_loaded = sem("vec_loaded"), sem("params_loaded")
        x_loaded = [sem(f"x_loaded{i}") for i in range(2)]
        consts = sem("consts")
        vec_turned, vec_ready = sem("vec_turned"), sem("vec_ready")
        chain = sem("chain")
        chain_done, par_turned = sem("chain_done"), sem("par_turned")
        par_evac = [sem(f"par_evac{i}") for i in range(2)]
        den_ready, den_inverted = sem("den_ready"), sem("den_inverted")
        powers_turned, powers_ready = sem("powers_turned"), sem("powers_ready")
        tab_stored, tab_back, tab_zeroed = sem("tab_stored"), sem("tab_back"), sem("tab_zeroed")
        prods_ready, mb_ready, mc_ready = sem("prods_ready"), sem("mb_ready"), sem("mc_ready")
        quad_turned, k_ready = sem("quad_turned"), sem("k_ready")
        m1_evac, k_evac = sem("m1_evac"), sem("k_evac")
        m1_stored = [sem(f"m1_stored{i}") for i in range(2)]
        m2_stored = [sem(f"m2_stored{i}") for i in range(2)]
        k_stored = [sem(f"k_stored{i}") for i in range(2)]
        xt_turned, xt_ready = sem("xt_turned"), sem("xt_ready")
        sq_ready, sq_summed = sem("sq_ready"), sem("sq_summed")
        norm_step, var_ready, root_ready = sem("norm_step"), sem("var_ready"), sem("root_ready")
        hn_ready, hn_hi, hn_lo = sem("hn_ready"), sem("hn_hi"), sem("hn_lo")
        x_stored, x_back = sem("x_stored"), sem("x_back")
        pool_step, pooled_ready = sem("pool_step"), sem("pooled_ready")
        silu_done = sem("silu_done")
        gated_ready, gated_hi, gated_lo = sem("gated_ready"), sem("gated_hi"), sem("gated_lo")
        resid_half = sem("resid_half")
        m1_loaded = [sem(f"m1_loaded{i}") for i in range(2)]
        uj_ready, m1_done, xs_ready = sem("uj_ready"), sem("m1_done"), sem("xs_ready")
        rec_a, rec_b, rec_half, rec_done = sem("rec_a"), sem("rec_b"), sem("rec_half"), sem("rec_done")
        m2_loaded = [sem(f"m2_loaded{i}") for i in range(4)]
        k_loaded = [sem(f"k_loaded{i}") for i in range(4)]
        state_ready = sem("state_ready")
        bd_spread, y_done = sem("bd_spread"), sem("y_done")
        yd_ready, gelu_ready = sem("yd_ready"), sem("gelu_ready")
        g_hi, g_lo, gz_ready = sem("g_hi"), sem("g_lo"), sem("gz_ready")
        sig_ready = sem("sig_ready")
        out_turned, out_evac, out_stored = sem("out_turned"), sem("out_evac"), sem("out_stored")
        gain_loaded, out_ready, sq_added = sem("gain_loaded"), sem("out_ready"), sem("sq_added")

        block = ctx.enter_context(nc.Block())

        def flat(table):
            return table[:].rearrange("p r q a -> p (r q a)")

        QUAD_AT = {s: k for k, s in enumerate(range(1, O0.bu, 2))}
        QUAD_AT_FIRST = {s: k for k, s in enumerate((7, 9, 10, 11, 12, 13, 14, 15))}
        QPB = O0.bu // 2

        PAR_BODY = 5

        def quad_at(first, s):
            return (QUAD_AT_FIRST if first else QUAD_AT).get(s)

        def later(i):
            return not isinstance(i, int) or i > 0

        def u0_bodies(eng, body):
            body(0, True)
            with eng.Fori(1, PAR_BODY) as i:
                body(i, False)
            body(PAR_BODY, False, turning=True)
            with eng.Fori(PAR_BODY + 1, U0.bodies) as i:
                body(i, False)

        def bodies(eng, ph, body):
            body(0, True)
            with eng.Fori(1, ph.bodies) as i:
                body(i, False)

        def weight_rows(w):
            return w.rearrange("(k p) n -> p k n", p=P)

        half_blocks = E // NW
        weights = {
            U0: (weight_rows(pool_w_in[0]), 0), Z0: (weight_rows(pool_w_in[0]), half_blocks),
            GR: (weight_rows(pool_w_grp[0].rearrange("g k n -> (g k) n")), 0),
            O0: (weight_rows(pool_w_out[0]), 0),
            U2: (weight_rows(ssm_w_in[0]), 0), Z2: (weight_rows(ssm_w_in[0]), half_blocks),
            GL: (weight_rows(w_glu[0]), 0), O2: (weight_rows(ssm_w_out[0]), 0),
        }

        GROUPS_AT = {s: (2 * s, 2 * s + 1) for s in range(U0.bu - 1)}
        GROUPS_AT[U0.bu - 2] += (2 * U0.bu - 2, 2 * U0.bu - 1)
        LAST_GROUPS = 2 * U0.bu - 2

        def parameter_bank(n):
            return tb2[n % 2][:] if n >= LAST_GROUPS else tb01[:, n % 2, :]

        def parameters_out(copy, n):
            table, r, col = (BTst, CTst)[n // 8], n // 4 % 2, n % 4 * 4
            return copy(table[:, r, :, col:col + 4].rearrange("p q a -> p a q"),
                        parameter_bank(n).rearrange("p (a q) -> p a q", a=4), -1.0 if n // 4 == 3 else 1.0)

        def powers_out(copy, r):
            src = tb2[r][:].rearrange("p (k q) -> p k q", k=T)
            for k in range(1, T):
                copy(PWst[:, r, :, T - 1 - k], src[:, k - 1, :], 1.0)
            return copy(PWst[:, r, :, T:2 * T].rearrange("p q k -> p k q"), src, 1.0)

        @block.sync
        def _(sp):
            for half in range(2):
                cols = slice(half * (D // 2), (half + 1) * (D // 2))
                sp.dma_start(xrows[:, :, cols], x[0].rearrange("(s p) d -> p s d", p=P)[:, :, cols])\
                  .then_inc(x_loaded[half], 16)
            for col, vector in ((V_NORM, norm_g), (V_SCALE, pool_scale), (V_BGLU, b_glu), (V_D, ssm_d)):
                sp.dma_start(vrow[col:col + 32, :], vector.rearrange("a (t p) -> (a t) p", p=P)).then_inc(vec_loaded, 16)

            def load_unit(ph, i, s):
                w, col0 = weights[ph]
                U = ph.u0 + i * ph.bu + s
                b, su = divmod(s, ph.upb)
                if ph is GR:
                    k0, col = i * GT + su * UK, b * NW
                else:
                    k0, col = su * UK, (col0 + b) * NW + i * (ph.bb * NW)
                if ph.u0 + s >= RAW or later(i):
                    sp.wait_ge(lo_ready, U - RAW + 1)
                dst = raw[s % RAW]
                src = w[:, bass.ds(k0, UK), bass.ds(col, NW)]
                sp.dma_start(dst[:], src).then_inc(raw_loaded[s % RAW], 16)

            def plain(ph):
                def body(i, first):
                    for s in range(ph.bu):
                        load_unit(ph, i, s)
                return body

            def tables_back(part):
                if later(part):
                    sp.wait_ge(tab_back, part * (16 * 3))
                for table, dram, width in zip((BT, CT, PW), tab_dram, (PG, PG, 2 * T)):
                    pairs = 4 * QPB
                    src = dram.rearrange("p (r q a) -> p r q a", r=2, a=width)
                    sp.dma_start(table[:, :, bass.ds(part * pairs, pairs), :],
                                 src[:, :, bass.ds(part * pairs, pairs), :]).then_inc(tab_back, 16)

            def out0_body(i, first, last=False):
                for s in range(O0.bu):
                    load_unit(O0, i, s)
                    if first and s == 3:
                        sp.wait_ge(unit_done, O0.u0)
                        sp.wait_ge(tab_stored, 16 * 3)
                        tables_back(0)
                    if s == O0.bu - 5 and not last:
                        tables_back(i + 1)
                    if first and s == O0.upb - 1:
                        sp.wait_ge(gated_ready, GR.blocks)
                        sp.wait_ge(x_stored, 16)
                        sp.dma_start(xT[:], x_dram[0].rearrange("p (t l) -> p t l", t=DT)).then_inc(x_back, 16)

            def u2_body(i, first):
                for b in range(U2.bb):
                    for su in range(U2.upb):
                        load_unit(U2, i, b * U2.upb + su)
                    if first and b == 0:
                        for st in m1_stored + k_stored:
                            sp.wait_ge(st, 8 * NQUAD)
                        sp.wait_ge(gated_ready, GR.blocks)
                    if not first:
                        sp.wait_ge(m1_done, 2 * (i * 2 + b) - 2)
                    src = m1_dram[bass.ds(i * 4 + 2 * b, 2)].rearrange("q p m -> p q m")
                    sp.dma_start(m1ring[:, b].rearrange("p q r s m -> p q (r s m)"), src).then_inc(m1_loaded[b], 16)

            def load_quad(j, k):
                for ring, dram, loaded in ((kring[:, k].rearrange("p l m -> p (l m)"), k_dram, k_loaded),
                                           (m2ring[:, k].rearrange("p r s j m -> p (r s j m)"), m2_dram, m2_loaded)):
                    sp.dma_start(ring, dram[bass.ds(j * 4 + k, 1)].rearrange("q p m -> p (q m)")).then_inc(loaded[k], 16)

            def glu_body(i, first):
                for s in range(GL.bu):
                    load_unit(GL, i, s)
                    if first and s == 3:
                        sp.wait_ge(unit_done, GL.u0)
                        for st in m2_stored + k_stored:
                            sp.wait_ge(st, 8 * NQUAD)
                        for k in range(4):
                            load_quad(0, k)
                        with sp.Fori(1, NQUAD // 4) as j:
                            for k in range(4):
                                sp.wait_ge(y_done, 4 * j + k - 3)
                                load_quad(j, k)

            def out2_body(i, first):
                for s in range(O2.bu):
                    load_unit(O2, i, s)
                    if first and s == 3:
                        sp.wait_ge(unit_done, O2.u0)
                        sp.dma_start(gain[:], final_norm_g.unsqueeze(0).to_broadcast([P, D])).then_inc(gain_loaded, 16)
                    if first and s == O2.upb - 1:
                        sp.wait_ge(gated_ready, GR.blocks + GL.blocks)
                        sp.wait_ge(x_stored, 32)
                        sp.dma_start(xT[:], x_dram[1].rearrange("p (t l) -> p t l", t=DT)).then_inc(x_back, 16)

            def load_parameters():
                sp.dma_start(sw[0][:], a_re[0].rearrange("(q s) n -> q (s n)", s=2)).then_inc(params_loaded, 16)
                sp.dma_start(sw[1][:], a_im[0].rearrange("(q s) n -> q (s n)", s=2)).then_inc(params_loaded, 16)
                sp.dma_start(ldt[:], log_dt[0].rearrange("(q s) -> q s", s=2)).then_inc(params_loaded, 16)
                for i, par in enumerate((b_re, b_im)):
                    sp.dma_start(praw[:, i, :], par[0].rearrange("(q s) a b -> q (s a b)", s=2)).then_inc(params_loaded, 16)
                for i, par in enumerate((c_re, c_im)):
                    for s in range(2):
                        sp.dma_start(praw[:, 2 + i, :].rearrange("q (a s n) -> q s a n", a=PG, s=2)[:, s],
                                     par[0].rearrange("(q s) a n -> q s a n", s=2)[:, s]).then_inc(params_loaded, 16)

            def u0_body(i, first):
                for s in range(U0.bu):
                    load_unit(U0, i, s)
                    if first and s == RAW - 1:
                        load_parameters()

            bodies(sp, U0, u0_body)
            bodies(sp, Z0, plain(Z0))
            bodies(sp, GR, plain(GR))
            out0_body(0, True)
            with sp.Fori(1, O0.bodies - 1) as i:
                out0_body(i, False)
            out0_body(O0.bodies - 1, False, last=True)
            bodies(sp, U2, u2_body)
            bodies(sp, Z2, plain(Z2))
            bodies(sp, GL, glu_body)
            bodies(sp, O2, out2_body)
            rows = out[0].rearrange("(s p) d -> p s d", p=P)
            for n in range(4):
                cols = slice(n // 2 * (D // 2), (n // 2 + 1) * (D // 2))
                sp.wait_ge(out_ready, n + 1)
                sp.dma_start(rows[:, n % 2, cols], orows[:, n % 2, cols]).then_inc(out_stored, 16)
            sp.wait_ge(out_stored, 16 * 4)

        @block.gpsimd
        def _(pool):
            pool.memset(ident[:], 0.0).then_inc(consts, 1)
            pool.memset(ones[:], 1.0).then_inc(consts, 1)
            pool.memset(qmask[:], 0.0).then_inc(consts, 1)
            pool.wait_ge(consts, 3)
            pool.affine_select(out=ident[:], in_=ident[:], compare_op=ALU.not_equal, fill=1.0, base=0,
                               pattern=[[-1, P]], channel_multiplier=1).then_inc(consts, 1)
            for q in range(4):
                pool.wait_ge(consts, 4 + q)
                pool.memset(qmask[32 * q:32 * q + 32, q, :], 1.0).then_inc(consts, 1)
            pool.wait_ge(consts, 8)
            for wi, w in enumerate(WINDOWS):
                pool.memset(corr[:, wi, w - 1:], 1.0 / w).then_inc(consts, 1)
                for t in range(w - 1):
                    pool.memset(corr[:, wi, t:t + 1], 1.0 / (t + 1)).then_inc(consts, 1)

            done = [0]

            def step(ins):
                ins.then_inc(chain, 1)
                done[0] += 1
                pool.wait_ge(chain, done[0])

            def mul(o, a, b):
                step(pool.tensor_tensor(o, a, b, ALU.mult))

            def add(o, a, b):
                step(pool.tensor_tensor(o, a, b, ALU.add))

            def sub(o, a, b):
                step(pool.tensor_tensor(o, a, b, ALU.subtract))

            def affine(o, a, m, c):
                step(pool.tensor_scalar(o, a, m, c, ALU.mult, ALU.add))

            MAGIC = 12582912.0

            def nearest(o, a, m):
                affine(o, a, m, MAGIC)
                step(pool.tensor_scalar(o, o, MAGIC, None, ALU.subtract))

            def cody(c, *bits):
                parts, rest = [], c
                for b in bits:
                    e = math.floor(math.log2(abs(rest)))
                    q = 2.0 ** (e - b + 1)
                    parts.append(math.floor(rest / q) * q)
                    rest -= parts[-1]
                return parts + [float(np.float32(rest))]

            def reduce_by(o, a, k, parts, t):
                for n, part in enumerate(parts):
                    step(pool.tensor_scalar(t, k, -part, None, ALU.mult))
                    add(o, a if n == 0 else o, t)

            def horner(o, c, r):
                step(pool.tensor_scalar(o, o, c, None, ALU.add))
                mul(o, o, r)

            def exp(o, a, t):
                k, r, e = t
                step(pool.tensor_scalar(o, a, -110.0, 90.0, ALU.max, ALU.min))
                nearest(k, o, 1.0 / math.log(2.0))
                reduce_by(r, o, k, cody(math.log(2.0), 9, 12), e)
                step(pool.tensor_scalar(e, r, 1.0 / math.factorial(7), None, ALU.mult))
                for n in range(6, 0, -1):
                    horner(e, 1.0 / math.factorial(n), r)
                step(pool.tensor_scalar(e, e, 1.0, None, ALU.add))
                nearest(r, k, 0.5)
                sub(k, k, r)
                for half in (r, k):
                    pw = swi[0] if half is r else swi[1]
                    pw = pw[:, 0:half.shape[1]]
                    affine(half, half, 2.0 ** 23, 127.0 * 2.0 ** 23)
                    step(pool.tensor_copy(pw, half))
                    mul(e if half is r else o, e, pw.bitcast(F32))

            pool.wait_ge(params_loaded, 16 * 9)
            are, aim = sw[0][:], sw[1][:]
            t0, t1, den = sw[14][:], sw[15][:], sden[:]
            mul(t0, are, are)
            mul(t1, aim, aim)
            add(den, t0, t1)
            pool.sem_inc(den_ready, 1)
            dtv = sw[2][:, 0:2]
            exp(dtv, ldt[:], (sw[3][:, 0:2], sw[4][:, 0:2], sw[5][:, 0:2]))
            dtb = sw[2][:, 0:2].unsqueeze(2).to_broadcast([P, 2, NS])
            y, th, mag = sw[6][:], sw[7][:], sw[8][:]
            mul(y.rearrange("p (s n) -> p s n", s=2), are.rearrange("p (s n) -> p s n", s=2), dtb)
            mul(th.rearrange("p (s n) -> p s n", s=2), aim.rearrange("p (s n) -> p s n", s=2), dtb)
            exp(mag, y, (sw[3][:], sw[4][:], sw[5][:]))
            q, r, r2, m = sw[3][:], sw[4][:], sw[5][:], sw[6][:]
            nearest(q, th, 2.0 / math.pi)
            reduce_by(r, th, q, cody(math.pi / 2, 8, 11, 11), r2)
            mul(r2, r, r)
            sn, cs = sw[9][:], sw[10][:]
            for o, top, low in ((sn, 9, 3), (cs, 8, 2)):
                sign = lambda n: -1.0 if n % 4 in (2, 3) else 1.0
                step(pool.tensor_scalar(o, r2, sign(top) / math.factorial(top), None, ALU.mult))
                for n in range(top - 2, low - 1, -2):
                    horner(o, sign(n) / math.factorial(n), r2)
                step(pool.tensor_scalar(o, o, 1.0, None, ALU.add))
            mul(sn, sn, r)
            nearest(m, q, 0.25)
            step(pool.tensor_scalar(m, m, -4.0, None, ALU.mult))
            add(m, m, q)
            ab, cm, sm = sw[11][:], sw[12][:], sw[13][:]
            step(pool.tensor_scalar(ab, m, 0.0, 2.0, ALU.max, ALU.mult))
            sub(ab, ab, m)
            affine(cm, ab, -1.0, 1.0)
            affine(sm, ab, -1.0, 2.0)
            mul(sm, sm, m)
            co, si = sw[16][:], sw[17][:]
            mul(t0, cs, cm)
            mul(t1, sn, sm)
            sub(co, t0, t1)
            mul(t0, sn, cm)
            mul(t1, cs, sm)
            add(si, t0, t1)
            mul(co, co, mag)
            mul(si, si, mag)
            for k in range(2, T + 1):
                pr, pi = sw[14 + 2 * (k - 1)][:], sw[15 + 2 * (k - 1)][:]
                nr_, ni_ = sw[14 + 2 * k][:], sw[15 + 2 * k][:]
                mul(t0, pr, co)
                mul(t1, pi, si)
                sub(nr_, t0, t1)
                mul(t0, pr, si)
                mul(t1, pi, co)
                add(ni_, t0, t1)
            nr, fr, fi = sw[3][:], sw[5][:], sw[6][:]
            step(pool.tensor_scalar(nr, co, -1.0, None, ALU.add))
            pool.wait_ge(den_inverted, 1)
            mul(t0, nr, are)
            mul(t1, si, aim)
            add(fr, t0, t1)
            mul(fr, fr, den)
            mul(t0, si, are)
            mul(t1, nr, aim)
            sub(fi, t0, t1)
            mul(fi, fi, den)
            view = lambda a: a.rearrange("p (s a) -> p s a", a=PG)
            frb = fr.unsqueeze(2).to_broadcast([P, 2 * NS, PG])
            fib = fi.unsqueeze(2).to_broadcast([P, 2 * NS, PG])
            pool.wait_ge(x_stored, 16)
            pool.wait_ge(hn_ready, DT // 2)
            mul(view(bbar[:, 0, :]), view(praw[:, 0, :]), frb)
            mul(view(fbp[:]), view(praw[:, 1, :]), fib)
            sub(bbar[:, 0, :], bbar[:, 0, :], fbp[:])
            mul(view(bbar[:, 1, :]), view(praw[:, 1, :]), frb)
            mul(view(fbp[:]), view(praw[:, 0, :]), fib)
            add(bbar[:, 1, :], bbar[:, 1, :], fbp[:])
            pool.sem_inc(chain_done, 1)

            pool.wait_ge(xt_ready, 8)
            pool.memset(u0[:, :, 0:PAD], 0.0).then_inc(pool_step, 1)
            pool.wait_ge(tab_stored, 16 * 3)
            steps = 1
            for wi, w in enumerate(WINDOWS):
                nd = wi + 1
                per = nd + 4
                with pool.Fori(0, GT // 2) as i:
                    for b in range(2):
                        t = wi * GT + i * 2 + b
                        at0 = steps + i * (2 * per) + b * per
                        if b == 0:
                            pool.wait_ge(nb_evac, wi * (GT // 2) + i + 1)
                        src = u0[:, bass.ds(t, 1), :].rearrange("p a l -> p (a l)")
                        spot = pwin_b[:, bass.ds(t, 1), :].rearrange("p a l -> p (a l)")
                        bufs = (pwin_a[:], spot)
                        if nd % 2 == 0:
                            order = (0, 1)
                        else:
                            order = (1, 0)
                        cur, lo = src, 0
                        for k in range(nd):
                            sh = 1 << k
                            lo += sh
                            dst = bufs[order[k % 2]]
                            pool.wait_ge(pool_step, at0 + k)
                            pool.tensor_tensor(dst[:, lo:PAD + L], cur[:, lo:PAD + L],
                                               cur[:, lo - sh:PAD + L - sh], ALU.add).then_inc(pool_step, 1)
                            cur = dst
                        pool.wait_ge(pool_step, at0 + nd)
                        pool.tensor_tensor(pwin_a[:, PAD:2 * PAD], cur[:, PAD:2 * PAD], corr[:, wi, :], ALU.mult)
                        pool.tensor_tensor(pwin_a[:, 2 * PAD:], cur[:, 2 * PAD:PAD + L],
                                           corr[:, wi, PAD - 1:].to_broadcast([P, L - PAD]),
                                           ALU.mult).then_inc(pool_step, 1)
                        pool.wait_ge(pool_step, at0 + nd + 1)
                        pool.tensor_tensor(pwin_a[:, PAD:], pwin_a[:, PAD:], src[:, PAD:PAD + L],
                                           ALU.subtract).then_inc(pool_step, 1)
                        pool.wait_ge(pool_step, at0 + nd + 2)
                        hi = pooled[:, bass.ds(t, 1), 0, :].rearrange("p a l -> p (a l)")
                        low = pooled[:, bass.ds(t, 1), 1, :].rearrange("p a l -> p (a l)")
                        pool.tensor_copy(hi, pwin_a[:, PAD:]).then_inc(pool_step, 1)
                        pool.wait_ge(pool_step, at0 + nd + 3)
                        pool.tensor_tensor(low, pwin_a[:, PAD:], hi.bitcast(F32), ALU.subtract).then_inc(pool_step, 1)
                    pool.wait_ge(pool_step, steps + i * (2 * per) + 2 * per)
                    pool.sem_inc(pooled_ready, 1)
                steps += per * GT

            pool.wait_ge(unit_done, O0.u0)
            pool.memset(MB[:], 0.0).then_inc(tab_zeroed, 1)
            pool.memset(MC[:], 0.0).then_inc(tab_zeroed, 1)
            pool.wait_ge(gated_ready, GR.blocks)

            def quad_products(i):
                for src, K, pr, used in ((BT, T, prodb, mb_ready), (CT, T + 1, prodc, mc_ready)):
                    if later(i):
                        pool.wait_ge(used, i)
                    for n, (r, part) in enumerate(((0, 0), (1, 1), (0, 1), (1, 0))):
                        in0 = src[:, r, bass.ds(i * 4, 4), :].unsqueeze(2).to_broadcast([P, 4, K, PG])
                        powers = slice(0, T) if src is BT else slice(T - 1, 2 * T)
                        pw = PW[:, part, bass.ds(i * 4, 4), powers]
                        ins = pool.tensor_tensor(pr[:, n], in0, pw.unsqueeze(3).to_broadcast([P, 4, K, PG]), ALU.mult)
                    ins.then_inc(prods_ready, 1)

            for part in range(O0.bodies):
                pool.wait_ge(tab_back, (part + 1) * (16 * 3))
                if part == 0:
                    quad_products(0)
                with pool.Fori(max(1, part * QPB), (part + 1) * QPB) as i:
                    quad_products(i)

            for n in range(DT // 2):
                pool.wait_ge(hn_hi, DT // 2 + n + 1)
                pool.tensor_tensor(h[:, 2 * n:2 * n + 2, 1, :], v[:, n % 2],
                                   h[:, 2 * n:2 * n + 2, 0, :].bitcast(F32), ALU.subtract).then_inc(hn_lo, 1)

            pool.wait_ge(xs_ready, NQUAD)
            with pool.Fori(0, 7) as i:
                for k in range(9):
                    c1 = i * 9 + k
                    pool.wait_ge(rec_done, c1 + 1)
                    src = XS[:, :, :, :, bass.ds(c1, 1)].rearrange("p a r s c -> p a r (s c)")
                    pool.tensor_tensor(rec2[:, :, ::-1, :], a4b[:], src, ALU.mult).then_inc(rec_b, 1)

            pool.wait_ge(silu_done, Z0.blocks + Z2.blocks)
            with pool.Fori(0, NQUAD // 2) as i:
                for b in range(2):
                    qd = i * 2 + b
                    pool.wait_ge(gelu_ready, qd + 1)
                    z = zs[:, bass.ds(qd, 1), :].rearrange("p a l -> p (a l)")
                    pool.tensor_tensor(z, z, tmp[:, b, 1, :], ALU.mult).then_inc(gz_ready, 1)

        @block.scalar
        def _(act):
            def split(ph, i, s):
                U = ph.u0 + i * ph.bu + s
                act.wait_ge(raw_loaded[s % RAW], 16 * ((ph.u0 + s) // RAW + 1) + i * (16 * ph.bu // RAW))
                if ph.u0 + s >= SPLIT or later(i):
                    act.wait_ge(unit_done, U - SPLIT + 1)
                act.copy(whi[s % SPLIT][:], raw[s % RAW][:]).then_inc(hi_ready, 1)

            def evac(ph, i, b):
                G = ph.g0 + i * ph.bb + b
                act.wait_ge(unit_done, ph.u0 + i * ph.bu + (b + 1) * ph.upb)
                if ph is U0 and (b > 0 or later(i)):
                    act.wait_ge(nb_evac, G)
                elif ph is not U0:
                    act.wait_ge(nb_evac, G - 1)
                act.copy(tmp[:, b % 2], acc[b % 2][:, :, L:2 * L]).then_inc(tmp_ready, 1)

            def before(ph, i, b, lag):
                b -= lag
                if b < 0:
                    b += ph.bb
                    i = i - 1
                return i, b

            def silu(ph, i, b):
                act.wait_ge(nb_evac, ph.g0 + i * ph.bb + b + 1)
                act.activation(zs[:, bass.ds(i * (2 * ph.bb) + 2 * b, 2), :], v[:, b % 2], ACT.Silu)\
                   .then_inc(silu_done, 1)

            def gated_round(ph, i, b, counted):
                n = counted + i * ph.bb + b
                act.wait_ge(gated_ready, n + 1)
                act.mul(gated[:, bass.ds(i * (2 * ph.bb) + 2 * b, 2), 0, :], v[:, b % 2], 1.0).then_inc(gated_hi, 1)

            def quad_out(i, k):
                b, qd = k % 2, i * QPB + k
                act.wait_ge(quad_turned, qd + 1)
                if k >= 2 or later(i):
                    act.wait_ge(m1_stored[b], i * (8 * QPB) + 16 * (k // 2))
                act.copy(m1st[:, b].rearrange("p r s m -> p (r s m)"),
                         tb01[:].rearrange("p r m -> p (r m)")).then_inc(m1_evac, 1)
                act.wait_ge(m1_evac, qd + 1)
                act.dma_start(m1_dram[bass.ds(qd, 1)].rearrange("q p m -> p (q m)"),
                              m1st[:, b].rearrange("p r s m -> p (r s m)")).then_inc(m1_stored[b], 16)
                act.wait_ge(mc_ready, qd + 1)
                act.dma_start(m2_dram[bass.ds(qd, 1)].rearrange("q p (r m) -> p (q r) m", r=8),
                              MC[:, b, :, :, 1:T + 1].rearrange("p r s k g a -> p (r s) (k g a)"))\
                   .then_inc(m2_stored[b], 16)
                act.wait_ge(k_evac, qd + 1)
                act.dma_start(k_dram[bass.ds(qd, 1)].rearrange("q p m -> p (q m)"), kst[:, b]).then_inc(k_stored[b], 16)

            def bring_root_table():
                act.activation(spare[:], ones[:, 0:1], ACT.Sqrt)

            def root(which, src, dst):
                act.wait_ge(var_ready, which + 1)
                act.activation(dst, src, ACT.Sqrt).then_inc(root_ready, 1)

            def norm(which, ph):
                root(which, tmp[:, 0, 0, :], tmp[:, 0, 1, :])
                for n in range(DT // 2):
                    if n == 4:
                        split(ph, 0, 2)
                    act.wait_ge(hn_ready, which * 8 + n + 1)
                    act.copy(h[:, 2 * n:2 * n + 2, 0, :], v[:, n % 2]).then_inc(hn_hi, 1)

            def square_pair(which, n, b, src):
                if isinstance(n, int) and n == 0:
                    act.activation(sqsum[:], src, ACT.Square).then_inc(sq_ready, 1)
                else:
                    if isinstance(n, int) and n >= 2:
                        act.wait_ge(sq_added, which * (DT // 2) + n - 1)
                    elif not isinstance(n, int) or which > 0:
                        act.wait_ge(sq_added, which * (DT // 2) + n)
                    act.activation(v[:, b], src, ACT.Square).then_inc(sq_ready, 1)

            def squares(ph, i, b):
                n = i * ph.bb + b
                act.wait_ge(nb_evac, ph.g0 + n + 1)
                if ph is O0:
                    square_pair(1, n, b, xT[:, bass.ds(2 * n, 2), :])
                else:
                    square_pair(2, n, b, last[:, b])

            for n in range(DT // 2 + 1):
                if n < DT // 2:
                    act.wait_ge(xt_turned, n + 1)
                    act.copy(xT[:, 2 * n:2 * n + 2, :], tb01[:, n % 2, :].rearrange("p (t l) -> p t l", t=2))\
                       .then_inc(xt_ready, 1)
                if n > 0:
                    act.wait_ge(xt_ready, n)
                    square_pair(0, n - 1, (n - 1) % 2, xT[:, 2 * n - 2:2 * n, :])
            act.wait_ge(vec_turned, 1)
            act.copy(vec[:], tb2[0][:, 0:P]).then_inc(vec_ready, 1)
            act.dma_start(x_dram[0].rearrange("p (t l) -> p t l", t=DT), xT[:]).then_inc(x_stored, 16)
            norm(0, U0)

            def tables_out(s):
                if s == 0:
                    act.wait_ge(powers_turned, 1)
                    powers_out(act.mul, 0).then_inc(powers_ready, 1)
                for n in GROUPS_AT[s][0::2]:
                    act.wait_ge(par_turned, n + 1)
                    parameters_out(act.mul, n).then_inc(par_evac[0], 1)
                if s == 2:
                    act.wait_ge(powers_ready, 3)
                    act.dma_start(tab_dram[2], flat(PWst)).then_inc(tab_stored, 16)
                if s in (U0.bu // 2 - 1, U0.bu - 2):
                    done = GROUPS_AT[s][-1] // 2 + 1
                    act.wait_ge(par_evac[0], done)
                    act.wait_ge(par_evac[1], done)
                    table, dram = ((BTst, tab_dram[0]), (CTst, tab_dram[1]))[s == U0.bu - 2]
                    act.dma_start(dram, flat(table)).then_inc(tab_stored, 16)

            def u0_body(i, first, turning=False):
                for b in range(U0.bb):
                    for su in range(U0.upb):
                        s = b * U0.upb + su
                        if not (first and s <= SPLIT):
                            split(U0, i, s)
                        if su == 1 and not (first and b == 0):
                            evac(U0, *before(U0, i, b, 1))
                        if turning and s > 0:
                            tables_out(s - 1)

            def z0_body(i, first):
                for b in range(Z0.bb):
                    for su in range(Z0.upb):
                        split(Z0, i, b * Z0.upb + su)
                        if first and b == 0:
                            if su == 1:
                                evac(U0, U0.bodies - 1, U0.bb - 1)
                                act.wait_ge(x_stored, 16)
                                act.wait_ge(tab_stored, 16 * 3)
                        elif su == 1:
                            evac(Z0, *before(Z0, i, b, 1))
                        elif su == 3:
                            silu(Z0, *before(Z0, i, b, 1))

            def grp_body(i, first):
                for b in range(GR.bb):
                    for su in range(GR.upb):
                        split(GR, i, b * GR.upb + su)
                        if su == 0 and not (first and b < 2):
                            gated_round(GR, *before(GR, i, b, 2), 0)
                        if su == 1:
                            if first and b == 0:
                                evac(Z0, Z0.bodies - 1, Z0.bb - 1)
                                silu(Z0, Z0.bodies - 1, Z0.bb - 1)
                                act.wait_ge(pooled_ready, ET // 2)
                            else:
                                evac(GR, *before(GR, i, b, 1))

            def out0_body(i, first):
                for b in range(O0.bb):
                    for su in range(O0.upb):
                        split(O0, i, b * O0.upb + su)
                        if first and b == 0:
                            if su == 0:
                                gated_round(GR, GR.bodies - 1, GR.bb - 2, 0)
                            if su == 1:
                                evac(GR, GR.bodies - 1, GR.bb - 1)
                            if su == 3:
                                gated_round(GR, GR.bodies - 1, GR.bb - 1, 0)
                        elif su == 1:
                            evac(O0, *before(O0, i, b, 1))
                        elif su == 3:
                            squares(O0, *before(O0, i, b, 1))
                        k = quad_at(first, b * O0.upb + su)
                        if k is not None and not (first and k == 0):
                            quad_out(i if k else i - 1, (k - 1) % QPB)

            def chunk_inputs_out(n):
                for tt in range(2):
                    act.wait_ge(m1_done, 2 * n + tt + 1)
                    act.mul(XS[:, bass.ds(2 * n + tt, 1)].rearrange("p a r s c -> p (a r s c)"),
                            tb01[:, tt, :], 1.0).then_inc(xs_ready, 1)

            def u2_body(i, first):
                for b in range(U2.bb):
                    for su in range(U2.upb):
                        if not (first and b == 0 and su == 2):
                            split(U2, i, b * U2.upb + su)
                        if su == 1:
                            if first and b == 0:
                                evac(O0, O0.bodies - 1, O0.bb - 1)
                                bring_root_table()
                                act.wait_ge(nb_evac, U2.g0)
                                squares(O0, O0.bodies - 1, O0.bb - 1)
                                act.dma_start(x_dram[1].rearrange("p (t l) -> p t l", t=DT), xT[:])\
                                   .then_inc(x_stored, 16)
                                quad_out(O0.bodies - 1, QPB - 1)
                                norm(1, U2)
                            else:
                                evac(U2, *before(U2, i, b, 1))
                        if su == 1 and not (first and b < 2):
                            chunk_inputs_out(i * 2 + b - 2)

            def z2_body(i, first):
                for b in range(Z2.bb):
                    for su in range(Z2.upb):
                        split(Z2, i, b * Z2.upb + su)
                        if first and b == 0:
                            if su == 1:
                                evac(U2, U2.bodies - 1, U2.bb - 1)
                                chunk_inputs_out(U2.blocks - 2)
                        elif su == 1:
                            evac(Z2, *before(Z2, i, b, 1))
                            if first:
                                chunk_inputs_out(U2.blocks - 1)
                        elif su == 3:
                            silu(Z2, *before(Z2, i, b, 1))

            def state_out(j, k):
                if later(j) or k >= 2:
                    act.wait_ge(y_done, j * 4 + k - 1)
                act.mul(state[:, k % 2].rearrange("p r s c -> p (r s c)"),
                        XS[:, bass.ds(j * 4 + k, 1)].rearrange("p a r s c -> p (a r s c)"), 1.0).then_inc(state_ready, 1)

            def gelu_out(j, k):
                qd, bb = j * 4 + k, k % 2
                act.wait_ge(yd_ready, qd + 1)
                act.activation(tmp[:, bb, 1, :], tmp[:, bb, 0, :], ACT.Gelu_apprx_tanh).then_inc(gelu_ready, 1)
                act.activation(g[:, bass.ds(qd, 1), 0, :].rearrange("p a l -> p (a l)"), tmp[:, bb, 0, :],
                               ACT.Gelu_apprx_tanh).then_inc(g_hi, 1)

            def glu_body(i, first):
                for b in range(GL.bb):
                    for su in range(GL.upb):
                        split(GL, i, b * GL.upb + su)
                        if first and b == 0:
                            if su == 1:
                                evac(Z2, Z2.bodies - 1, Z2.bb - 1)
                                silu(Z2, Z2.bodies - 1, Z2.bb - 1)
                                act.wait_ge(rec_done, NC)
                                act.wait_ge(unit_done, GL.u0)
                                for k in range(4):
                                    if k >= 2:
                                        gelu_out(0, k - 2)
                                    state_out(0, k)
                                with act.Fori(1, NQUAD // 4) as j:
                                    for k in range(4):
                                        gelu_out(j, k - 2)
                                        state_out(j, k)
                                gelu_out(NQUAD // 4 - 1, 2)
                                gelu_out(NQUAD // 4 - 1, 3)
                        elif su == 1:
                            if first:
                                act.wait_ge(gz_ready, NQUAD)
                            evac(GL, *before(GL, i, b, 1))
                        elif su == 3:
                            sigmoid(*before(GL, i, b, 1))
                        elif su == 5:
                            gated_round(GL, *before(GL, i, b, 1), GR.blocks)

            def sigmoid(i, b):
                act.wait_ge(nb_evac, GL.g0 + i * 2 + b + 1)
                for tt in range(2):
                    bias = vec[:, bass.ds(V_BGLU + i * 4 + b * 2 + tt, 1)]
                    ins = act.activation(v[:, b % 2, tt, :], v[:, b % 2, tt, :], ACT.Sigmoid, bias=bias)
                ins.then_inc(sig_ready, 1)

            def out2_body(i, first):
                for b in range(O2.bb):
                    for su in range(O2.upb):
                        split(O2, i, b * O2.upb + su)
                        if first and b == 0:
                            if su == 1:
                                evac(GL, GL.bodies - 1, GL.bb - 1)
                                sigmoid(GL.bodies - 1, GL.bb - 1)
                            if su == 3:
                                gated_round(GL, GL.bodies - 1, GL.bb - 1, GR.blocks)
                        elif su == 1:
                            evac(O2, *before(O2, i, b, 1))
                        elif su == 3:
                            squares(O2, *before(O2, i, b, 1))
                        elif su == 5:
                            rows_out(*before(O2, i, b, 1))

            def rows_out(i, b):
                n = i * O2.bb + b
                act.wait_ge(out_turned, n + 1)
                act.mul(orows[:, :, bass.ds(256 * n, 256)], tb01[:, b % 2, :].rearrange("p (s c) -> p s c", s=2), 1.0)\
                   .then_inc(out_evac, 1)

            u0_bodies(act, u0_body)
            bodies(act, Z0, z0_body)
            bodies(act, GR, grp_body)
            bodies(act, O0, out0_body)
            bodies(act, U2, u2_body)
            bodies(act, Z2, z2_body)
            bodies(act, GL, glu_body)
            bodies(act, O2, out2_body)
            evac(O2, O2.bodies - 1, O2.bb - 1)
            bring_root_table()
            squares(O2, O2.bodies - 1, O2.bb - 1)
            rows_out(O2.bodies - 1, O2.bb - 1)
            root(2, tmp[:, 0, 0, 0:2], tmp[:, 0, 1, 0:2])

        @block.vector
        def _(dve):
            def powers_for_recurrence():
                for r_, scale, dst in ((0, 1.0, a4a[:, :, 0, :]), (0, 1.0, a4a[:, :, 1, :]),
                                       (1, 1.0, a4b[:, :, 0, :]), (1, -1.0, a4b[:, :, 1, :])):
                    pw = PW[:, r_, :, 2 * T - 1].rearrange("p (a s) -> p a s", s=4)
                    ins = dve.tensor_scalar(dst, pw, scale, None, ALU.mult)

            def quad_sums(i, k):
                b, qd = k % 2, i * QPB + k
                for M, pr, ready, minus in ((MB, prodb, mb_ready, 0), (MC, prodc, mc_ready, 1)):
                    dve.wait_ge(prods_ready, 2 * qd + minus + 1)
                    if k >= 2 or later(i):
                        if minus == 0:
                            dve.wait_ge(quad_turned, qd - 1)
                            dve.wait_ge(k_ready, qd - 1)
                        else:
                            dve.wait_ge(m2_stored[b], i * (8 * QPB) + 16 * (k // 2))
                    for r in range(2):
                        a_, b_ = (0, 1) if r == 0 else ((2, 3) if minus == 0 else (3, 2))
                        for half in range(2):
                            rows = slice(64 * half, 64 * half + 64)
                            ins = dve.tensor_tensor(M[rows, b, r, :, :, half, :], pr[rows, a_], pr[rows, b_],
                                                    ALU.subtract if r == minus else ALU.add)
                    ins.then_inc(ready, 1)

            def quad_k(i, k):
                b, qd = k % 2, i * QPB + k
                dve.wait_ge(k_ready, qd + 1)
                if k >= 2 or later(i):
                    dve.wait_ge(k_stored[b], i * (8 * QPB) + 16 * (k // 2))
                dve.tensor_scalar(kst[:, b], tb2[b][:, 0:T * 32], 1.0, None, ALU.mult).then_inc(k_evac, 1)

            def split(ph, i, s):
                U = ph.u0 + i * ph.bu + s
                dve.wait_ge(hi_ready, U + 1)
                dve.tensor_tensor(wlo[s % SPLIT][:], raw[s % RAW][:], whi[s % SPLIT][:].bitcast(F32),
                                  ALU.subtract).then_inc(lo_ready, 1)

            norm_steps = [0]

            def nstep(ins):
                ins.then_inc(norm_step, 1)
                norm_steps[0] += 1
                dve.wait_ge(norm_step, norm_steps[0])

            def inverse_root(which, var, root, inv, t, sums):
                dve.wait_ge(sq_summed, which + 1)
                dve.tensor_scalar(var, sums, 1.0 / D, EPS, ALU.mult, ALU.add).then_inc(var_ready, 1)
                dve.wait_ge(root_ready, which + 1)
                nstep(dve.reciprocal(inv, root))
                nstep(dve.tensor_tensor(t, inv, inv, ALU.mult))
                nstep(dve.tensor_tensor(t, t, var, ALU.mult))
                nstep(dve.tensor_scalar(t, t, -0.5, 1.5, ALU.mult, ALU.add))
                nstep(dve.tensor_tensor(inv, inv, t, ALU.mult))

            def norm(which, ph, v_gain, order):
                inv = tmp[:, 1, 0, :]
                inverse_root(which, tmp[:, 0, 0, :], tmp[:, 0, 1, :], inv, tmp[:, 1, 1, :], tb2[1 - which][:, 0:L])
                for n in range(DT // 2 + 1):
                    if n < DT // 2:
                        if n >= 2:
                            dve.wait_ge(hn_lo, which * 8 + n - 1)
                        for tt in range(2):
                            ft = 2 * n + tt
                            o, i_, iv = v[:, n % 2, tt, :], xT[:, ft, :], inv
                            if order == "chunks":
                                o = o.rearrange("p (j c) -> p c j", j=T)
                                i_ = i_.rearrange("p (c j) -> p c j", j=T)
                                iv = iv.rearrange("p (c j) -> p c j", j=T)
                            ins = dve.scalar_tensor_tensor(o, i_, vec[:, v_gain + ft:v_gain + ft + 1], iv,
                                                           ALU.mult, ALU.mult)
                        ins.then_inc(hn_ready, 1)
                    if n == 5:
                        split(ph, 0, 2)
                    if n >= 1 and which == 0:
                        m_ = n - 1
                        dve.wait_ge(hn_hi, which * 8 + n)
                        dve.tensor_tensor(h[:, 2 * m_:2 * m_ + 2, 1, :], v[:, m_ % 2],
                                          h[:, 2 * m_:2 * m_ + 2, 0, :].bitcast(F32), ALU.subtract)\
                           .then_inc(hn_lo, 1)

            def add_square_pair(which, n, b):
                dve.wait_ge(sq_ready, which * (DT // 2) + n + 1)
                if isinstance(n, int) and n == 0:
                    dve.sem_inc(sq_added, 1)
                else:
                    dve.wait_ge(sq_added, which * (DT // 2) + n)
                    dve.tensor_tensor(sqsum[:], sqsum[:], v[:, b], ALU.add).then_inc(sq_added, 1)

            def add_squares(ph, i, b):
                add_square_pair(1 if ph is O0 else 2, i * ph.bb + b, b)

            def split_first(s):
                dve.wait_ge(raw_loaded[s], 16)
                dve.tensor_copy(whi[s][:], raw[s][:]).then_inc(hi_ready, 1)
                split(U0, 0, s)

            for n in range(DT // 2):
                add_square_pair(0, n, n % 2)
                if n in (4, 6):
                    split_first((n - 4) // 2)
            dve.wait_ge(vec_ready, 1)
            norm(0, U0, V_NORM, "tokens")

            def before(ph, i, b, lag):
                b -= lag
                if b < 0:
                    b += ph.bb
                    i = i - 1
                return i, b

            def add_up(ph, i, b, dst):
                G = ph.g0 + i * ph.bb + b
                dve.wait_ge(tmp_ready, G + 1)
                dve.tensor_tensor(dst, acc[b % 2][:, :, 0:L], tmp[:, b % 2], ALU.add).then_inc(nb_evac, 1)

            def tiles(i, ph, b):
                return bass.ds(i * (2 * ph.bb) + 2 * b, 2)

            def gated_low(ph, i, b, counted):
                n = counted + i * ph.bb + b
                dve.wait_ge(gated_hi, n + 1)
                dve.tensor_tensor(gated[:, tiles(i, ph, b), 1, :], v[:, b % 2],
                                  gated[:, tiles(i, ph, b), 0, :].bitcast(F32), ALU.subtract).then_inc(gated_lo, 1)

            def u0_out(i, b):
                add_up(U0, i, b, u0[:, tiles(i, U0, b), PAD:PAD + L])

            def scaled(dst, src, scale):
                return dve.tensor_scalar(dst, src, scale, None, ALU.mult)

            def tables_out(s):
                if s == 0:
                    dve.wait_ge(powers_turned, 1)
                    powers_out(scaled, 1).then_inc(powers_ready, 1)
                    dve.memset(PWst[:, 0, :, T - 1], 1.0)
                    dve.memset(PWst[:, 1, :, T - 1], 0.0).then_inc(powers_ready, 1)
                for n in GROUPS_AT[s][1::2]:
                    dve.wait_ge(par_turned, n + 1)
                    parameters_out(scaled, n).then_inc(par_evac[1], 1)

            def u0_body(i, first, turning=False):
                for b in range(U0.bb):
                    for su in range(U0.upb):
                        s = b * U0.upb + su
                        if not (first and s <= SPLIT):
                            split(U0, i, s)
                        if turning and s > 0:
                            tables_out(s - 1)
                        if su == 1 and not (first and b == 0):
                            if first:
                                dve.wait_ge(xt_ready, 8)
                            u0_out(*before(U0, i, b, 1))
                if first:
                    dve.wait_ge(den_ready, 1)
                    dve.reciprocal(sden[:], sden[:]).then_inc(den_inverted, 1)

            def z_out(ph, i, b, counted):
                n = counted + i * ph.bb + b
                if later(i) or i * ph.bb + b > 0 or counted > 0:
                    dve.wait_ge(silu_done, n)
                add_up(ph, i, b, v[:, b % 2])

            def z0_body(i, first):
                for b in range(Z0.bb):
                    for su in range(Z0.upb):
                        split(Z0, i, b * Z0.upb + su)
                        if su == 1:
                            if first and b == 0:
                                u0_out(U0.bodies - 1, U0.bb - 1)
                            else:
                                z_out(Z0, *before(Z0, i, b, 1), 0)

            def grp_out(i, b):
                n = i * GR.bb + b
                if not (isinstance(i, int) and i == 0 and b < 2):
                    dve.wait_ge(gated_lo, n - 1)
                if isinstance(i, int) and i == 0 and b == 0:
                    dve.wait_ge(silu_done, Z0.blocks)
                add_up(GR, i, b, v[:, b % 2])
                dve.wait_ge(nb_evac, GR.g0 + n + 1)
                for tt in range(2):
                    ft = i * (2 * GR.bb) + 2 * b + tt
                    ins = dve.scalar_tensor_tensor(
                        v[:, b % 2, tt, :], v[:, b % 2, tt, :], vec[:, bass.ds(V_SCALE + ft, 1)],
                        zs[:, bass.ds(ft, 1), :].rearrange("p a l -> p (a l)"), ALU.mult, ALU.mult)
                ins.then_inc(gated_ready, 1)

            def grp_body(i, first):
                for b in range(GR.bb):
                    for su in range(GR.upb):
                        split(GR, i, b * GR.upb + su)
                        if su == 0 and not (first and b < 2):
                            gated_low(GR, *before(GR, i, b, 2), 0)
                        if su == 1:
                            if first and b == 0:
                                z_out(Z0, Z0.bodies - 1, Z0.bb - 1, 0)
                            else:
                                grp_out(*before(GR, i, b, 1))

            def resid(ph, i, b, order, counted):
                G = ph.g0 + i * ph.bb + b
                xv = xT[:, tiles(i, ph, b), :]
                hl, hh = tmp[:, b % 2], acc[b % 2][:, :, 0:L]
                if order == "chunks":
                    xv = xv.rearrange("p t (c j) -> p t c j", j=T)
                    hl = hl.rearrange("p t (j c) -> p t c j", j=T)
                    hh = hh.rearrange("p t (j c) -> p t c j", j=T)
                dve.wait_ge(tmp_ready, G + 1)
                dve.tensor_tensor(xv, xv, hl, ALU.add).then_inc(resid_half, 1)
                dve.wait_ge(resid_half, counted + i * ph.bb + b + 1)
                if ph is O2:
                    n = i * ph.bb + b
                    if later(n):
                        dve.wait_ge(out_turned, n)
                        dve.wait_ge(sq_ready, 2 * (DT // 2) + n)
                    dst = last[:, b].rearrange("p t (c j) -> p t c j", j=T)
                else:
                    dst = xv
                dve.tensor_tensor(dst, hh, xv, ALU.add).then_inc(nb_evac, 1)

            def out0_body(i, first):
                for b in range(O0.bb):
                    for su in range(O0.upb):
                        split(O0, i, b * O0.upb + su)
                        if first and b == 0:
                            if su == 0:
                                gated_low(GR, GR.bodies - 1, GR.bb - 2, 0)
                            if su == 1:
                                grp_out(GR.bodies - 1, GR.bb - 1)
                            if su == 3:
                                gated_low(GR, GR.bodies - 1, GR.bb - 1, 0)
                        elif su == 1:
                            if first:
                                dve.wait_ge(x_back, 16)
                            resid(O0, *before(O0, i, b, 1), "tokens", 0)
                        elif su == 5:
                            add_squares(O0, *before(O0, i, b, 1))
                        k = quad_at(first, b * O0.upb + su)
                        if k is not None:
                            if first and k == 0:
                                dve.wait_ge(tab_zeroed, 2)
                                dve.wait_ge(consts, N_CONSTS)
                            if not (first and k == 0):
                                quad_k(i if k else i - 1, (k - 1) % QPB)
                            quad_sums(i, k)

            def u2_out(i, b):
                n = i * 2 + b
                add_up(U2, i, b, u2[:, tiles(i, U2, b), :])
                if isinstance(i, int) and i == 0 and b == 0:
                    dve.wait_ge(x_stored, 32)
                if later(i) or n > 0:
                    dve.wait_ge(m1_done, 2 * n)
                dve.wait_ge(nb_evac, U2.g0 + n + 1)
                for j in range(T):
                    for q in range(4):
                        ins = dve.tensor_scalar(uj[32 * j:32 * j + 32, b, :, q, :],
                                                u2[32 * q:32 * q + 32, tiles(i, U2, b), NC * j:NC * j + NC],
                                                1.0, None, ALU.mult)
                ins.then_inc(uj_ready, 1)

            def u2_body(i, first):
                for b in range(U2.bb):
                    for su in range(U2.upb):
                        if not (first and b == 0 and su == 2):
                            split(U2, i, b * U2.upb + su)
                        if su == 1:
                            if first and b == 0:
                                resid(O0, O0.bodies - 1, O0.bb - 1, "tokens", 0)
                                add_squares(O0, O0.bodies - 1, O0.bb - 1)
                                quad_k(O0.bodies - 1, QPB - 1)
                                norm(1, U2, V_NORM + DT, "chunks")
                                powers_for_recurrence()
                            else:
                                u2_out(*before(U2, i, b, 1))

            def rec_products(k, i):
                c1 = i * 9 + k
                prev = XS[:, :, :, :, bass.ds(c1, 1)].rearrange("p a r s c -> p a r (s c)")
                dve.wait_ge(rec_done, c1 + 1)
                dve.tensor_tensor(rec1[:], a4a[:], prev, ALU.mult).then_inc(rec_a, 1)

            def rec_sums(k, i):
                c1 = i * 9 + k
                cur = XS[:, :, :, :, bass.ds(c1 + 1, 1)].rearrange("p a r s c -> p a r (s c)")
                dve.wait_ge(rec_a, c1 + 1)
                dve.tensor_tensor(cur, cur, rec1[:], ALU.add).then_inc(rec_half, 1)
                dve.wait_ge(rec_half, c1 + 1)
                dve.wait_ge(rec_b, c1 + 1)
                dve.tensor_tensor(cur, cur, rec2[:], ALU.add).then_inc(rec_done, 1)

            def z2_first():
                for b in range(Z2.bb):
                    for su in range(Z2.upb):
                        split(Z2, 0, b * Z2.upb + su)
                        if su == 1:
                            if b == 0:
                                u2_out(U2.bodies - 1, U2.bb - 1)
                            else:
                                z_out(Z2, 0, b - 1, Z0.blocks)

            def z2_body(i):
                for b in range(Z2.bb):
                    for su in range(Z2.upb):
                        s = b * Z2.upb + su
                        rec_products(s, i - 1)
                        split(Z2, i, s)
                        rec_sums(s, i - 1)
                        if su == 1:
                            z_out(Z2, *before(Z2, i, b, 1), Z0.blocks)
                rec_products(8, i - 1)
                rec_sums(8, i - 1)

            def glu_out(i, b):
                if not (isinstance(i, int) and i == 0 and b < 2):
                    dve.wait_ge(gated_lo, GR.blocks + i * 2 + b - 1)
                add_up(GL, i, b, v[:, b % 2])

            def glu_gate(i, b):
                dve.wait_ge(sig_ready, i * 2 + b + 1)
                dve.tensor_tensor(v[:, b % 2], v[:, b % 2], zs[:, tiles(i, GL, b), :], ALU.mult)\
                   .then_inc(gated_ready, 1)

            def y_skip(j, k):
                qd, bb = j * 4 + k, k % 2
                dve.wait_ge(y_done, qd + 1)
                if later(j) or k >= 2:
                    dve.wait_ge(gz_ready, qd - 1)
                dve.scalar_tensor_tensor(tmp[:, bb, 0, :], u2[:, bass.ds(qd, 1), :].rearrange("p a l -> p (a l)"),
                                         vec[:, bass.ds(V_D + qd, 1)], tb2[bb][:, 0:L], ALU.mult, ALU.add)\
                   .then_inc(yd_ready, 1)

            def spread(j, k):
                j, k = (j + 1, k - 4) if k >= 4 else (j, k)
                bb = k % 2
                dve.wait_ge(k_loaded[k], j * 16 + 16)
                src = kring[:, k].unsqueeze(2).to_broadcast([P, T, 4, 32])
                mask = qmask[:].unsqueeze(1).to_broadcast([P, T, 4, 32])
                dve.tensor_tensor(bdring[:, bb].rearrange("p l (s m) -> p l s m", s=4), src, mask, ALU.mult)\
                   .then_inc(bd_spread, 1)

            def y_quads(j, last=False):
                for k in range(4):
                    y_skip(j, k)
                    if not (last and k >= 2):
                        spread(j, k + 2)
                    y_low(j, k)

            def y_low(j, k):
                qd, bb = j * 4 + k, k % 2
                dve.wait_ge(g_hi, qd + 1)
                gv = g[:, bass.ds(qd, 1)].rearrange("p a r l -> p (a r) l")
                dve.tensor_tensor(gv[:, 1, :], tmp[:, bb, 1, :], gv[:, 0, :].bitcast(F32), ALU.subtract)\
                   .then_inc(g_lo, 1)

            def glu_body(i, first):
                for b in range(GL.bb):
                    for su in range(GL.upb):
                        split(GL, i, b * GL.upb + su)
                        if first and b == 0:
                            if su == 1:
                                z_out(Z2, Z2.bodies - 1, Z2.bb - 1, Z0.blocks)
                                spread(0, 0)
                                spread(0, 1)
                                y_quads(0)
                                with dve.Fori(1, NQUAD // 4 - 1) as j:
                                    y_quads(j)
                                y_quads(NQUAD // 4 - 1, last=True)
                                dve.wait_ge(gz_ready, NQUAD)
                        elif su == 1:
                            glu_out(*before(GL, i, b, 1))
                        elif su == 3:
                            glu_gate(*before(GL, i, b, 1))
                        elif su == 5:
                            gated_low(GL, *before(GL, i, b, 1), GR.blocks)

            def out2_body(i, first):
                for b in range(O2.bb):
                    for su in range(O2.upb):
                        split(O2, i, b * O2.upb + su)
                        if first and b == 0:
                            if su == 1:
                                glu_out(GL.bodies - 1, GL.bb - 1)
                                glu_gate(GL.bodies - 1, GL.bb - 1)
                            if su == 3:
                                gated_low(GL, GL.bodies - 1, GL.bb - 1, GR.blocks)
                        elif su == 1:
                            if first:
                                dve.wait_ge(x_back, 32)
                            resid(O2, *before(O2, i, b, 1), "chunks", O0.blocks)
                        elif su == 5:
                            add_squares(O2, *before(O2, i, b, 1))

            u0_bodies(dve, u0_body)
            bodies(dve, Z0, z0_body)
            bodies(dve, GR, grp_body)
            bodies(dve, O0, out0_body)
            bodies(dve, U2, u2_body)
            z2_first()
            dve.wait_ge(xs_ready, NQUAD)
            dve.sem_inc(rec_done, 1)
            with dve.Fori(1, Z2.bodies) as i:
                z2_body(i)
            bodies(dve, GL, glu_body)
            bodies(dve, O2, out2_body)
            resid(O2, O2.bodies - 1, O2.bb - 1, "chunks", O0.blocks)
            add_squares(O2, O2.bodies - 1, O2.bb - 1)
            inverse_root(2, tmp[:, 0, 0, 0:2], tmp[:, 0, 1, 0:2], tmp[:, 1, 0, 0:2], tmp[:, 1, 1, 0:2],
                         tb2[1][:, 0:2])
            dve.wait_ge(gain_loaded, 16)
            dve.wait_ge(out_evac, O2.blocks)
            for n in range(4):
                cols = slice(n // 2 * (D // 2), (n // 2 + 1) * (D // 2))
                dve.scalar_tensor_tensor(orows[:, n % 2, cols], orows[:, n % 2, cols], tmp[:, 1, 0, n % 2:n % 2 + 1],
                                         gain[:, cols], ALU.mult, ALU.mult).then_inc(out_ready, 1)

        @block.tensor
        def _(pe):
            mm = pe.matmul

            def unit(ph, i, s, operand, ready=None, count=0):
                U = ph.u0 + i * ph.bu + s
                b, su = divmod(s, ph.upb)
                ps = acc[b % 2]
                pe.wait_ge(lo_ready, U + 1)
                if su == 0 and (ph.g0 + b >= 2 or later(i)):
                    pe.wait_ge(nb_evac, ph.g0 + i * ph.bb + b - 1)
                for kk in range(UK):
                    kt = su * UK + kk
                    if ready is not None and kt % 2 == 0:
                        pe.wait_ge(ready, count + kt // 2 + 1)
                    rhs = operand(kt)
                    for tt in range(2):
                        cols = slice(tt * P, tt * P + P)
                        mm(ps[:, tt, :], whi[s % SPLIT][:, kk, cols], rhs[:, 0:2, :],
                           start=(kt == 0), stop=False, skip_group_check=True)
                        ins = mm(ps[:, tt, 0:L], wlo[s % SPLIT][:, kk, cols], rhs[:, 0, :],
                                 start=False, stop=(su == ph.upb - 1 and kk == UK - 1), skip_group_check=True)
                ins.then_inc(unit_done, 1)

            def turn_powers():
                pe.wait_ge(chain_done, 1)
                for r in range(2):
                    for k in range(T):
                        ins = pe.transpose(tb2[r][:, k * P:k * P + P], sw[16 + 2 * k + r][:], ident[:])
                ins.then_inc(powers_turned, 1)

            def turn_parameters(n):
                if n >= LAST_GROUPS:
                    pe.wait_ge(powers_ready, 3)
                elif n >= 2:
                    pe.wait_ge(par_evac[n % 2], n // 2)
                for a in range(4):
                    r, feature = n // 4, n % 4 * 4 + a
                    if r < 2:
                        src = bbar[:, r, :].rearrange("q (s a) -> q s a", a=PG)[:, :, feature]
                    else:
                        src = praw[:, r, feature * P:feature * P + P]
                    ins = pe.transpose(parameter_bank(n)[:, a * P:a * P + P], src, ident[:])
                ins.then_inc(par_turned, 1)

            def quad(i, k):
                b, qd = k % 2, i * QPB + k
                pe.wait_ge(mb_ready, qd + 1)
                if k or later(i):
                    pe.wait_ge(m1_evac, qd)
                for r in range(2):
                    for q in range(4):
                        ins = pe.transpose(tb01[:, r, q * P:q * P + P],
                                           MB[:, b, r, q].rearrange("p j g a -> p (j g a)"), ident[:])
                ins.then_inc(quad_turned, 1)
                pe.wait_ge(mc_ready, qd + 1)
                if k >= 2 or later(i):
                    pe.wait_ge(k_evac, qd - 1)
                for q in range(4):
                    for r in range(2):
                        ins = mm(tb2[b][32 * q:32 * q + 32, 0:T * 32],
                                 MB[:, b, r, q, T - 1].rearrange("p g a -> p (g a)"),
                                 MC[:, b, r, q, 0:T].rearrange("p k g a -> p (k g a)"),
                                 start=(r == 0), stop=(r == 1))
                ins.then_inc(k_ready, 1)

            pe.wait_ge(consts, 4)
            for n in range(DT // 2):
                if n % (DT // 4) == 0:
                    pe.wait_ge(x_loaded[n // (DT // 4)], 16)
                if n >= 2:
                    pe.wait_ge(xt_ready, n - 1)
                for tt in range(2):
                    for s in range(2):
                        ft = 2 * n + tt
                        ins = pe.transpose(tb01[:, n % 2, tt * L + s * P:tt * L + s * P + P],
                                           xrows[:, s, ft * P:ft * P + P], ident[:])
                ins.then_inc(xt_turned, 1)

            pe.wait_ge(vec_loaded, 16 * 4)
            pe.transpose(tb2[0][:, 0:P], vrow[:], ident[:]).then_inc(vec_turned, 1)

            def sum_squares(which, bank):
                pe.wait_ge(sq_added, (which + 1) * (DT // 2))
                for tt in range(2):
                    ins = mm(bank[:, 0:L], ones[:], sqsum[:, tt, :], start=(tt == 0), stop=(tt == 1))
                ins.then_inc(sq_summed, 1)

            sum_squares(0, tb2[1])

            def h_operand(kt):
                return h[:, kt]

            def gated_operand(kt):
                return gated[:, kt]

            def u0_body(i, first, turning=False):
                for s in range(U0.bu):
                    unit(U0, i, s, h_operand, hn_lo if first and s < U0.upb else None, 0)
                    if turning:
                        if s == 0:
                            turn_powers()
                        for n in GROUPS_AT.get(s, ()):
                            turn_parameters(n)

            def z0_body(i, first):
                for s in range(Z0.bu):
                    unit(Z0, i, s, h_operand)

            def grp_body(i, first):
                for s in range(GR.bu):
                    def operand(kt):
                        return pooled[:, bass.ds(i * GT + kt, 1)].rearrange("p a r l -> p (a r) l")
                    unit(GR, i, s, operand, pooled_ready if s < GR.upb else None, i * (GT // 2))

            def out0_body(i, first):
                for s in range(O0.bu):
                    unit(O0, i, s, gated_operand, gated_lo if first and s < O0.upb else None, 0)
                    k = quad_at(first, s)
                    if k is not None:
                        quad(i, k)

            def m1_products(i, b):
                n = i * 2 + b
                pe.wait_ge(m1_loaded[b], i * 16 + 16)
                pe.wait_ge(uj_ready, n + 1)
                for tt in range(2):
                    if not (isinstance(i, int) and i == 0 and b == 0):
                        pe.wait_ge(xs_ready, 2 * n + tt - 1)
                    for r in range(2):
                        for q in range(4):
                            col = (r * 4 + q) * NC
                            ins = mm(tb01[:, tt, col:col + NC], m1ring[:, b, tt, r, q, :], uj[:, b, tt, q, :],
                                     start=True, stop=True)
                    ins.then_inc(m1_done, 1)

            def u2_body(i, first):
                for b in range(U2.bb):
                    for su in range(U2.upb):
                        unit(U2, i, b * U2.upb + su, h_operand,
                             hn_lo if first and b == 0 else None, 8)
                        if su == 3 and not (first and b == 0):
                            m1_products(i - 1, 1) if b == 0 else m1_products(i, 0)

            def z2_body(i, first):
                for b in range(Z2.bb):
                    for su in range(Z2.upb):
                        unit(Z2, i, b * Z2.upb + su, h_operand)
                        if first and b == 0 and su == 3:
                            m1_products(U2.bodies - 1, 1)

            def y_products(j, k):
                qd, bb = j * 4 + k, k % 2
                pe.wait_ge(bd_spread, qd + 1)
                if later(j) or k >= 2:
                    pe.wait_ge(yd_ready, qd - 1)
                ps = tb2[bb]
                ut = u2[:, bass.ds(qd, 1), :].rearrange("p a l -> p (a l)")
                for l in range(T):
                    mm(ps[:, NC * l:L], bdring[:, bb, l, :], ut[:, 0:L - NC * l],
                       start=(l == 0), stop=False, skip_group_check=True)
                pe.wait_ge(m2_loaded[k], j * 16 + 16)
                pe.wait_ge(state_ready, qd + 1)
                for q in range(4):
                    for r in range(2):
                        for jt in range(T):
                            ins = mm(ps[32 * q:32 * q + 32, NC * jt + 1:NC * jt + NC],
                                     m2ring[:, k, r, q, jt, :], state[:, bb, r, q, 0:NC - 1],
                                     start=False, stop=(q == 3 and r == 1), skip_group_check=True)
                ins.then_inc(y_done, 1)

            def g_operand(kt):
                return g[:, kt]

            def glu_body(i, first):
                if first:
                    pe.wait_ge(rec_done, NC)
                    for k in range(4):
                        y_products(0, k)
                    with pe.Fori(1, NQUAD // 4) as j:
                        for k in range(4):
                            y_products(j, k)
                    pe.wait_ge(g_lo, NQUAD)
                for s in range(GL.bu):
                    unit(GL, i, s, g_operand)

            def out2_body(i, first):
                for s in range(O2.bu):
                    unit(O2, i, s, gated_operand, gated_lo if first and s < O2.upb else None, GR.blocks)
                    if s % O2.upb == 3 and not (first and s < O2.upb):
                        turn_rows(i, 0) if s > O2.upb else turn_rows(i - 1, 1)

            def turn_rows(i, b):
                n = i * O2.bb + b
                pe.wait_ge(nb_evac, O2.g0 + n + 1)
                if later(i):
                    pe.wait_ge(out_evac, n)
                for half in range(2):
                    for tt in range(2):
                        ins = pe.transpose(tb01[:, b, half * L + tt * P:half * L + tt * P + P],
                                           last[:, b, tt, half * P:half * P + P], ident[:])
                ins.then_inc(out_turned, 1)

            u0_bodies(pe, u0_body)
            bodies(pe, Z0, z0_body)
            bodies(pe, GR, grp_body)
            bodies(pe, O0, out0_body)
            pe.wait_ge(k_evac, NQUAD - 1)
            sum_squares(1, tb2[0])
            bodies(pe, U2, u2_body)
            bodies(pe, Z2, z2_body)
            bodies(pe, GL, glu_body)
            bodies(pe, O2, out2_body)
            turn_rows(O2.bodies - 1, O2.bb - 1)
            pe.wait_ge(sq_added, 3 * (DT // 2))
            pe.wait_ge(yd_ready, NQUAD)
            for half in range(2):
                for tt in range(2):
                    ins = mm(tb2[1][:, half:half + 1], sqsum[:, tt, half * P:half * P + P], ones[:, 0:1],
                             start=(tt == 0), stop=(tt == 1))
            ins.then_inc(sq_summed, 1)


N_CONSTS = 3 + 1 + 4 + sum(WINDOWS)

_INS = ["x", "norm_g", "final_norm_g", "pool_w_in", "pool_w_grp", "pool_scale", "pool_w_out",
        "ssm_w_in", "ssm_a_re", "ssm_a_im", "ssm_log_dt", "ssm_b_re", "ssm_b_im", "ssm_c_re",
        "ssm_c_im", "ssm_d", "ssm_w_glu", "ssm_b_glu", "ssm_w_out"]
_OUT = (1, L, D)


def kernel(**inputs):
    import concourse.bacc as bacc
    from concourse.bass_utils import run_bass_kernel_spmd

    nc = bacc.Bacc("TRN2", target_bir_lowering=False, num_devices=1)
    arrays, args = {}, []
    for name in _INS:
        a = np.ascontiguousarray(inputs[name])
        arrays[f"in_{name}"] = a
        args.append(nc.dram_tensor(f"in_{name}", a.shape, mybir.dt.from_np(a.dtype), kind="ExternalInput").ap())
    args.append(nc.dram_tensor("out_0", _OUT, F32, kind="ExternalOutput").ap())
    build_program(nc, *args)
    r = run_bass_kernel_spmd(nc, [arrays], core_ids=[0])
    return r.results[0]["out_0"]
```
